# Optimizing a Trainium2 kernel written in Bass

```python
import jax, jax.numpy as jnp
from jax import lax
import numpy as np

D_MODEL = 1024
BATCH = 1
SEQ = 512
DEPTH = 2

N_A = DEPTH // 2
N_B = DEPTH - N_A

GLA_HEADS = 4
GLA_QK = D_MODEL // 2
GLA_V = D_MODEL
GLA_HEAD_K = GLA_QK // GLA_HEADS
GLA_HEAD_V = GLA_V // GLA_HEADS
GATE_RANK = 16
GATE_TAU = 16.0
GLA_CHUNK = 64
GLA_IN = 2 * GLA_QK + 2 * GLA_V + GATE_RANK

SB_HEADS = 16
SB_HEAD_DIM = D_MODEL // SB_HEADS
BLOCK_Q = 128

D_FF = 4 * D_MODEL

DEEPNORM_ALPHA = (2.0 * DEPTH) ** 0.25
DEEPNORM_BETA = (8.0 * DEPTH) ** -0.25
LN_EPS = 1e-5
RMS_EPS = 1e-6


def layer_norm(x, g, b):
    xf = x.astype(jnp.float32)
    mu = jnp.mean(xf, axis=-1, keepdims=True)
    var = jnp.mean(jnp.square(xf - mu), axis=-1, keepdims=True)
    y = (xf - mu) * lax.rsqrt(var + LN_EPS)
    return (y * g.astype(jnp.float32) + b.astype(jnp.float32)).astype(x.dtype)

def gla_chunked(q, k, v, log_a):
    B, S, H, dk = q.shape
    dv = v.shape[-1]
    n = S // GLA_CHUNK

    def to_chunks(t):
        return t.astype(jnp.float32).reshape(B, n, GLA_CHUNK, H, t.shape[-1]).transpose(0, 3, 1, 2, 4)

    qc = to_chunks(q) * (dk ** -0.5)
    kc = to_chunks(k)
    vc = to_chunks(v)
    b = jnp.cumsum(to_chunks(log_a), axis=3)
    b_last = b[:, :, :, -1:, :]
    q_dec = qc * jnp.exp(b)
    k_dec = kc * jnp.exp(-b)
    k_end = kc * jnp.exp(b_last - b)

    causal = jnp.tril(jnp.ones((GLA_CHUNK, GLA_CHUNK), dtype=bool))
    att = jnp.where(causal, jnp.einsum('bhncd,bhnsd->bhncs', q_dec, k_dec), 0.0)
    o_intra = jnp.einsum('bhncs,bhnse->bhnce', att, vc)

    u = jnp.einsum('bhnsd,bhnse->bhnde', k_end, vc)
    decay = jnp.exp(b_last[:, :, :, 0, :])

    def step(state, inp):
        d_n, u_n = inp
        return d_n[..., None] * state + u_n, state

    init = jnp.zeros((B, H, dk, dv), jnp.float32)
    _, s_prev = lax.scan(step, init, (jnp.moveaxis(decay, 2, 0), jnp.moveaxis(u, 2, 0)))
    s_prev = jnp.moveaxis(s_prev, 0, 2)
    o_inter = jnp.einsum('bhncd,bhnde->bhnce', q_dec, s_prev)
    o = o_intra + o_inter
    return o.transpose(0, 2, 3, 1, 4).reshape(B, S, H, dv)

def gla_mixer(x, w_in, w_a2, b_a, norm_g, w_o):
    B, S, _ = x.shape
    proj = x @ w_in
    q, k, v, g, a1 = jnp.split(
        proj, [GLA_QK, 2 * GLA_QK, 2 * GLA_QK + GLA_V, 2 * GLA_QK + 2 * GLA_V], axis=-1)
    log_a = jax.nn.log_sigmoid((a1 @ w_a2 + b_a).astype(jnp.float32)) / GATE_TAU
    hk = lambda t: t.reshape(B, S, GLA_HEADS, GLA_HEAD_K)
    o = gla_chunked(hk(q), hk(k), v.reshape(B, S, GLA_HEADS, GLA_HEAD_V), hk(log_a))
    o = o * lax.rsqrt(jnp.mean(jnp.square(o), axis=-1, keepdims=True) + RMS_EPS)
    o = o * norm_g.astype(jnp.float32)
    o = o * jax.nn.silu(g.astype(jnp.float32).reshape(B, S, GLA_HEADS, GLA_HEAD_V))
    return o.reshape(B, S, GLA_V).astype(x.dtype) @ w_o

def stick_breaking_attention(q, k, v):
    S = q.shape[1]
    scale = SB_HEAD_DIM ** -0.5
    outs = []
    for i in range(S // BLOCK_Q):
        kv_len = (i + 1) * BLOCK_Q
        q_blk = q[:, i * BLOCK_Q:kv_len].astype(jnp.float32)
        k_blk = k[:, :kv_len].astype(jnp.float32)
        v_blk = v[:, :kv_len].astype(jnp.float32)
        z = jnp.einsum('bqhd,bkhd->bhqk', q_blk, k_blk) * scale
        t_idx = i * BLOCK_Q + jnp.arange(BLOCK_Q)
        s_idx = jnp.arange(kv_len)
        mask = s_idx[None, :] < t_idx[:, None]
        log_1m = jnp.where(mask, jax.nn.log_sigmoid(-z), 0.0)
        rev = lax.cumsum(log_1m, axis=3, reverse=True)
        log_w = jax.nn.log_sigmoid(z) + (rev - log_1m)
        w = jnp.where(mask, jnp.exp(log_w), 0.0)
        outs.append(jnp.einsum('bhqk,bkhd->bqhd', w, v_blk))
    return jnp.concatenate(outs, axis=1)

def sq_relu_mlp(x, w_up, w_down):
    h = jax.nn.relu(x @ w_up)
    return (h * h) @ w_down

def first_inputs(seed: int = 0) -> dict:
    key = jax.random.key(seed)
    ks = jax.random.split(key, 16)
    nrm = lambda k, shape, s: jax.random.normal(k, shape, jnp.float32) * s
    return {
        "x": nrm(ks[0], (BATCH, SEQ, D_MODEL), 1.0),
        "gla_w_in": nrm(ks[1], (N_A, D_MODEL, GLA_IN), D_MODEL ** -0.5),
        "gla_w_a2": nrm(ks[2], (N_A, GATE_RANK, GLA_QK), GATE_RANK ** -0.5),
        "gla_b_a": nrm(ks[3], (N_A, GLA_QK), 0.1),
        "gla_norm_g": 1.0 + nrm(ks[4], (N_A, GLA_HEAD_V), 0.02),
        "gla_w_o": nrm(ks[5], (N_A, GLA_V, D_MODEL), GLA_V ** -0.5 * DEEPNORM_BETA),
        "kv_w": nrm(ks[6], (D_MODEL, 2 * D_MODEL), D_MODEL ** -0.5),
        "sb_w_q": nrm(ks[7], (N_B, D_MODEL, D_MODEL), D_MODEL ** -0.5),
        "sb_w_o": nrm(ks[8], (N_B, D_MODEL, D_MODEL), D_MODEL ** -0.5 * DEEPNORM_BETA),
        "mlp_w_up": nrm(ks[9], (DEPTH, D_MODEL, D_FF), D_MODEL ** -0.5),
        "mlp_w_down": nrm(ks[10], (DEPTH, D_FF, D_MODEL), D_FF ** -0.5 * DEEPNORM_BETA),
        "ln_g": 1.0 + nrm(ks[11], (DEPTH, 2, D_MODEL), 0.02),
        "ln_b": nrm(ks[12], (DEPTH, 2, D_MODEL), 0.02),
    }

def first_block(x, gla_w_in, gla_w_a2, gla_b_a, gla_norm_g, gla_w_o, kv_w, sb_w_q, sb_w_o,
              mlp_w_up, mlp_w_down, ln_g, ln_b):
    B, S, D = x.shape
    h = x
    k_sh = None
    v_sh = None
    for layer in range(DEPTH):
        if layer < N_A:
            mix = gla_mixer(h, gla_w_in[layer], gla_w_a2[layer], gla_b_a[layer],
                            gla_norm_g[layer], gla_w_o[layer])
        else:
            j = layer - N_A
            if j == 0:
                kv = h @ kv_w
                k_sh = kv[..., :D].reshape(B, S, SB_HEADS, SB_HEAD_DIM)
                v_sh = kv[..., D:].reshape(B, S, SB_HEADS, SB_HEAD_DIM)
            q = (h @ sb_w_q[j]).reshape(B, S, SB_HEADS, SB_HEAD_DIM)
            o = stick_breaking_attention(q, k_sh, v_sh)
            mix = o.reshape(B, S, D).astype(h.dtype) @ sb_w_o[j]
        h = layer_norm(DEEPNORM_ALPHA * h + mix, ln_g[layer, 0], ln_b[layer, 0])
        h = layer_norm(DEEPNORM_ALPHA * h + sq_relu_mlp(h, mlp_w_up[layer], mlp_w_down[layer]),
                       ln_g[layer, 1], ln_b[layer, 1])
    return h


DEPTH_2 = 1

EPS = 1e-6
D_FF_2 = 4 * D_MODEL
M_HEADS = 4
M_DV = D_MODEL // 8
M_DQK = M_DV // 2
M_CONV = 5
M_CHUNK = 128
A_HEADS = 4
A_NOPE = D_MODEL // 8
A_ROPE = D_MODEL // 16
A_DV = D_MODEL // 8
A_DH = A_NOPE + A_ROPE
Q_LORA = D_MODEL // 4
KV_LORA = D_MODEL // 8
ROPE_THETA = 10000.0
Q_BLOCK = 128
M_QK_W = M_HEADS * M_DQK
M_V_W = M_HEADS * M_DV
N_GATES = 4 * M_HEADS
D_MIX = M_HEADS * M_DV + A_HEADS * A_DV
IN_WIDTHS = (M_QK_W, M_QK_W, M_V_W, M_V_W, N_GATES, Q_LORA, KV_LORA, A_ROPE)
D_IN = M_QK_W * 2 + M_V_W * 2 + N_GATES + Q_LORA + KV_LORA + A_ROPE


def rms_norm(x, g):
    xf = x.astype(jnp.float32)
    y = xf * lax.rsqrt(jnp.mean(xf * xf, axis=-1, keepdims=True) + EPS)
    return (y * g.astype(jnp.float32)).astype(x.dtype)

def rope(x, cos, sin):
    extra = x.ndim - 3
    c = cos.reshape(cos.shape[:2] + (1,) * extra + cos.shape[2:]).astype(jnp.float32)
    s = sin.reshape(sin.shape[:2] + (1,) * extra + sin.shape[2:]).astype(jnp.float32)
    xf = x.astype(jnp.float32)
    x1, x2 = xf[..., : A_ROPE // 2], xf[..., A_ROPE // 2:]
    return jnp.concatenate([x1 * c - x2 * s, x2 * c + x1 * s], axis=-1).astype(x.dtype)

def conv_centred(u, w, b):
    out = lax.conv_general_dilated(
        u, w[:, None, :].astype(u.dtype), window_strides=(1,),
        padding=[(M_CONV // 2, M_CONV // 2)],
        dimension_numbers=("NWC", "WIO", "NWC"), feature_group_count=u.shape[-1])
    return out + b.astype(u.dtype)

def mlstm_chunkwise(q, k, v, log_i, log_f):
    B, H, S, _ = q.shape
    L = M_CHUNK
    NC = S // L
    qc = q.reshape(B, H, NC, L, M_DQK)
    kc = k.reshape(B, H, NC, L, M_DQK)
    vc = v.reshape(B, H, NC, L, M_DV)
    li = log_i.reshape(B, H, NC, L)
    b = jnp.cumsum(log_f.reshape(B, H, NC, L), axis=-1)
    a = b[..., -1]
    w_log = a[..., None] - b + li
    g = jnp.max(w_log, axis=-1)
    w = jnp.exp(w_log - g[..., None])
    S_c = jnp.einsum('bhclv,bhcld->bhcvd', w[..., None] * vc, kc)
    n_c = jnp.einsum('bhcl,bhcld->bhcd', w, kc)

    def step(carry, inp):
        C, n, m = carry
        a_k, g_k, S_k, n_k = inp
        m_new = jnp.maximum(a_k + m, g_k)
        dec = jnp.exp(a_k + m - m_new)
        add = jnp.exp(g_k - m_new)
        C_new = dec[..., None, None] * C + add[..., None, None] * S_k
        n_new = dec[..., None] * n + add[..., None] * n_k
        return (C_new, n_new, m_new), (C, n, m)

    init = (jnp.zeros((B, H, M_DV, M_DQK), jnp.float32),
            jnp.zeros((B, H, M_DQK), jnp.float32),
            jnp.zeros((B, H), jnp.float32))
    xs = (jnp.moveaxis(a, 2, 0), jnp.moveaxis(g, 2, 0),
          jnp.moveaxis(S_c, 2, 0), jnp.moveaxis(n_c, 2, 0))
    _, (C_prev, n_prev, m_prev) = lax.scan(step, init, xs)
    C_prev = jnp.moveaxis(C_prev, 0, 2)
    n_prev = jnp.moveaxis(n_prev, 0, 2)
    m_prev = jnp.moveaxis(m_prev, 0, 2)

    D = b[..., :, None] - b[..., None, :] + li[..., None, :]
    causal_in_chunk = jnp.tril(jnp.ones((L, L), dtype=bool))
    D = jnp.where(causal_in_chunk, D, -jnp.inf)
    m_t = jnp.maximum(b + m_prev[..., None], jnp.max(D, axis=-1))
    P = jnp.exp(D - m_t[..., None]) * jnp.einsum('bhctd,bhcsd->bhcts', qc, kc)
    inter = jnp.exp(b + m_prev[..., None] - m_t)
    num = (jnp.einsum('bhcts,bhcsv->bhctv', P, vc)
           + inter[..., None] * jnp.einsum('bhctd,bhcvd->bhctv', qc, C_prev))
    den = jnp.sum(P, axis=-1) + inter * jnp.einsum('bhctd,bhcd->bhct', qc, n_prev)
    den = jnp.maximum(jnp.abs(den), jnp.exp(-m_t))
    return (num / den[..., None]).reshape(B, H, S, M_DV)

def mlstm_group(q, k, v, o, gates, b_gates, g_out):
    B, S, _ = q.shape
    f32 = jnp.float32

    def heads(t, d):
        return t.reshape(B, S, M_HEADS, d).transpose(0, 2, 1, 3).astype(f32)

    qh = heads(q, M_DQK) * (M_DQK ** -0.5)
    kh = heads(k, M_DQK)
    vh = heads(v, M_DV)
    gp = (gates.astype(f32) + b_gates.astype(f32)).reshape(B, S, 4, M_HEADS).transpose(2, 0, 3, 1)
    i_fw, f_fw, i_bw, f_bw = gp[0], gp[1], gp[2], gp[3]
    h_fw = mlstm_chunkwise(qh, kh, vh, i_fw, jax.nn.log_sigmoid(f_fw))

    def flip(t):
        return jnp.flip(t, axis=2)

    h_bw = flip(mlstm_chunkwise(flip(qh), flip(kh), flip(vh), flip(i_bw),
                                flip(jax.nn.log_sigmoid(f_bw))))
    h = (h_fw + h_bw).transpose(0, 2, 1, 3)
    h = rms_norm(h, g_out.reshape(M_HEADS, M_DV)).reshape(B, S, M_V_W)
    return (jax.nn.sigmoid(o.astype(f32)) * h).astype(q.dtype)

def mla_group(c_q, c_kv, k_pe, cos, sin, g_cq, g_ckv, w_uq, w_ukv, g_q, g_k):
    B, S, _ = c_q.shape
    q = (rms_norm(c_q, g_cq) @ w_uq).reshape(B, S, A_HEADS, A_DH)
    kv = (rms_norm(c_kv, g_ckv) @ w_ukv).reshape(B, S, A_HEADS, A_NOPE + A_DV)
    k_nope, v = kv[..., :A_NOPE], kv[..., A_NOPE:]
    k = jnp.concatenate(
        [k_nope, jnp.broadcast_to(k_pe[:, :, None, :], (B, S, A_HEADS, A_ROPE))], axis=-1)
    q = rms_norm(q, g_q)
    k = rms_norm(k, g_k)
    q = jnp.concatenate([q[..., :A_NOPE], rope(q[..., A_NOPE:], cos, sin)], axis=-1)
    k = jnp.concatenate([k[..., :A_NOPE], rope(k[..., A_NOPE:], cos, sin)], axis=-1)
    nb = S // Q_BLOCK
    qb = q.reshape(B, nb, Q_BLOCK, A_HEADS, A_DH).transpose(1, 0, 3, 2, 4)
    kh = k.transpose(0, 2, 1, 3)
    vh = v.transpose(0, 2, 1, 3)
    scale = A_DH ** -0.5

    def attend(q_blk):
        s = jnp.einsum('bhqd,bhkd->bhqk', q_blk, kh,
                       preferred_element_type=jnp.float32) * scale
        p = jax.nn.softmax(s, axis=-1)
        return jnp.einsum('bhqk,bhkv->bhqv', p.astype(vh.dtype), vh)

    out = lax.map(attend, qb)
    return out.transpose(1, 0, 3, 2, 4).reshape(B, S, A_HEADS * A_DV)

def second_inputs(seed: int = 0) -> dict:
    key = jax.random.key(seed)
    ks = jax.random.split(key, 24)
    f32 = jnp.float32

    def nrm(k, shape, scale):
        return jax.random.normal(k, shape, f32) * scale

    def gain(k, shape):
        return 1.0 + 0.02 * jax.random.normal(k, shape, f32)

    x = jax.random.normal(ks[0], (BATCH, SEQ, D_MODEL), f32)
    offset = jax.random.randint(ks[1], (BATCH, 1), 0, 1024, dtype=jnp.int32)
    positions = (jnp.arange(SEQ, dtype=jnp.int32)[None, :] + offset).astype(jnp.int32)
    gb = jax.random.normal(ks[2], (DEPTH_2, 4, M_HEADS), f32)
    forget_bias = 3.0 + jnp.linspace(0.0, 3.0, M_HEADS, dtype=f32)
    b_gates = jnp.stack([0.1 * gb[:, 0], forget_bias + 0.3 * gb[:, 1],
                         0.1 * gb[:, 2], forget_bias + 0.3 * gb[:, 3]], axis=1).reshape(DEPTH_2, N_GATES)
    return {
        "x": x,
        "positions": positions,
        "g_mix_norm": gain(ks[3], (DEPTH_2, D_MODEL)),
        "w_in": nrm(ks[4], (DEPTH_2, D_MODEL, D_IN), D_MODEL ** -0.5),
        "conv_w": nrm(ks[5], (DEPTH_2, M_CONV, 2 * M_QK_W), M_CONV ** -0.5),
        "conv_b": nrm(ks[6], (DEPTH_2, 2 * M_QK_W), 0.01),
        "b_gates": b_gates,
        "g_mlstm_out": gain(ks[7], (DEPTH_2, M_V_W)),
        "g_cq": gain(ks[8], (DEPTH_2, Q_LORA)),
        "g_ckv": gain(ks[9], (DEPTH_2, KV_LORA)),
        "w_uq": nrm(ks[10], (DEPTH_2, Q_LORA, A_HEADS * A_DH), Q_LORA ** -0.5),
        "w_ukv": nrm(ks[11], (DEPTH_2, KV_LORA, A_HEADS * (A_NOPE + A_DV)), KV_LORA ** -0.5),
        "g_q": gain(ks[12], (DEPTH_2, A_DH)),
        "g_k": gain(ks[13], (DEPTH_2, A_DH)),
        "w_out": nrm(ks[14], (DEPTH_2, D_MIX, D_MODEL), D_MIX ** -0.5),
        "g_ffn_norm": gain(ks[15], (DEPTH_2, D_MODEL)),
        "w_ff1": nrm(ks[16], (DEPTH_2, D_MODEL, D_FF_2), D_MODEL ** -0.5),
        "w_ff2": nrm(ks[17], (DEPTH_2, D_FF_2, D_MODEL), D_FF_2 ** -0.5),
    }

def second_block(x, positions, g_mix_norm, w_in, conv_w, conv_b, b_gates, g_mlstm_out,
              g_cq, g_ckv, w_uq, w_ukv, g_q, g_k, w_out, g_ffn_norm, w_ff1, w_ff2):
    inv_freq = ROPE_THETA ** (-jnp.arange(0, A_ROPE, 2, dtype=jnp.float32) / A_ROPE)
    ang = positions.astype(jnp.float32)[..., None] * inv_freq
    cos, sin = jnp.cos(ang), jnp.sin(ang)
    splits = [int(s) for s in np.cumsum(IN_WIDTHS)[:-1]]
    for l in range(DEPTH_2):
        h = rms_norm(x, g_mix_norm[l])
        z = h @ w_in[l]
        q_m, k_m, v_m, o_m, gates, c_q, c_kv, k_pe = jnp.split(z, splits, axis=-1)
        qk = jax.nn.silu(conv_centred(jnp.concatenate([q_m, k_m], axis=-1), conv_w[l], conv_b[l]))
        q_m, k_m = qk[..., :M_QK_W], qk[..., M_QK_W:]
        y_a = mlstm_group(q_m, k_m, v_m, o_m, gates, b_gates[l], g_mlstm_out[l])
        y_b = mla_group(c_q, c_kv, k_pe, cos, sin, g_cq[l], g_ckv[l], w_uq[l], w_ukv[l],
                        g_q[l], g_k[l])
        x = x + jnp.concatenate([y_a, y_b], axis=-1) @ w_out[l]
        h = rms_norm(x, g_ffn_norm[l])
        x = x + jnp.square(jax.nn.relu(h @ w_ff1[l])) @ w_ff2[l]
    return x


def setup_inputs(seed=0):
    out = dict(first_inputs(seed))
    for name, value in second_inputs(seed + 1).items():
        if name != "x":
            out[name + "_2"] = value
    return out


def reference(
    x, gla_w_in, gla_w_a2, gla_b_a, gla_norm_g, gla_w_o, kv_w, sb_w_q, sb_w_o, mlp_w_up,
    mlp_w_down, ln_g, ln_b, positions_2, g_mix_norm_2, w_in_2, conv_w_2, conv_b_2, b_gates_2,
    g_mlstm_out_2, g_cq_2, g_ckv_2, w_uq_2, w_ukv_2, g_q_2, g_k_2, w_out_2, g_ffn_norm_2,
    w_ff1_2, w_ff2_2,
):
    x = first_block(
        x, gla_w_in, gla_w_a2, gla_b_a, gla_norm_g, gla_w_o, kv_w, sb_w_q, sb_w_o, mlp_w_up,
        mlp_w_down, ln_g, ln_b,
    )
    return second_block(
        x, positions_2, g_mix_norm_2, w_in_2, conv_w_2, conv_b_2, b_gates_2, g_mlstm_out_2,
        g_cq_2, g_ckv_2, w_uq_2, w_ukv_2, g_q_2, g_k_2, w_out_2, g_ffn_norm_2, w_ff1_2, w_ff2_2,
    )


_drawn_inputs = setup_inputs


def setup_inputs(seed=0):
    import zlib

    import numpy as np

    out = dict(_drawn_inputs(seed))
    spreads = {}
    factors = {'gla_b_a': 5.54,
     'gla_norm_g': 8.0,
     'g_mix_norm_2': 4.28,
     'conv_b_2': 48.615,
     'g_mlstm_out_2': 37.822,
     'g_cq_2': 8.0,
     'g_ckv_2': 8.0,
     'g_q_2': 8.0,
     'g_k_2': 8.0,
     'g_ffn_norm_2': 9.321}
    for name, (base, spread) in spreads.items():
        noise = np.random.default_rng([zlib.crc32(name.encode()), seed]).standard_normal(out[name].shape)
        drawn = base * np.exp(spread * noise) if base else spread * noise
        out[name] = __import__('jax').numpy.asarray(drawn.astype(out[name].dtype))
    for name, factor in factors.items():
        out[name] = (out[name] * factor).astype(out[name].dtype)
    return out
```

```python
from contextlib import ExitStack

import numpy as np
import concourse.bass as bass
from concourse import mybir

F32 = mybir.dt.float32
F32R = mybir.dt.float32r
ALU = mybir.AluOpType
ACT = mybir.ActivationFunctionType
AX = mybir.AxisListType

P = 128
D = 1024
T = 512
C = D // P
TT = T // P
FFQ = 4
ALPHA = 4.0 ** 0.25
LN_EPS, RMS_EPS = 1e-5, 1e-6
GH = 4
GC = 64
SH = 16
MH = 4
AH = 4
RAW = 4
TWO_PI = 2 * np.pi
NEG = -1.0e30
ROUND = 12582912.0
_rest = TWO_PI - 6.28125
_mid = float(np.float16(_rest))
TWO_PI_PARTS = (6.28125, _mid, float(np.float32(_rest - _mid)))

MLP_BLOCKS = 2 * FFQ * C
B_GLA = 0
B_GLA_OUT = B_GLA + 25
B_MLP1 = B_GLA_OUT + C
B_SB = B_MLP1 + MLP_BLOCKS
B_SB_OUT = B_SB + 3 * C
B_MLP2 = B_SB_OUT + C
B_MIX = B_MLP2 + MLP_BLOCKS
B_MIX_OUT = B_MIX + 17
B_MLP3 = B_MIX_OUT + C
NB = B_MLP3 + MLP_BLOCKS

_cols = {}
_n = 0
for _name, _w in (("ba", 4), ("normg", 2), ("ln", 2 * 2 * 2 * C), ("gmix", C), ("gffn", C), ("gout", MH),
                  ("gcq", 2), ("gckv", 1), ("gqn", 1), ("gqr", 1), ("gkn", 1), ("gkr", 1), ("convw", 20),
                  ("convb", 4), ("bf", 1), ("bi", 1), ("freq", 1), ("ident", P), ("strict", P), ("gla_mask", P),
                  ("tri", P), ("ones", P), ("one", P), ("ln_eps", 1), ("rms_eps", 1), ("half_pi", 1), ("neg_fw", P), ("neg_sb", P), ("neg_bw", P), ("reset", T), ("wa2", T),
                  ("mixer's", 0), ("sel", 8 * P), ("swap", 64), ("wuq", 2 * 768), ("wukv", 1024)):
    _cols[_name] = (_n, _w)
    _n += _w
NPAR = _n
NPAR1 = _cols["mixer's"][0]
TRI = [0, 512, 1024, 896]


class Steps:

    def __init__(self, semaphore, noted):
        self.semaphore, self.noted, self.count, self.seen = semaphore, noted, 0, set()

    def did(self, instruction, *name):
        instruction.then_inc(self.semaphore, 1)
        self.count += 1
        if name:
            assert name not in self.seen, name
            self.seen.add(name)
            self.noted[name] = self.count

    def __getitem__(self, name):
        name = name if isinstance(name, tuple) else (name,)
        if name not in self.noted and FINAL:
            raise KeyError(name)
        return self.noted.get(name, 1)


FINAL = []


def build(nc, counts, W, X, PAR, POS, Y, STOP=99):
    with ExitStack() as ctx:
        scopes = [ctx]

        def sb(name, shape, dt=F32):
            return scopes[-1].enter_context(nc.sbuf_tensor(name, shape, dt))

        def sem(name):
            return ctx.enter_context(nc.semaphore(name))

        raw = sb("raw", [P, RAW, D])
        whi = [sb(f"whi{k}", [P, D], F32R) for k in range(2)]
        wlo = [sb(f"wlo{k}", [P, D], F32R) for k in range(2)]
        zero = sb("zero", [P, T])
        par = sb("par", [P, NPAR1])
        res = sb("res", [P, C, T])
        xh = sb("xh", [P, C, T], F32R)
        xl = sb("xl", [P, C, T], F32R)
        s1 = sb("s1", [P, T])
        s2 = sb("s2", [P, T])
        sq = sb("sq", [P, 2, T])
        mean = sb("mean", [P, T])
        rstd = sb("rstd", [P, T])
        tmp = sb("tmp", [P, 2, T])
        tmp2 = sb("tmp2", [P, 2, T])
        relu = sb("relu", [P, 2, T])

        with ExitStack() as mlp_scope:
            scopes.append(mlp_scope)
            hh = [sb(f"hh{k}", [P, C, T], F32R) for k in range(2)]
            hl = [sb(f"hl{k}", [P, C, T], F32R) for k in range(2)]
            scopes.pop()
        with ExitStack() as gla_scope:
            scopes.append(gla_scope)
            g_qk = sb("g_qk", [P, 8, T])
            g_vT = sb("g_vT", [P, C, T])
            g_g = sb("g_g", [P, C, T])
            g_v = sb("g_v", [P, TT, D])
            g_a1 = sb("g_a1", [16, T])
            g_z, g_ab, g_e, g_b, g_qd, g_kd, g_ke = (g_vT[:, c, :] for c in range(7))
            g_dec = sb("g_dec", [P, 8])
            g_att = sb("g_att", [P, 2, P])
            g_ket = sb("g_ket", [P, 2, P])
            g_S = sb("g_S", [P, 2, 256])
            g_on = sb("g_on", [P, 2, 256])
            g_junk = sb("g_junk", [P, 256])
            g_ss = sb("g_ss", [P, 4])
            scopes.pop()
        with ExitStack() as sb_scope:
            scopes.append(sb_scope)
            t_q, t_k, t_vT, t_v = (sb(f"t_{n}", [P, 2, T]) for n in ("q", "k", "vT", "v"))
            t_z, t_e, t_sp = (sb(f"t_{n}", [P, 2, 1280]) for n in ("z", "e", "sp"))
            t_sh, t_sl = (sb(f"t_{n}", [P, 1280], F32R) for n in ("sh", "sl"))
            t_oh, t_ol = (sb(f"t_{n}", [P, C, T], F32R) for n in ("oh", "ol"))
            t_one = sb("t_one", [P, 2, P], F32R)
            scopes.pop()
        with ExitStack() as mix_scope:
            scopes.append(mix_scope)
            par2 = sb("par2", [P, NPAR - NPAR1])
            m_o = sb("m_o", [P, 4, T])
            m_cq = sb("m_cq", [P, 2, T])
            m_ckv = sb("m_ckv", [P, T])
            m_kpe = sb("m_kpe", [64, T])
            m_dn = sb("m_dn", [P, 4])
            m_ss = sb("m_ss", [P, 4])
            with ExitStack() as mlstm_scope:
                scopes.append(mlstm_scope)
                m_raw = sb("m_raw", [P, 4, T])
                m_qk = sb("m_qk", [P, 4, T])
                m_vT = sb("m_vT", [P, 4, T])
                m_v = sb("m_v", [P, TT, MH, 130])
                m_I = sb("m_I", [64, T])
                m_F = sb("m_F", [64, T])
                m_B = sb("m_B", [64, T])
                m_M = sb("m_M", [64, T])
                m_u = sb("m_u", [64, T])
                m_Gc = sb("m_Gc", [P, TT, 64])
                m_Ec = sb("m_Ec", [P, TT, 64])
                m_Md = sb("m_Md", [P, T])
                m_Mb = sb("m_Mb", [P, T])
                m_E = sb("m_E", [P, 1280])
                m_P = sb("m_P", [P, 1280])
                m_h, m_hn = (m_raw[:, k, :].rearrange("p (t n) -> p t n", n=P) for k in range(2))
                scopes.pop()
            with ExitStack() as mla_scope:
                scopes.append(mla_scope)
                a_cos = sb("a_cos", [64, T])
                a_sin = sb("a_sin", [64, T])
                a_posi = sb("a_posi", [64, T], mybir.dt.int32)
                a_ang = sb("a_ang", [64, 2, T])
                a_n = [sb(f"a_n{k}", [P, T]) for k in range(2)]
                a_r = [sb(f"a_r{k}", [64, 3, T]) for k in range(2)]
                a_v = sb("a_v", [P, TT, T])
                a_p = sb("a_p", [P, 2, T])
                a_pT = sb("a_pT", [P, TT, T])
                scopes.pop()
            scopes.pop()

        banks = ctx.enter_context(nc.psum_tensor("banks", [P, 8, 512], F32))
        gb = [banks[:, k, :] for k in range(2)]

        def pc(name, a=0, b=None, rows=P):
            o, w = _cols[name]
            tile, o = (par, o) if o < NPAR1 else (par2, o - NPAR1)
            return tile[0:rows, o + a:o + (w if b is None else b)]

        loaded = [sem(f"loaded{r}") for r in range(RAW)]
        par_in = sem("par_in")
        par2_in = sem("par2_in")
        pos_in = sem("pos_in")
        x_in = [sem(f"x_in{c}") for c in range(C)]
        out_sem = sem("out_sem")
        zero_set = sem("zero_set")
        w_hi_done = sem("w_hi_done")
        w_ready = sem("w_ready")
        block_done = sem("block_done")
        bank_free = [sem(f"bank_free{k}") for k in range(2)]
        relu_done = sem("relu_done")
        up_squared = sem("up_squared")
        up_hi = sem("up_hi")
        hidden_ready = sem("hidden_ready")
        pe_step = sem("pe_step")
        act_step = sem("act_step")
        dve_step = sem("dve_step")


        PE = Steps(pe_step, counts[0])
        AS = Steps(act_step, counts[1])
        VS = Steps(dve_step, counts[2])
        NBX = B_SB if STOP == 1 else B_MIX if STOP == 2 else NB

        block = ctx.enter_context(nc.Block())

        def evacuated(eng, b):
            eng.wait_ge(bank_free[b % 2], b // 2 + 1)

        @block.sync
        def _(sp):
            sp.dma_start(par[:, :], PAR[:, 0:NPAR1]).then_inc(par_in, 16)
            for c in range(C):
                sp.dma_start(res[:, c, :], X[c]).then_inc(x_in[c], 16)
            for b in range(RAW):
                sp.dma_start(raw[:, b, :], W[b]).then_inc(loaded[b], 16)
            last = NBX // RAW * RAW
            with sp.Fori(RAW, last - RAW + 1, RAW) as i:
                for r in range(RAW):
                    sp.wait_ge(w_ready, i + (r - RAW + 1))
                    sp.dma_start(raw[:, r, :], W[i + r]).then_inc(loaded[r], 16)
            for b in range(last, NBX):
                sp.wait_ge(w_ready, b - RAW + 1)
                sp.dma_start(raw[:, b % RAW, :], W[b]).then_inc(loaded[b % RAW], 16)
            for c in range(C):
                sp.wait_ge(dve_step, VS["out", c])
                sp.dma_start(Y[c], res[:, c, :]).then_inc(out_sem, 16)
            sp.wait_ge(out_sem, 16 * C)

        @block.gpsimd
        def _(pool):
            nc.gpsimd.memset(zero[:, :], 0.0).then_inc(zero_set, 1)
            pool.wait_ge(zero_set, 1)

            def split(b, r, k, first=False):
                pool.wait_ge(loaded[r], (b // RAW + 1) * 16 if isinstance(b, int) else (b - r) * (16 // RAW) + 16)
                if not first:
                    pool.wait_ge(block_done, b - 1)
                nc.gpsimd.tensor_tensor(
                    whi[k][:, :].rearrange("p (a b) -> p a b", b=T), raw[:, r, :].rearrange("p (a b) -> p a b", b=T),
                    zero[:, :].unsqueeze(1).broadcast_to([P, D // T, T]), ALU.add).then_inc(w_hi_done, 1)
                pool.wait_ge(w_hi_done, b + 1)
                nc.gpsimd.tensor_tensor(wlo[k][:, :], raw[:, r, :], whi[k][:, :].bitcast(F32),
                                        ALU.subtract).then_inc(w_ready, 1)

            for b in range(RAW):
                split(b, b, b % 2, b < 2)
            last = NBX // RAW * RAW
            with pool.Fori(RAW, last - RAW + 1, RAW) as i:
                for r in range(RAW):
                    split(i + r, r, r % 2)
            for b in range(last, NBX):
                split(b, b % RAW, b % 2)

        @block.tensor
        def _(pe):
            def product(b, k, free, hi, lo, chunk_ready=None, out=None):
                out = gb[k] if out is None else out
                pe.wait_ge(w_ready, b + 1)
                if free is not None:
                    pe.wait_ge(bank_free[k], free)
                for c in range(C):
                    if chunk_ready:
                        pe.wait_ge(dve_step, chunk_ready[c])
                    w = slice(c * P, c * P + P)
                    pe.matmul(out, whi[k][:, w], hi[:, c, :], start=(c == 0), stop=False)
                    pe.matmul(out, wlo[k][:, w], hi[:, c, :], start=False, stop=False)
                    m = pe.matmul(out, whi[k][:, w], lo[:, c, :], start=False, stop=(c == C - 1))
                m.then_inc(block_done, 1)

            def products(b0, n, hi=xh, lo=xl, chunk_ready=None):
                if n % 2:
                    product(b0, b0 % 2, b0 // 2 if b0 >= 2 else None, hi, lo, chunk_ready)
                    b0, n = b0 + 1, n - 1
                if b0 < 2:
                    for b in range(b0, b0 + 2):
                        product(b, b % 2, b // 2 if b >= 2 else None, hi, lo, chunk_ready)
                    b0, n = b0 + 2, n - 2
                with pe.Fori(0, n // 2) as i:
                    for j in range(2):
                        product(i * 2 + (b0 + j), (b0 + j) % 2, i + (b0 + j) // 2, hi, lo, chunk_ready)

            def mlp(b0, u0, chunk_ready):
                for q in range(FFQ):
                    products(b0, C, xh, xl, chunk_ready)
                    b0 += C
                    if q:
                        pe.wait_ge(hidden_ready, u0 + C * q)
                        products(b0, C, hh[(q - 1) % 2], hl[(q - 1) % 2])
                        b0 += C
                pe.wait_ge(hidden_ready, u0 + C * FFQ)
                products(b0, C, hh[(FFQ - 1) % 2], hl[(FFQ - 1) % 2])

            def norm_sums(name, parts):
                for k, part in enumerate(parts):
                    pe.wait_ge(dve_step, VS[name, "part", k])
                    PE.did(pe.matmul(banks[:, 2 + k, :], pc("ones"), part[:, :], start=True, stop=True),
                           name, "sum", k)

            def program(pe):
                products(B_GLA, 25, chunk_ready=[VS["x split", c] for c in range(C)])
                for t in range(TT):
                    for half in range(2):
                        n = 2 * t + half
                        evacuated(pe, B_GLA + 15)
                        evacuated(pe, B_GLA + 16)
                        if n >= 2:
                            pe.wait_ge(act_step, AS["v turned", n - 2])
                        for c in range(4):
                            m = pe.transpose(banks[:, 2 + n % 2, c * P:c * P + P],
                                             g_vT[:, 4 * half + c, t * P:t * P + P], pc("ident"))
                        PE.did(m, "v turned", n)
                for h in range(GH):
                    evacuated(pe, B_GLA)
                    pe.wait_ge(act_step, AS["v turned", 7])
                    if h:
                        pe.wait_ge(act_step, AS["z", h - 1])
                        pe.wait_ge(dve_step, VS["state", 4 * h - 1])
                    PE.did(pe.matmul(banks[:, 2, :], pc("wa2", h * P, h * P + P, rows=16), g_a1[:, :],
                                     start=True, stop=True), "gate", h)
                    def turn_o(n):
                        pe.wait_ge(dve_step, VS["o normed", n])
                        if h and n == 4 * h:
                            pe.wait_ge(dve_step, VS["o gated", h - 1, 1])
                        for e in range(2):
                            m = pe.transpose(banks[:, e, (n % 4) * P:(n % 4) * P + P],
                                             g_on[:, n % 2, e * P:e * P + P], pc("ident"))
                        PE.did(m, "o turned", n)
                    for t in range(TT):
                        n = 4 * h + t
                        ts = slice(t * P, t * P + P)
                        pe.wait_ge(dve_step, VS["k end", h])
                        if n >= 1:
                            pe.wait_ge(dve_step, VS["att masked", n - 1])
                            pe.wait_ge(act_step, AS["k turned", n - 1])
                        PE.did(pe.matmul(banks[:, 3, 0:P], g_kd[:, ts], g_qd[:, ts], start=True, stop=True),
                               "att", n)
                        PE.did(pe.transpose(banks[:, 4, 0:P], g_ke[:, ts], pc("ident")), "k turned", n)
                        pe.wait_ge(act_step, AS["k turned", n])
                        if t == 0:
                            pe.wait_ge(act_step, AS["z", h])
                        if n:
                            pe.wait_ge(dve_step, VS["state", n - 1])
                        vs = g_v[:, t, h * 256:h * 256 + 256]
                        m = pe.matmul(banks[:, 7, 0:256], g_ket[0:64, n % 2, :], vs[0:64], start=True, stop=True)
                        if t < 3:
                            m = pe.matmul(banks[:, 2, 0:256], g_ket[64:P, n % 2, :], vs[64:P], start=True, stop=True)
                        PE.did(m, "u", n)
                        pe.wait_ge(dve_step, VS["att masked", n])
                        if n >= 2:
                            pe.wait_ge(dve_step, VS["o normed", n - 2])
                        o = banks[:, 5 + n % 2, 0:256]
                        PE.did(pe.matmul(o, g_att[:, n % 2, :], vs, start=True, stop=True, skip_group_check=True))
                        for k in range(2):
                            c = 2 * t + k
                            if c:
                                pe.wait_ge(dve_step, VS["S", h, c])
                                r = slice(64 * k, 64 * k + 64)
                                PE.did(pe.matmul(o[r], g_qd[:, t * P + 64 * k:t * P + 64 * k + 64], g_S[:, c % 2, :],
                                                 start=False, stop=True, skip_group_check=True), "inter", h, c)
                        if t:
                            turn_o(n - 1)
                    turn_o(4 * h + 3)
                pe.wait_ge(dve_step, VS["o gated", GH - 1, 1])
                products(B_GLA_OUT, C, chunk_ready=[VS["mix1 split", c] for c in range(C)])
                norm_sums("ln1", (s1, s2))
                mlp(B_MLP1, 0, [VS["ln1 split", c] for c in range(C)])
                norm_sums("ln2", (s1, s2))
                if STOP > 1:
                    Z = banks[:, 2:5, :].rearrange("p a b -> p (a b)")
                    R = banks[:, 5:8, :].rearrange("p a b -> p (a b)")

                    def project(c, part):
                        b = B_SB + 3 * c + part
                        evacuated(pe, b - 1)
                        if part == 0 and c:
                            pe.wait_ge(act_step, AS["sv turned", c - 1])
                        product(b, b % 2, None, xh, xl,
                                [VS["ln2 split", k] for k in range(C)] if c == 0 else None, gb[0])

                    def turn_v(c):
                        evacuated(pe, B_SB + 3 * c + 2)
                        for t in range(TT):
                            m = pe.transpose(gb[0][:, t * P:t * P + P], t_vT[:, c % 2, t * P:t * P + P], pc("ident"))
                        PE.did(m, "sv turned", c)

                    def scores(h):
                        r, c = slice(64 * (h % 2), 64 * (h % 2) + 64), h // 2
                        evacuated(pe, B_SB + 3 * c)
                        evacuated(pe, B_SB + 3 * c + 1)
                        if h:
                            pe.wait_ge(dve_step, VS["sb z", h - 1])
                        for i in range(TT):
                            m = pe.matmul(Z[:, TRI[i]:TRI[i] + T - i * P], t_k[r, c % 2, i * P:i * P + P],
                                          t_q[r, c % 2, i * P:T], start=True, stop=True, skip_group_check=True)
                        PE.did(m, "sb z", h)

                    def sums(h):
                        pe.wait_ge(dve_step, VS["sb sp", h])
                        for i in range(TT):
                            for j in range(i, TT):
                                for part, tile in enumerate((t_sh, t_sl)):
                                    m = pe.matmul(R[:, TRI[i] + (j - i) * P:TRI[i] + T - i * P],
                                                  t_one[:, 1 if j == i else 0, :],
                                                  tile[:, TRI[j]:TRI[j] + T - j * P],
                                                  start=(j == i and part == 0), stop=(j == TT - 1 and part == 1),
                                                  skip_group_check=True)
                        PE.did(m, "sb R", h)

                    def outputs(h):
                        r0, c = 64 * (h % 2), h // 2
                        pe.wait_ge(act_step, AS["sb w", h])
                        if h >= 2:
                            pe.wait_ge(dve_step, VS["sb split", c - 1])
                        for i in range(TT):
                            m = pe.matmul(gb[1][r0:r0 + 64, i * P:T], t_v[:, c % 2, i * P + r0:i * P + r0 + 64],
                                          t_e[:, h % 2, TRI[i]:TRI[i] + T - i * P], start=(i == 0), stop=(i == 3),
                                          skip_group_check=True)
                        PE.did(m, "sb o", h)

                    for part in range(3):
                        project(0, part)
                    turn_v(0)
                    scores(0)
                    for h in range(SH):
                        c = h // 2 + 1
                        if h + 1 < SH:
                            scores(h + 1)
                        if h:
                            outputs(h - 1)
                        if c < C:
                            project(c, 2 if h % 2 else 0)
                        sums(h)
                        if c < C:
                            if h % 2:
                                turn_v(c)
                            else:
                                project(c, 1)
                    outputs(SH - 1)
                    pe.wait_ge(dve_step, VS["sb split", C - 1])
                    products(B_SB_OUT, C, t_oh, t_ol)
                    norm_sums("ln3", (s1, s2))
                    mlp(B_MLP2, 32, [VS["ln3 split", c] for c in range(C)])
                    norm_sums("ln4", (s1, s2))
                if STOP > 2:
                    norm_sums("rms1", (s2,))
                    products(B_MIX, 17, chunk_ready=[VS["rms1 split", c] for c in range(C)])
                    mixer_pe(pe)
                    products(B_MIX_OUT, C, chunk_ready=[VS["mix split", c] for c in range(C)])
                    norm_sums("rms2", (s2,))
                    mlp(B_MLP3, 64, [VS["rms2 split", c] for c in range(C)])

            def mixer_pe(pe):
                pe.wait_ge(par2_in, 16)
                evacuated(pe, B_MIX + 6)
                evacuated(pe, B_MIX + 7)
                for t in range(TT):
                    if t >= 2:
                        pe.wait_ge(act_step, AS["mv turned", t - 2])
                    for h in range(MH):
                        m = pe.transpose(banks[:, 2 + t % 2, h * P:h * P + P], m_vT[:, h, t * P:t * P + P], pc("ident"))
                    PE.did(m, "mv turned", t)
                pe.wait_ge(act_step, AS["mv turned", 3])
                for k, (name, tile) in enumerate((("ml G", m_I), ("ml e", m_u))):
                    pe.wait_ge(*((dve_step, VS["ml G"]) if k == 0 else (act_step, AS["ml e"])))
                    for t in range(TT):
                        m = pe.transpose(banks[:, 2 + k, t * 64:t * 64 + 64], tile[:, t * P:t * P + P],
                                         pc("ident", 0, 64, rows=64))
                    PE.did(m, name)
                pe.wait_ge(dve_step, VS["ml cols"])
                pe.wait_ge(dve_step, VS["ml qk", 3])
                Z = banks[:, 2:5, :].rearrange("p a b -> p (a b)")
                for h in range(MH):
                    r = slice(64 * (h % 2), 64 * (h % 2) + 64)
                    q, k = m_qk[r, h // 2, :], m_qk[r, 2 + h // 2, :]
                    for d in range(2):
                        if (h, d) != (0, 0):
                            pe.wait_ge(dve_step, VS[("ml P", h, 0) if d else ("ml P", h - 1, 1)])
                        for i in range(TT):
                            ts = slice(i * P, T) if d == 0 else slice(0, i * P + P)
                            o = TRI[3 - i if d else i]
                            m = pe.matmul(Z[:, o:o + ts.stop - ts.start], k[:, i * P:i * P + P], q[:, ts],
                                          start=True, stop=True, skip_group_check=True)
                        PE.did(m, "ml z", h, d)
                        PE.did(pe.matmul(banks[:, 5, :], pc("sel", (4 * d + h) * P, (4 * d + h + 1) * P, rows=64),
                                         m_M[:, :], start=True, stop=True), "ml M", h, d)
                        pe.wait_ge(dve_step, VS["ml P", h, d])
                        if (h, d) != (0, 0):
                            pe.wait_ge(dve_step, VS[("ml h", h, 0) if d else ("ml h", h - 1, 1)])
                        for t in range(TT):
                            ss = range(t, TT) if d else range(t + 1)
                            for i in ss:
                                o = TRI[3 - i] + t * P if d else TRI[i] + (t - i) * P
                                m = pe.matmul(banks[:, 6 + t // 2, (t % 2) * 256:(t % 2) * 256 + 129],
                                              m_P[:, o:o + P], m_v[:, i, h, 0:129], start=(i == ss[0]),
                                              stop=(i == ss[-1]), skip_group_check=True)
                        PE.did(m, "ml num", h, d)
                    for t in range(TT):
                        pe.wait_ge(dve_step, VS["ml hn", h])
                        m = pe.transpose(banks[:, 0, t * P:t * P + P], m_hn[:, t, :], pc("ident"))
                    PE.did(m, "ml hT", h)
                pe.wait_ge(dve_step, VS["la sq"])
                PE.did(pe.matmul(banks[:, 2, :], pc("ones"), s1[:, :], start=True, stop=True), "la sum", 0)
                pe.wait_ge(act_step, AS["la sq", 2])
                PE.did(pe.matmul(banks[:, 3, :], pc("ones"), s2[:, :], start=True, stop=True), "la sum", 1)
                pe.wait_ge(dve_step, VS["la c"])
                v_cols = pc("wukv").rearrange("p (h n) -> p h n", n=256)[:, :, P:2 * P]
                for t in range(TT):
                    PE.did(pe.matmul(banks[:, 4 + t, :], m_ckv[:, t * P:t * P + P], v_cols, start=True, stop=True),
                           "la v", t)
                pe.wait_ge(act_step, AS["la v", 3])
                for h in range(AH):
                    for side in range(2):
                        if h or side:
                            pe.wait_ge(dve_step, VS[("la pre", h, 0) if side else ("la pre", h - 1, 1)])
                        if side == 0:
                            for k in range(2):
                                m = pe.matmul(banks[:, 2, :], pc("wuq", k * 768 + h * 192, k * 768 + h * 192 + 128),
                                              m_cq[:, k, :], start=(k == 0), stop=(k == 1))
                            for k in range(2):
                                m = pe.matmul(banks[0:64, 3, :],
                                              pc("wuq", k * 768 + h * 192 + 128, k * 768 + h * 192 + 192),
                                              m_cq[:, k, :], start=(k == 0), stop=(k == 1))
                        else:
                            m = pe.matmul(banks[:, 2, :], pc("wukv", h * 256, h * 256 + 128), m_ckv[:, :],
                                          start=True, stop=True)
                        PE.did(m, "la n", h, side)
                        pe.wait_ge(act_step, AS["la nsq", h, side])
                        pe.matmul(banks[:, 4, :], pc("ones"), sq[:, 0, :], start=True, stop=False)
                        PE.did(pe.matmul(banks[:, 4, :], pc("ones", rows=64), sq[0:64, 1, :], start=False,
                                         stop=True), "la nsum", h, side)
                        pe.wait_ge(dve_step, VS["la pre", h, side])
                        if h and side == 0:
                            pe.wait_ge(dve_step, VS["la out", h - 1])
                        PE.did(pe.matmul(banks[0:64, 5, :], pc("swap", rows=64), a_r[side][:, 0, :], start=True,
                                         stop=True), "la swap", h, side)

                    def turn_p(t):
                        n = 4 * h + t
                        pe.wait_ge(dve_step, VS["la p", n])
                        if n >= 2:
                            pe.wait_ge(act_step, AS["la pT", n - 2])
                        for i in range(TT):
                            m = pe.transpose(banks[:, n % 2, i * P:i * P + P], a_p[:, n % 2, i * P:i * P + P],
                                             pc("ident"))
                        PE.did(m, "la pT", n)

                    pe.wait_ge(dve_step, VS["la rope", h, 0])
                    pe.wait_ge(dve_step, VS["la rope", h, 1])
                    for t in range(TT):
                        n = 4 * h + t
                        ts = slice(t * P, t * P + P)
                        if n >= 2:
                            pe.wait_ge(act_step, AS["la e", n - 2])
                        pe.matmul(banks[:, 6 + n % 2, :], a_n[0][:, ts], a_n[1][:, :], start=True, stop=False)
                        PE.did(pe.matmul(banks[:, 6 + n % 2, :], a_r[0][:, 1, ts], a_r[1][:, 1, :], start=False,
                                         stop=True), "la s", n)
                        if t:
                            turn_p(t - 1)
                    turn_p(3)
                    pe.wait_ge(act_step, AS["la pT", 4 * h + 3])
                    for i in range(TT):
                        m = pe.matmul(banks[:, 5, :], a_v[:, i, h * P:h * P + P], a_pT[:, i, :], start=(i == 0),
                                      stop=(i == 3))
                    PE.did(m, "la out", h)

            program(pe)

        @block.scalar
        def _(act):
            def last():
                act.wait_ge(act_step, AS.count)

            def exp_and_ln():
                act.preload_act_table_set("natural_log_exp_and_others")

            def bank(b):
                act.wait_ge(block_done, b + 1)
                return gb[b % 2]

            def mlp(b0, u0):
                for q in range(FFQ):
                    b = b0 + (2 * q - 1 if q else 0) * C
                    u = u0 + C * q
                    with act.Fori(0, C // 2) as i:
                        for j in range(2):
                            act.wait_ge(up_squared, i * 2 + (u + j + 1))
                            act.wait_ge(block_done, i * 2 + (b + j + 1))
                            nc.scalar.activation(relu[:, j, :], gb[(b + j) % 2], ACT.Relu).then_inc(relu_done, 1)

            def squares(name, b0=None, normed=None):
                for c in range(C):
                    if b0 is None:
                        act.wait_ge(act_step, AS[normed, "out", c])
                    else:
                        evacuated(act, b0 + c)
                    if c >= 2:
                        act.wait_ge(dve_step, VS[name, "sq added", c - 2])
                    AS.did(nc.scalar.activation(sq[:, c % 2, :], res[:, c, :], ACT.Square), name, "sq", c)

            def norm(name, g, b, eps, center, split):
                act.wait_ge(dve_step, VS[name, "var"])
                AS.did(nc.scalar.activation(rstd[:, :], tmp2[:, 0, :], ACT.Ln, bias=pc(eps)))
                last()
                AS.did(nc.scalar.activation(rstd[:, :], rstd[:, :], ACT.Exp, scale=-0.5), name, "rstd")
                for c in range(C):
                    act.wait_ge(dve_step, VS[name, "scaled", c])
                    if center:
                        AS.did(nc.scalar.activation(res[:, c, :], tmp[:, c % 2, :], ACT.Identity,
                                                    scale=pc(g[0], g[1] + c, g[1] + c + 1),
                                                    bias=pc(b[0], b[1] + c, b[1] + c + 1)), name, "out", c)
                        if split:
                            last()
                            AS.did(nc.scalar.activation(xh[:, c, :], res[:, c, :], ACT.Copy), name, "hi", c)
                    else:
                        AS.did(nc.scalar.activation(tmp2[:, c % 2, :], tmp[:, c % 2, :], ACT.Copy,
                                                    scale=pc(g[0], g[1] + c, g[1] + c + 1)), name, "out", c)
                        last()
                        AS.did(nc.scalar.activation(xh[:, c, :], tmp2[:, c % 2, :], ACT.Copy), name, "hi", c)

            def mixer_act(act):
                act.dma_start(par2[:, :], PAR[:, NPAR1:NPAR]).then_inc(par2_in, 16)
                for t in range(TT):
                    act.wait_ge(pe_step, PE["mv turned", t])
                    AS.did(nc.scalar.activation(m_v[:, t, :, 0:P], banks[:, 2 + t % 2, :].rearrange(
                        "p (h n) -> p h n", n=P), ACT.Copy), "mv turned", t)
                for c in range(4):
                    act.wait_ge(dve_step, VS["ml conv", c])
                    if c >= 2:
                        act.wait_ge(dve_step, VS["ml qk", c - 2])
                    AS.did(nc.scalar.activation(tmp[:, c % 2, :], m_qk[:, c, :], ACT.Sigmoid), "ml sig", c)
                for c in range(4):
                    evacuated(act, B_MIX + 8 + c)
                    AS.did(nc.scalar.activation(m_o[:, c, :], m_o[:, c, :], ACT.Sigmoid), "ml o", c)
                exp_and_ln()
                act.wait_ge(dve_step, VS["ml F"])
                AS.did(nc.scalar.activation(m_u[:, :], m_F[:, :], ACT.Abs))
                last()
                AS.did(nc.scalar.activation(m_u[:, :], m_u[:, :], ACT.Exp, scale=-1.0))
                last()
                AS.did(nc.scalar.activation(m_u[:, :], m_u[:, :], ACT.Ln, bias=pc("one", 0, 1, rows=64)), "ml l")
                act.wait_ge(dve_step, VS["ml m"])
                AS.did(nc.scalar.activation(m_u[:, :], m_F[:, :], ACT.Exp, scale=-1.0), "ml e")
                for h in range(MH):
                    for d in range(2):
                        act.wait_ge(dve_step, VS["ml Md", h, d])
                        if (h, d) != (0, 0):
                            act.wait_ge(dve_step, VS[("ml P", h, 0) if d else ("ml P", h - 1, 1)])
                        for i in range(TT):
                            G = m_Gc[:, i, 32 * d + h:32 * d + h + 1]
                            a, b = (0, i * P) if d else (i * P + P, T)
                            o = TRI[3 - i] if d else TRI[i] + P
                            od = TRI[3 - i] + i * P if d else TRI[i]
                            if b > a:
                                AS.did(nc.scalar.activation(m_E[:, o:o + b - a], m_Mb[:, a:b], ACT.Exp, bias=G,
                                                            scale=-1.0))
                            AS.did(nc.scalar.activation(m_E[:, od:od + P], m_Md[:, i * P:i * P + P], ACT.Exp,
                                                        bias=G, scale=-1.0), *(("ml E", h, d) if i == 3 else ()))
                        act.wait_ge(pe_step, PE["ml num", h, d])
                        if (h, d) != (0, 0):
                            act.wait_ge(dve_step, VS[("ml h", h, 0) if d else ("ml h", h - 1, 1)])
                        dens = banks[:, 6:8, :].rearrange("p a (b c) -> p (a b) c", c=256)[:, :, 128]
                        AS.did(nc.scalar.activation(m_dn[:, :], dens, ACT.Abs), "ml den", h, d)
                    act.wait_ge(dve_step, VS["ml h", h, 1])
                    if h:
                        act.wait_ge(dve_step, VS["ml hn", h - 1])
                    for t in range(TT):
                        AS.did(nc.scalar.activation(tmp[:, 0, t * P:t * P + P], m_h[:, t, :], ACT.Square,
                                                    accum_out=m_ss[:, t:t + 1]))
                    last()
                    AS.did(nc.scalar.activation(m_ss[:, :], m_ss[:, :], ACT.Ln, scale=1 / 128.0, bias=pc("rms_eps")))
                    last()
                    AS.did(nc.scalar.activation(m_ss[:, :], m_ss[:, :], ACT.Exp, scale=-0.5), "ml rstd", h)
                act.wait_ge(dve_step, VS["out h", MH - 1])
                act.dma_start(a_posi[:, :], POS).then_inc(pos_in, 16)
                for k in range(2):
                    AS.did(nc.scalar.activation(sq[:, k, :], m_cq[:, k, :], ACT.Square), "la sq", k)
                AS.did(nc.scalar.activation(s2[:, :], m_ckv[:, :], ACT.Square), "la sq", 2)
                for k, scale in enumerate((D / 256, D / 128)):
                    act.wait_ge(pe_step, PE["la sum", k])
                    r = (mean, rstd)[k]
                    AS.did(nc.scalar.activation(r[:, :], banks[:, 2 + k, :], ACT.Ln, scale=scale, bias=pc("rms_eps")))
                    last()
                    AS.did(nc.scalar.activation(r[:, :], r[:, :], ACT.Exp, scale=-0.5), "la rstd", k)
                for t in range(TT):
                    act.wait_ge(pe_step, PE["la v", t])
                    AS.did(nc.scalar.activation(a_v[:, t, :], banks[:, 4 + t, :], ACT.Copy), "la v", t)
                act.wait_ge(dve_step, VS["la ang"])
                AS.did(nc.scalar.activation(a_sin[:, :], a_ang[:, 0, :], ACT.Sin))
                AS.did(nc.scalar.activation(a_ang[:, 1, :], a_ang[:, 0, :], ACT.Abs))
                last()
                AS.did(nc.scalar.activation(a_cos[:, :], a_ang[:, 1, :], ACT.Sin, scale=-1.0,
                                            bias=pc("half_pi", rows=64)), "la tables")
                exp_and_ln()
                for h in range(AH):
                    for side in range(2):
                        act.wait_ge(pe_step, PE["la n", h, side])
                        if h or side:
                            act.wait_ge(pe_step, PE["la nsum", h if side else h - 1, 1 - side])
                            act.wait_ge(dve_step, VS["la pre", h if side else h - 1, 1 - side])
                        AS.did(nc.scalar.activation(sq[:, 0, :], banks[:, 2, :], ACT.Square))
                        AS.did(nc.scalar.activation(sq[0:64, 1, :], m_kpe[:, :] if side else banks[0:64, 3, :],
                                                    ACT.Square), "la nsq", h, side)
                        act.wait_ge(pe_step, PE["la nsum", h, side])
                        AS.did(nc.scalar.activation(rstd[:, :], banks[:, 4, :], ACT.Ln, scale=D / 192,
                                                    bias=pc("rms_eps")))
                        last()
                        AS.did(nc.scalar.activation(rstd[:, :], rstd[:, :], ACT.Exp, scale=-0.5), "la nrstd", h, side)
                    for t in range(TT):
                        n = 4 * h + t
                        act.wait_ge(dve_step, VS["la max", n])
                        if n >= 2:
                            act.wait_ge(pe_step, PE["la pT", n - 2])
                        AS.did(nc.scalar.activation(a_p[:, n % 2, :], banks[:, 6 + n % 2, :], ACT.Exp,
                                                    scale=192 ** -0.5, bias=m_dn[:, n % 2:n % 2 + 1],
                                                    accum_out=m_ss[:, n % 2:n % 2 + 1]), "la e", n)
                        last()
                        AS.did(nc.scalar.activation(m_ss[:, 3:4], m_ss[:, n % 2:n % 2 + 1], ACT.Copy), "la l", n)
                        act.wait_ge(pe_step, PE["la pT", n])
                        if h and t == 0:
                            act.wait_ge(pe_step, PE["la out", h - 1])
                        AS.did(nc.scalar.activation(a_pT[:, :, t * P:t * P + P], banks[:, n % 2, :].rearrange(
                            "p (i t) -> p i t", t=P), ACT.Copy), "la pT", n)

            act.wait_ge(par_in, 16)
            for c in range(C):
                act.wait_ge(x_in[c], 16)
                AS.did(nc.scalar.activation(xh[:, c, :], res[:, c, :], ACT.Copy), "x hi", c)
            b = bank(0)
            nc.scalar.activation(g_a1[:, :], b[0:16, :], ACT.Copy).then_inc(bank_free[0], 1)
            for c in range(C):
                evacuated(act, B_GLA + 17 + c)
                if c >= 2:
                    act.wait_ge(dve_step, VS["g silu", c - 2])
                AS.did(nc.scalar.activation(tmp[:, c % 2, :], g_g[:, c, :], ACT.Sigmoid), "g sig", c)
            exp_and_ln()
            for n in range(8):
                act.wait_ge(pe_step, PE["v turned", n])
                AS.did(nc.scalar.activation(g_v[:, n // 2, (n % 2) * 512:(n % 2) * 512 + 512], banks[:, 2 + n % 2, :],
                                            ACT.Copy), "v turned", n)
            for h in range(GH):
                act.wait_ge(pe_step, PE["gate", h])
                AS.did(nc.scalar.activation(g_z[:, :], banks[:, 2, :], ACT.Identity, bias=pc("ba", h, h + 1)), "z", h)
                last()
                AS.did(nc.scalar.activation(g_ab, g_z, ACT.Abs))
                last()
                AS.did(nc.scalar.activation(g_e[:, :], g_ab[:, :], ACT.Exp, scale=-1.0))
                last()
                AS.did(nc.scalar.activation(g_e[:, :], g_e[:, :], ACT.Ln, bias=pc("one", 0, 1)), "l", h)
                act.wait_ge(dve_step, VS["to end", h])
                bl = g_b[:, :].rearrange("p (n c) -> p n c", c=GC)[:, :, GC - 1]
                AS.did(nc.scalar.activation(tmp[:, 0, :], g_b[:, :], ACT.Exp, scale=1 / 16.0), "eb", h)
                AS.did(nc.scalar.activation(tmp[:, 1, :], g_b[:, :], ACT.Exp, scale=-1 / 16.0), "enb", h)
                AS.did(nc.scalar.activation(tmp2[:, 1, :], tmp2[:, 0, :], ACT.Exp, scale=1 / 16.0), "ee", h)
                if h:
                    act.wait_ge(dve_step, VS["S", h - 1, 7])
                AS.did(nc.scalar.activation(g_dec[:, :], bl, ACT.Exp, scale=1 / 16.0), "dec", h)
                for t in range(TT):
                    n = 4 * h + t
                    act.wait_ge(pe_step, PE["k turned", n])
                    AS.did(nc.scalar.activation(g_ket[:, n % 2, :], banks[:, 4, 0:P], ACT.Copy),
                           "k turned", n)
                    act.wait_ge(pe_step, PE["inter", h, 2 * t + 1])
                    o = banks[:, 5 + n % 2, 0:256]
                    if n >= 2:
                        act.wait_ge(dve_step, VS["o normed", n - 2])
                    AS.did(nc.scalar.activation(g_junk[:, :], o, ACT.Square, accum_out=g_ss[:, 2 * (n % 2):2 * (n % 2) + 1]))
                    last()
                    s = g_ss[:, 2 * (n % 2):2 * (n % 2) + 1]
                    d = g_ss[:, 2 * (n % 2) + 1:2 * (n % 2) + 2]
                    AS.did(nc.scalar.activation(d, s, ACT.Ln, scale=1 / 256.0, bias=pc("rms_eps")))
                    last()
                    AS.did(nc.scalar.activation(d, d, ACT.Exp, scale=-0.5), "o rstd", n)
            squares("ln1", B_GLA_OUT)
            norm("ln1", ("ln", 0), ("ln", 8), "ln_eps", True, True)
            mlp(B_MLP1, 0)
            squares("ln2", B_MLP1 + 7 * C)
            norm("ln2", ("ln", 16), ("ln", 24), "ln_eps", True, STOP > 1)
            if STOP > 1:
                AS.did(nc.scalar.activation(t_one[:, 0, :], pc("one"), ACT.Copy))
                AS.did(nc.scalar.activation(t_one[:, 1, :], pc("tri"), ACT.Copy), "ones split")

                def v_turned(c):
                    act.wait_ge(pe_step, PE["sv turned", c])
                    if c >= 2:
                        act.wait_ge(pe_step, PE["sb o", 2 * c - 3])
                    AS.did(nc.scalar.activation(t_v[:, c % 2, :], gb[0], ACT.Copy), "sv turned", c)

                def softplus(h):
                    e = t_e[:, h % 2, :]
                    act.wait_ge(dve_step, VS["sb m", h])
                    AS.did(nc.scalar.activation(e, e, ACT.Exp))
                    last()
                    AS.did(nc.scalar.activation(e, e, ACT.Ln, bias=pc("one", 0, 1)), "sb l", h)

                def take_pair(c, part):
                    b = B_SB + 3 * c + part
                    if c >= 2:
                        act.wait_ge(pe_step, PE[("sv turned", c - 2) if part == 2 else ("sb z", 2 * c - 3)])
                    bank(b)
                    nc.scalar.activation((t_q, t_k, t_vT)[part][:, c % 2, :], gb[0], ACT.Copy,
                                         scale=0.125 if part == 0 else 1.0).then_inc(bank_free[b % 2], 1)

                for part in range(3):
                    take_pair(0, part)
                v_turned(0)
                softplus(0)
                for h in range(SH):
                    c = h // 2 + 1
                    if h + 1 < SH:
                        softplus(h + 1)
                    if c < C:
                        take_pair(c, 2 if h % 2 else 0)
                    act.wait_ge(dve_step, VS["sb lw", h])
                    AS.did(nc.scalar.activation(t_e[:, h % 2, :], t_sp[:, h % 2, :], ACT.Exp), "sb w", h)
                    if c < C:
                        if h % 2:
                            v_turned(c)
                        else:
                            take_pair(c, 1)
                squares("ln3", B_SB_OUT)
                norm("ln3", ("ln", 32), ("ln", 40), "ln_eps", True, True)
                mlp(B_MLP2, 32)
                squares("ln4", B_MLP2 + 7 * C)
                norm("ln4", ("ln", 48), ("ln", 56), "ln_eps", True, False)
            if STOP > 2:
                squares("rms1", normed="ln4")
                norm("rms1", ("gmix", 0), None, "rms_eps", False, True)
                mixer_act(act)
                squares("rms2", B_MIX_OUT)
                norm("rms2", ("gffn", 0), None, "rms_eps", False, True)
                mlp(B_MLP3, 64)

        @block.vector
        def _(dve):
            def last():
                dve.wait_ge(dve_step, VS.count)

            def take(dst, b, scale=1.0, bank=None):
                dve.wait_ge(block_done, b + 1)
                nc.vector.tensor_scalar(dst, gb[b % 2] if bank is None else bank, scale, None, ALU.mult).then_inc(bank_free[b % 2], 1)

            def add_residual(name, b0, alpha, sums):
                for c in range(C):
                    b = b0 + c
                    dve.wait_ge(block_done, b + 1)
                    nc.vector.scalar_tensor_tensor(out=res[:, c, :], in0=res[:, c, :], scalar=alpha, in1=gb[b % 2],
                                                   op0=ALU.mult, op1=ALU.add).then_inc(bank_free[b % 2], 1)
                    evacuated(dve, b)
                    if sums:
                        add_sums(name, c, sums)

            def add_sums(name, c, sums):
                if sums == 2:
                    if c == 0:
                        VS.did(nc.vector.tensor_copy(s1[:, :], res[:, c, :]))
                    else:
                        last()
                        VS.did(nc.vector.tensor_tensor(s1[:, :], s1[:, :], res[:, c, :], ALU.add),
                               *((name, "part", 0) if c == C - 1 else ()))
                dve.wait_ge(act_step, AS[name, "sq", c])
                if c == 0:
                    VS.did(nc.vector.tensor_copy(s2[:, :], sq[:, 0, :]), name, "sq added", 0)
                else:
                    dve.wait_ge(dve_step, VS[name, "sq added", c - 1])
                    VS.did(nc.vector.tensor_tensor(s2[:, :], s2[:, :], sq[:, c % 2, :], ALU.add), name, "sq added", c)
                if c == C - 1:
                    last()
                    VS.did(nc.vector.tensor_copy(sq[0:1, 0, 0:2], s2[0:1, 0:2]), name, "part", 1 if sums == 2 else 0)

            def norm(name, center, split):
                if center:
                    dve.wait_ge(pe_step, PE[name, "sum", 0])
                    VS.did(nc.vector.tensor_copy(mean[:, :], banks[:, 2, :]))
                    last()
                    VS.did(nc.vector.tensor_tensor(tmp2[:, 1, :], mean[:, :], mean[:, :], ALU.mult))
                    last()
                    dve.wait_ge(pe_step, PE[name, "sum", 1])
                    VS.did(nc.vector.tensor_tensor(tmp2[:, 0, :], banks[:, 3, :], tmp2[:, 1, :], ALU.subtract))
                    last()
                    VS.did(nc.vector.tensor_scalar(tmp2[:, 0, :], tmp2[:, 0, :], 0.0, None, ALU.max), name, "var")
                else:
                    dve.wait_ge(pe_step, PE[name, "sum", 0])
                    VS.did(nc.vector.tensor_copy(tmp2[:, 0, :], banks[:, 2, :]), name, "var")

                def low(c):
                    dve.wait_ge(act_step, AS[name, "hi", c])
                    src = res[:, c, :] if center else tmp2[:, c % 2, :]
                    VS.did(nc.vector.tensor_tensor(xl[:, c, :], src, xh[:, c, :].bitcast(F32), ALU.subtract),
                           name + " split", c)

                dve.wait_ge(act_step, AS[name, "rstd"])
                for c in range(C):
                    if c >= 2:
                        dve.wait_ge(act_step, AS[name, "out", c - 2])
                    if center:
                        VS.did(nc.vector.tensor_tensor(tmp[:, c % 2, :], res[:, c, :], mean[:, :], ALU.subtract))
                        last()
                        VS.did(nc.vector.tensor_tensor(tmp[:, c % 2, :], tmp[:, c % 2, :], rstd[:, :], ALU.mult),
                               name, "scaled", c)
                    else:
                        VS.did(nc.vector.tensor_tensor(tmp[:, c % 2, :], res[:, c, :], rstd[:, :], ALU.mult),
                               name, "scaled", c)
                    if split and c:
                        low(c - 1)
                if split:
                    low(C - 1)

            def split_pair(c):
                dve.wait_ge(pe_step, PE["sb o", 2 * c + 1])
                VS.did(nc.vector.tensor_copy(t_oh[:, c, :], gb[1]))
                last()
                VS.did(nc.vector.tensor_tensor(t_ol[:, c, :], gb[1], t_oh[:, c, :].bitcast(F32), ALU.subtract),
                       "sb split", c)

            def mlp(b0, u0, alpha, name, sums):
                def down(b, first):
                    with dve.Fori(0, C // 2) as i:
                        for j in range(2):
                            dve.wait_ge(block_done, i * 2 + (b + j + 1))
                            r = res[:, bass.ds(i * 2 + j, 1), :].rearrange("p a t -> p (a t)")
                            nc.vector.scalar_tensor_tensor(
                                out=r, in0=r, scalar=alpha if first else 1.0, in1=gb[(b + j) % 2],
                                op0=ALU.mult, op1=ALU.add).then_inc(bank_free[(b + j) % 2], 1)

                for q in range(FFQ):
                    b = b0 + (2 * q - 1 if q else 0) * C
                    u = u0 + C * q
                    with dve.Fori(0, C // 2) as i:
                        for j in range(2):
                            dve.wait_ge(relu_done, i * 2 + (u + j + 1))
                            nc.vector.scalar_tensor_tensor(out=tmp2[:, j, :], in0=gb[(b + j) % 2], scalar=0.0,
                                                           in1=relu[:, j, :], op0=ALU.max,
                                                           op1=ALU.mult).then_inc(bank_free[(b + j) % 2], 1)
                            dve.wait_ge(bank_free[(b + j) % 2], i + ((b + j) // 2 + 1))
                            h = hh[q % 2][:, bass.ds(i * 2 + j, 1), :].rearrange("p a t -> p (a t)")
                            l = hl[q % 2][:, bass.ds(i * 2 + j, 1), :].rearrange("p a t -> p (a t)")
                            nc.vector.tensor_scalar(h, tmp2[:, j, :], 1.0, None, ALU.mult).then_inc(up_squared, 1)
                            dve.wait_ge(up_squared, i * 2 + (u + j + 3))
                            nc.vector.tensor_tensor(l, tmp2[:, j, :], h.bitcast(F32),
                                                    ALU.subtract).then_inc(hidden_ready, 1)
                    if q:
                        down(b + C, q == 1)
                add_residual(name, b0 + 7 * C, 1.0, sums)

            def split_out(c, src):
                last()
                VS.did(nc.vector.tensor_scalar(xh[:, c, :], src, 1.0, None, ALU.mult))
                last()
                VS.did(nc.vector.tensor_tensor(xl[:, c, :], src, xh[:, c, :].bitcast(F32), ALU.subtract),
                       "mix split", c)

            def mixer_dve(dve):
                VS.did(nc.vector.memset(m_v[:, :, :, P:P + 2], 1.0))
                for c in range(4):
                    take(m_raw[:, c, :], B_MIX + c)
                for c in range(4):
                    take(m_vT[:, c, :], B_MIX + 4 + c)
                for c in range(4):
                    take(m_o[:, c, :], B_MIX + 8 + c)
                for c in range(2):
                    take(m_cq[:, c, :], B_MIX + 12 + c)
                take(m_ckv[:, :], B_MIX + 14)
                dve.wait_ge(block_done, B_MIX + 16)
                nc.vector.tensor_copy(m_kpe[:, :], banks[0:64, (B_MIX + 15) % 2, :])\
                    .then_inc(bank_free[(B_MIX + 15) % 2], 1)
                k = (B_MIX + 16) % 2
                dve.wait_ge(block_done, B_MIX + 17)
                VS.did(nc.vector.tensor_copy(m_F[:, :], banks[0:64, k, :]))
                nc.vector.tensor_copy(m_I[:, :], banks[64:P, k, :]).then_inc(bank_free[k], 1)
                last()
                VS.did(nc.vector.tensor_scalar(m_F[:, :], m_F[:, :], pc("bf", rows=64), None, ALU.add), "ml F")
                evacuated(dve, B_MIX + 16)
                VS.did(nc.vector.tensor_scalar(m_I[:, :], m_I[:, :], pc("bi", rows=64), None, ALU.add))
                for c in range(4):
                    w = [pc("convw", 5 * c + j, 5 * c + j + 1) for j in range(5)]
                    VS.did(nc.vector.tensor_scalar(m_qk[:, c, :], m_raw[:, c, :], w[2], pc("convb", c, c + 1),
                                                   ALU.mult, ALU.add))
                    for n, j in enumerate((0, 1, 3, 4)):
                        last()
                        a, b = max(0, 2 - j), T - max(0, j - 2)
                        o = m_qk[:, c, a:b]
                        VS.did(nc.vector.scalar_tensor_tensor(out=o, in0=m_raw[:, c, a + j - 2:b + j - 2],
                                                              scalar=w[j], in1=o, op0=ALU.mult, op1=ALU.add),
                               *(("ml conv", c) if n == 3 else ()))
                for c in range(4):
                    dve.wait_ge(act_step, AS["ml sig", c])
                    VS.did(nc.vector.scalar_tensor_tensor(out=m_qk[:, c, :], in0=m_qk[:, c, :],
                                                          scalar=0.125 if c < 2 else 1.0, in1=tmp[:, c % 2, :],
                                                          op0=ALU.mult, op1=ALU.mult), "ml qk", c)
                dve.wait_ge(act_step, AS["ml l"])
                VS.did(nc.vector.scalar_tensor_tensor(out=m_F[:, :], in0=m_F[:, :], scalar=0.0, in1=m_u[:, :],
                                                      op0=ALU.min, op1=ALU.subtract))
                last()
                for d in range(2):
                    r, step = slice(32 * d, 32 * d + 32), -1 if d else 1
                    VS.did(nc.vector.tensor_tensor_scan(m_B[r, ::step], zero[r, 0:T], m_F[r, ::step], 0.0,
                                                        ALU.add, ALU.add))
                last()
                VS.did(nc.vector.tensor_tensor(m_I[:, :], m_I[:, :], m_B[:, :], ALU.subtract), "ml G")
                last()
                for d in range(2):
                    r, step = slice(32 * d, 32 * d + 32), -1 if d else 1
                    VS.did(nc.vector.tensor_tensor_scan(m_M[r, ::step], m_I[r, ::step], zero[r, 0:T], 0.0,
                                                        ALU.max, ALU.add))
                last()
                VS.did(nc.vector.tensor_tensor(m_F[:, :], m_B[:, :], m_M[:, :], ALU.add), "ml m")
                dve.wait_ge(pe_step, PE["ml G"])
                VS.did(nc.vector.tensor_copy(m_Gc[:, :, :].rearrange("p a b -> p (a b)"), banks[:, 2, 0:256]))
                dve.wait_ge(pe_step, PE["ml e"])
                VS.did(nc.vector.tensor_copy(m_Ec[:, :, :].rearrange("p a b -> p (a b)"), banks[:, 3, 0:256]),
                       "ml cols")
                Z = banks[:, 2:5, :].rearrange("p a b -> p (a b)")[:, 0:1280]
                for h in range(MH):
                    for d in range(2):
                        dve.wait_ge(pe_step, PE["ml M", h, d])
                        VS.did(nc.vector.tensor_copy(m_Mb[:, :], banks[:, 5, :]))
                        last()
                        VS.did(nc.vector.tensor_tensor(m_Md[:, :].rearrange("p (a b) -> p a b", b=P),
                                                       m_Mb[:, :].rearrange("p (a b) -> p a b", b=P),
                                                       pc("neg_bw" if d else "neg_fw").unsqueeze(1)
                                                       .broadcast_to([P, 4, P]), ALU.add), "ml Md", h, d)
                        dve.wait_ge(act_step, AS["ml E", h, d])
                        if (h, d) != (0, 0):
                            dve.wait_ge(pe_step, PE[("ml num", h, 0) if d else ("ml num", h - 1, 1)])
                        VS.did(nc.vector.tensor_tensor(m_P[:, :], Z, m_E[:, :], ALU.mult), "ml P", h, d)
                        dve.wait_ge(act_step, AS["ml den", h, d])
                        VS.did(nc.vector.tensor_tensor(m_dn[:, :], m_dn[:, :], m_Ec[:, :, 32 * d + h], ALU.max))
                        last()
                        VS.did(nc.vector.reciprocal(m_dn[:, :], m_dn[:, :]))
                        last()
                        for t in range(TT):
                            num = banks[:, 6 + t // 2, (t % 2) * 256:(t % 2) * 256 + P]
                            if d == 0:
                                ins = nc.vector.tensor_scalar(m_h[:, t, :], num, m_dn[:, t:t + 1], None, ALU.mult)
                            else:
                                ins = nc.vector.scalar_tensor_tensor(out=m_h[:, t, :], in0=num,
                                                                     scalar=m_dn[:, t:t + 1], in1=m_h[:, t, :],
                                                                     op0=ALU.mult, op1=ALU.add)
                            VS.did(ins, *(("ml h", h, d) if t == 3 else ()))
                        last()
                    dve.wait_ge(act_step, AS["ml rstd", h])
                    if h:
                        dve.wait_ge(pe_step, PE["ml hT", h - 1])
                    for t in range(TT):
                        VS.did(nc.vector.tensor_scalar(m_hn[:, t, :], m_h[:, t, :], m_ss[:, t:t + 1], None,
                                                       ALU.mult), *(("ml hn", h) if t == 3 else ()))
                    dve.wait_ge(pe_step, PE["ml hT", h])
                    dve.wait_ge(act_step, AS["ml o", h])
                    VS.did(nc.vector.scalar_tensor_tensor(out=tmp2[:, 0, :], in0=gb[0], scalar=pc("gout", h, h + 1),
                                                          in1=m_o[:, h, :], op0=ALU.mult, op1=ALU.mult), "out h", h)
                    split_out(h, tmp2[:, 0, :])
                dve.wait_ge(act_step, AS["la sq", 1])
                VS.did(nc.vector.tensor_tensor(s1[:, :], sq[:, 0, :], sq[:, 1, :], ALU.add), "la sq")
                for k in range(2):
                    dve.wait_ge(act_step, AS["la rstd", 0])
                    VS.did(nc.vector.scalar_tensor_tensor(out=m_cq[:, k, :], in0=m_cq[:, k, :],
                                                          scalar=pc("gcq", k, k + 1), in1=mean[:, :], op0=ALU.mult,
                                                          op1=ALU.mult))
                dve.wait_ge(act_step, AS["la rstd", 1])
                VS.did(nc.vector.scalar_tensor_tensor(out=m_ckv[:, :], in0=m_ckv[:, :], scalar=pc("gckv"),
                                                      in1=rstd[:, :], op0=ALU.mult, op1=ALU.mult), "la c")
                dve.wait_ge(pos_in, 16)
                ang, k = a_ang[:, 0, :], a_ang[:, 1, :]
                VS.did(nc.vector.tensor_scalar(ang, a_posi[:, :], pc("freq", rows=64), None, ALU.mult))
                last()
                VS.did(nc.vector.tensor_scalar(k, ang, 1 / TWO_PI, ROUND, ALU.mult, ALU.add))
                last()
                VS.did(nc.vector.tensor_scalar(k, k, ROUND, None, ALU.subtract))
                for part in TWO_PI_PARTS:
                    last()
                    VS.did(nc.vector.scalar_tensor_tensor(out=ang, in0=k, scalar=-part, in1=ang, op0=ALU.mult,
                                                          op1=ALU.add))
                last()
                VS.did(nc.vector.tensor_scalar(ang, ang, 3.1415925, -3.1415925, ALU.min, ALU.max), "la ang")
                dve.wait_ge(act_step, AS["la tables"])
                for h in range(AH):
                    for side in range(2):
                        n_g, r_g = (("gqn", "gqr"), ("gkn", "gkr"))[side]
                        dve.wait_ge(act_step, AS["la nrstd", h, side])
                        if h:
                            dve.wait_ge(pe_step, PE["la s", 4 * h - 1])
                        VS.did(nc.vector.scalar_tensor_tensor(out=a_n[side][:, :], in0=banks[:, 2, :],
                                                              scalar=pc(n_g), in1=rstd[:, :], op0=ALU.mult,
                                                              op1=ALU.mult))
                        VS.did(nc.vector.scalar_tensor_tensor(out=a_r[side][:, 0, :],
                                                              in0=m_kpe[:, :] if side else banks[0:64, 3, :],
                                                              scalar=pc(r_g, rows=64), in1=rstd[0:64, :],
                                                              op0=ALU.mult, op1=ALU.mult), "la pre", h, side)
                        last()
                        VS.did(nc.vector.tensor_tensor(a_r[side][:, 1, :], a_r[side][:, 0, :], a_cos[:, :], ALU.mult))
                        dve.wait_ge(pe_step, PE["la swap", h, side])
                        VS.did(nc.vector.tensor_tensor(a_r[side][:, 2, :], banks[0:64, 5, :], a_sin[:, :], ALU.mult))
                        last()
                        VS.did(nc.vector.tensor_tensor(a_r[side][:, 1, :], a_r[side][:, 1, :], a_r[side][:, 2, :],
                                                       ALU.add), "la rope", h, side)
                    for t in range(TT):
                        n = 4 * h + t
                        dve.wait_ge(pe_step, PE["la s", n])
                        VS.did(nc.vector.reduce_max(m_dn[:, 2:3], banks[:, 6 + n % 2, :], AX.X))
                        last()
                        VS.did(nc.vector.tensor_scalar(m_dn[:, n % 2:n % 2 + 1], m_dn[:, 2:3], -(192 ** -0.5), None,
                                                       ALU.mult), "la max", n)
                        dve.wait_ge(act_step, AS["la l", n])
                        VS.did(nc.vector.reciprocal(m_dn[:, 3:4], m_ss[:, n % 2:n % 2 + 1]))
                        last()
                        VS.did(nc.vector.tensor_scalar(a_p[:, n % 2, :], a_p[:, n % 2, :], m_dn[:, 3:4], None,
                                                       ALU.mult), "la p", n)
                    dve.wait_ge(pe_step, PE["la out", h])
                    VS.did(nc.vector.tensor_copy(tmp2[:, 1, :], banks[:, 5, :]), "la out", h)
                    split_out(MH + h, tmp2[:, 1, :])

            dve.wait_ge(par_in, 16)
            VS.did(nc.vector.memset(g_att[:, :, :], 0.0))
            nc.vector.memset(tmp[:, :, :], 0.0).then_inc(up_squared, 2)
            for c in range(C):
                dve.wait_ge(act_step, AS["x hi", c])
                VS.did(nc.vector.tensor_tensor(xl[:, c, :], res[:, c, :], xh[:, c, :].bitcast(F32), ALU.subtract),
                       "x split", c)
            for c in range(8):
                take(g_qk[:, c, :], B_GLA + 1 + c)
            for c in range(C):
                take(g_vT[:, c, :], B_GLA + 9 + c)
            for c in range(C):
                take(g_g[:, c, :], B_GLA + 17 + c)
                if c:
                    dve.wait_ge(act_step, AS["g sig", c - 1])
                    VS.did(nc.vector.tensor_tensor(g_g[:, c - 1, :], g_g[:, c - 1, :], tmp[:, (c - 1) % 2, :],
                                                   ALU.mult), "g silu", c - 1)
            dve.wait_ge(act_step, AS["g sig", C - 1])
            VS.did(nc.vector.tensor_tensor(g_g[:, C - 1, :], g_g[:, C - 1, :], tmp[:, 1, :], ALU.mult),
                   "g silu", C - 1)
            for h in range(GH):
                dve.wait_ge(act_step, AS["l", h])
                VS.did(nc.vector.scalar_tensor_tensor(out=g_z[:, :], in0=g_z[:, :], scalar=0.0, in1=g_e[:, :],
                                                      op0=ALU.min, op1=ALU.subtract))
                last()
                VS.did(nc.vector.tensor_tensor_scan(g_b[:, :], pc("reset"), g_z[:, :], 0.0, ALU.mult, ALU.add))
                last()
                b3 = g_b[:, :].rearrange("p (n c) -> p n c", c=GC)
                bl = b3[:, :, GC - 1:GC].broadcast_to([P, T // GC, GC])
                VS.did(nc.vector.tensor_tensor(tmp2[:, 0, :].rearrange("p (n c) -> p n c", c=GC), bl, b3,
                                               ALU.subtract), "to end", h)
                if h:
                    dve.wait_ge(pe_step, PE["inter", h - 1, 7])
                dve.wait_ge(act_step, AS["ee", h])
                VS.did(nc.vector.scalar_tensor_tensor(out=g_qd[:, :], in0=g_qk[:, h, :], scalar=P ** -0.5,
                                                      in1=tmp[:, 0, :], op0=ALU.mult, op1=ALU.mult))
                VS.did(nc.vector.tensor_tensor(g_kd[:, :], g_qk[:, 4 + h, :], tmp[:, 1, :], ALU.mult))
                VS.did(nc.vector.tensor_tensor(g_ke[:, :], g_qk[:, 4 + h, :], tmp2[:, 1, :], ALU.mult), "k end", h)
                for t in range(TT):
                    n = 4 * h + t
                    dve.wait_ge(pe_step, PE["att", n])
                    if n >= 2:
                        dve.wait_ge(pe_step, PE["inter", (n - 2) // 4, 2 * ((n - 2) % 4) + 1])
                    VS.did(nc.vector.copy_predicated(g_att[:, n % 2, :], pc("gla_mask").bitcast(mybir.dt.uint32),
                                                     banks[:, 3, 0:P]), "att masked", n)
                    for k in range(2):
                        c = 2 * t + k
                        if c == 7:
                            continue
                        dve.wait_ge(pe_step, PE["u", n])
                        if c >= 2:
                            dve.wait_ge(pe_step, PE["inter", h, c - 1])
                        elif h:
                            dve.wait_ge(pe_step, PE["inter", h - 1, 7])
                        u = banks[:, 2 if k else 7, 0:256]
                        if c == 0:
                            VS.did(nc.vector.tensor_copy(g_S[:, 1, :], u), "S", h, 1)
                        else:
                            dve.wait_ge(dve_step, VS["S", h, c])
                            dve.wait_ge(act_step, AS["dec", h])
                            VS.did(nc.vector.scalar_tensor_tensor(out=g_S[:, (c + 1) % 2, :], in0=g_S[:, c % 2, :],
                                                                  scalar=g_dec[:, c:c + 1], in1=u, op0=ALU.mult,
                                                                  op1=ALU.add), "S", h, c + 1)
                    VS.noted[("state", n)] = VS.count
                    dve.wait_ge(act_step, AS["o rstd", n])
                    if n >= 2:
                        dve.wait_ge(pe_step, PE["o turned", n - 2])
                    VS.did(nc.vector.tensor_scalar(g_on[:, n % 2, :], banks[:, 5 + n % 2, 0:256],
                                                   g_ss[:, 2 * (n % 2) + 1:2 * (n % 2) + 2], None, ALU.mult),
                           "o normed", n)
                dve.wait_ge(pe_step, PE["o turned", 4 * h + 3])
                for e in range(2):
                    c = 2 * h + e
                    VS.did(nc.vector.scalar_tensor_tensor(out=tmp2[:, e, :], in0=banks[:, e, :],
                                                          scalar=pc("normg", e, e + 1), in1=g_g[:, c, :],
                                                          op0=ALU.mult, op1=ALU.mult), "o gated", h, e)
                    last()
                    VS.did(nc.vector.tensor_scalar(xh[:, c, :], tmp2[:, e, :], 1.0, None, ALU.mult))
                    last()
                    VS.did(nc.vector.tensor_tensor(xl[:, c, :], tmp2[:, e, :], xh[:, c, :].bitcast(F32),
                                                   ALU.subtract), "mix1 split", c)
            add_residual("ln1", B_GLA_OUT, ALPHA, 2)
            norm("ln1", True, True)
            mlp(B_MLP1, 0, ALPHA, "ln2", 2)
            norm("ln2", True, STOP > 1)
            if STOP > 1:
                Z = banks[:, 2:5, :].rearrange("p a b -> p (a b)")[:, 0:1280]
                R = banks[:, 5:8, :].rearrange("p a b -> p (a b)")[:, 0:1280]

                def take_scores(h):
                    dve.wait_ge(pe_step, PE["sb z", h])
                    VS.did(nc.vector.tensor_copy(t_z[:, h % 2, :], Z), "sb z", h)
                    last()
                    if h >= 2:
                        dve.wait_ge(pe_step, PE["sb o", h - 2])
                    VS.did(nc.vector.tensor_scalar(t_e[:, h % 2, :], t_z[:, h % 2, :], 40.0, None, ALU.min),
                           "sb m", h)

                def diagonal(tile, mask, op):
                    d = tile.rearrange("p (a b) -> p a b", b=256)[:, 0:5:2, 0:P]
                    VS.did(nc.vector.tensor_tensor(d, d, pc(mask).unsqueeze(1).broadcast_to([P, 3, P]), op))
                    return nc.vector.tensor_tensor(tile[:, 896:1024], tile[:, 896:1024], pc(mask), op)

                def softplus(h):
                    sp = t_sp[:, h % 2, :]
                    dve.wait_ge(act_step, AS["sb l", h])
                    if h >= 2:
                        dve.wait_ge(act_step, AS["sb w", h - 2])
                    VS.did(nc.vector.tensor_tensor(sp, t_z[:, h % 2, :], t_e[:, h % 2, :], ALU.max))
                    last()
                    VS.did(diagonal(sp, "strict", ALU.mult), "sb masked", h)

                def split_softplus(h):
                    sp = t_sp[:, h % 2, :]
                    dve.wait_ge(dve_step, VS["sb masked", h])
                    if h:
                        dve.wait_ge(pe_step, PE["sb R", h - 1])
                    VS.did(nc.vector.tensor_scalar(t_sh[:, :], sp, 1.0, None, ALU.mult))
                    last()
                    VS.did(nc.vector.tensor_tensor(t_sl[:, :], sp, t_sh[:, :].bitcast(F32), ALU.subtract),
                           "sb sp", h)

                take_scores(0)
                dve.wait_ge(act_step, AS["ones split"])
                softplus(0)
                split_softplus(0)
                for h in range(SH):
                    if h + 1 < SH:
                        take_scores(h + 1)
                        softplus(h + 1)
                    sp = t_sp[:, h % 2, :]
                    dve.wait_ge(pe_step, PE["sb R", h])
                    VS.did(nc.vector.tensor_tensor(sp, t_z[:, h % 2, :], R, ALU.subtract))
                    last()
                    VS.did(diagonal(sp, "neg_sb", ALU.add), "sb lw", h)
                    if h + 1 < SH:
                        split_softplus(h + 1)
                    if h % 2 == 0 and h:
                        split_pair(h // 2 - 1)
                split_pair(C - 1)
                add_residual("ln3", B_SB_OUT, ALPHA, 2)
                norm("ln3", True, True)
                mlp(B_MLP2, 32, ALPHA, "ln4", 2)
                norm("ln4", True, False)
            if STOP > 2:
                for c in range(C):
                    dve.wait_ge(act_step, AS["ln4", "out", c])
                    add_sums("rms1", c, 1)
                norm("rms1", False, True)
                mixer_dve(dve)
                add_residual("rms2", B_MIX_OUT, 1.0, 1)
                norm("rms2", False, True)
                mlp(B_MLP3, 64, 1.0, "last", 0)
            for c in range(C if STOP > 2 else 0):
                VS.did(nc.vector.tensor_copy(tmp2[0:1, 0, c:c + 1], res[0:1, c, 0:1]), "out", c)
            if STOP == 1:
                for c in range(C):
                    dve.wait_ge(act_step, AS["ln2", "out", c])
                    VS.did(nc.vector.tensor_copy(tmp2[0:1, 0, c:c + 1], res[0:1, c, 0:1]), "out", c)
            if STOP == 2:
                for c in range(C):
                    dve.wait_ge(act_step, AS["ln4", "out", c])
                    VS.did(nc.vector.tensor_copy(tmp2[0:1, 0, c:c + 1], res[0:1, c, 0:1]), "out", c)


def blocks(w):
    w = np.asarray(w)
    n = w.shape[1] // P
    return w.reshape(C, P, n, P).transpose(2, 1, 0, 3).reshape(n, P, D)


def placed(w, at):
    w = np.asarray(w)
    out = np.zeros((D, P), w.dtype)
    out[:, at] = w
    return blocks(out)


def mlp_stream(up, down):
    up, down = blocks(up), [blocks(np.asarray(down)[q * D:q * D + D]) for q in range(FFQ)]
    parts = [up[0:C]]
    for q in range(1, FFQ):
        parts += [up[q * C:q * C + C], down[q - 1]]
    return np.concatenate(parts + [down[FFQ - 1]])


def chunked(v, rows=P):
    return np.asarray(v).reshape(-1, rows).T


def _dram(**inp):
    g = np.asarray(inp["gla_w_in"])[0]
    stream = [placed(g[:, 3072:3088], np.arange(16)), blocks(g[:, 0:3072]), blocks(inp["gla_w_o"][0]),
              mlp_stream(inp["mlp_w_up"][0], inp["mlp_w_down"][0]),
              np.concatenate([blocks(inp["sb_w_q"][0]), blocks(inp["kv_w"])]).reshape(3, C, P, D).transpose(
                  1, 0, 2, 3).reshape(3 * C, P, D), blocks(inp["sb_w_o"][0]),
              mlp_stream(inp["mlp_w_up"][1], inp["mlp_w_down"][1])]
    m = np.asarray(inp["w_in_2"])[0]
    gates = 1536 + np.array([4, 5, 6, 7, 12, 13, 14, 15, 0, 1, 2, 3, 8, 9, 10, 11])
    at = np.concatenate([32 * k + np.arange(4) for k in range(4)])
    stream += [blocks(m[:, 0:1536]), blocks(m[:, 1552:1936]), placed(m[:, 1936:2000], np.arange(64)),
               placed(m[:, gates], at), blocks(inp["w_out_2"][0]), mlp_stream(inp["w_ff1_2"][0], inp["w_ff2_2"][0])]
    W = np.ascontiguousarray(np.concatenate(stream))
    par = np.zeros((P, NPAR), np.float32)

    def put(name, a, row=0):
        o, w = _cols[name]
        a = np.asarray(a)
        par[row:row + a.shape[0], o:o + a.shape[1]] = a

    put("ba", chunked(inp["gla_b_a"][0]))
    put("normg", chunked(inp["gla_norm_g"][0]))
    lg, lb = np.asarray(inp["ln_g"]), np.asarray(inp["ln_b"])
    put("ln", np.concatenate([chunked(a[l, k]) for l in range(2) for k in range(2) for a in (lg, lb)], axis=1))
    put("gmix", chunked(inp["g_mix_norm_2"][0]))
    put("gffn", chunked(inp["g_ffn_norm_2"][0]))
    put("gout", chunked(inp["g_mlstm_out_2"][0]))
    put("gcq", chunked(inp["g_cq_2"][0]))
    put("gckv", chunked(inp["g_ckv_2"][0]))
    for n, v in (("q", inp["g_q_2"][0]), ("k", inp["g_k_2"][0])):
        put(f"g{n}n", np.asarray(v)[0:128, None])
        put(f"g{n}r", np.asarray(v)[128:192, None])
    put("convw", np.asarray(inp["conv_w_2"][0]).reshape(5, 4, P).transpose(2, 1, 0).reshape(P, 20))
    put("convb", chunked(inp["conv_b_2"][0]))
    bg = np.asarray(inp["b_gates_2"][0]).reshape(4, 4)
    for n, k in (("bf", 1), ("bi", 0)):
        put(n, bg[k][:, None])
        put(n, bg[k + 2][:, None], 32)
    inv = (np.float32(10000.0) ** (-np.arange(0, 64, 2, dtype=np.float32) / np.float32(64))).astype(np.float32)
    put("freq", np.concatenate([inv, inv])[:, None])
    i = np.arange(P)
    s, t = i[:, None], i[None, :]
    put("ident", np.eye(P))
    put("strict", s < t)
    put("gla_mask", (s <= t) & (s // GC == t // GC))
    put("tri", s >= t)
    put("ones", np.full((P, P), 1.0 / D))
    put("one", np.ones((P, P)))
    put("ln_eps", np.full((P, 1), LN_EPS))
    put("rms_eps", np.full((P, 1), RMS_EPS))
    put("half_pi", np.full((P, 1), np.pi / 2))
    put("neg_fw", np.where(s > t, -NEG, 0.0))
    put("neg_bw", np.where(s < t, -NEG, 0.0))
    put("neg_sb", np.where(s >= t, NEG, 0.0))
    put("reset", np.broadcast_to((np.arange(T) % GC != 0), (P, T)))
    sel = np.zeros((64, 8, P))
    for d in range(2):
        for h in range(4):
            sel[32 * d + h, 4 * d + h] = 1
    put("sel", sel.reshape(64, 8 * P))
    swap = np.zeros((64, 64))
    swap[np.arange(32) + 32, np.arange(32)] = -1
    swap[np.arange(32), np.arange(32) + 32] = 1
    put("swap", swap)
    put("wa2", inp["gla_w_a2"][0])
    put("wuq", np.asarray(inp["w_uq_2"][0]).reshape(2, P, 768).transpose(1, 0, 2).reshape(P, 1536))
    put("wukv", inp["w_ukv_2"][0])
    x = np.ascontiguousarray(np.asarray(inp["x"])[0].T.reshape(C, P, T))
    pos = np.ascontiguousarray(np.broadcast_to(np.asarray(inp["positions_2"]).astype(np.int32), (64, T)))
    return W, x, par, pos


STOP_AT = 99


def kernel(**inputs):
    import concourse.bacc as bacc
    from concourse.bass_utils import run_bass_kernel_spmd

    W, x, par, pos = _dram(**inputs)
    counts = [{}, {}, {}]
    FINAL.clear()
    for second in range(2):
        if second:
            FINAL.append(True)
        nc = bacc.Bacc("TRN2", target_bir_lowering=False, num_devices=1)
        aps = [nc.dram_tensor(n, a.shape, mybir.dt.from_np(a.dtype), kind="ExternalInput").ap()
               for n, a in (("w_stream", W), ("x_t", x), ("params", par), ("pos", pos))]
        y = nc.dram_tensor("y_t", (C, P, T), F32, kind="ExternalOutput").ap()
        build(nc, counts, *aps, y, STOP=STOP_AT)
    r = run_bass_kernel_spmd(nc, [{"w_stream": W, "x_t": x, "params": par, "pos": pos}], core_ids=[0])
    return np.ascontiguousarray(r.results[0]["y_t"].reshape(D, T).T)[None]
```

```python
from contextlib import ExitStack

import numpy as np
import concourse.bass as bass
from concourse import mybir

F32 = mybir.dt.float32
F32R = mybir.dt.float32r
ALU = mybir.AluOpType
ACT = mybir.ActivationFunctionType
AX = mybir.AxisListType

P = 128
D = 1024
T = 512
C = D // P
TT = T // P
FFQ = 4
ALPHA = 4.0 ** 0.25
LN_EPS, RMS_EPS = 1e-5, 1e-6
GH = 4
GC = 64
SH = 16
MH = 4
AH = 4
RAW = 4
TWO_PI = 2 * np.pi
NEG = -1.0e30
ROUND = 12582912.0
_rest = TWO_PI - 6.28125
_mid = float(np.float16(_rest))
TWO_PI_PARTS = (6.28125, _mid, float(np.float32(_rest - _mid)))

MLP_BLOCKS = 2 * FFQ * C
B_GLA = 0
B_GLA_OUT = B_GLA + 25
B_MLP1 = B_GLA_OUT + C
B_SB = B_MLP1 + MLP_BLOCKS
B_SB_OUT = B_SB + 3 * C
B_MLP2 = B_SB_OUT + C
B_MIX = B_MLP2 + MLP_BLOCKS
B_MIX_OUT = B_MIX + 17
B_MLP3 = B_MIX_OUT + C
NB = B_MLP3 + MLP_BLOCKS

_cols = {}
_n = 0
for _name, _w in (("ba", 4), ("normg", 2), ("ln", 2 * 2 * 2 * C), ("gmix", C), ("gffn", C), ("gout", MH),
                  ("gcq", 2), ("gckv", 1), ("gqn", 1), ("gqr", 1), ("gkn", 1), ("gkr", 1), ("convw", 20),
                  ("convb", 4), ("bf", 1), ("bi", 1), ("freq", 1), ("ident", P), ("strict", P), ("gla_mask", P),
                  ("tri", P), ("ones", P), ("one", P), ("ln_eps", 1), ("rms_eps", 1), ("half_pi", 1), ("neg_fw", P), ("neg_sb", P), ("neg_bw", P), ("reset", T), ("wa2", T),
                  ("mixer's", 0), ("sel", 8 * P), ("swap", 64), ("wuq", 2 * 768), ("wukv", 1024)):
    _cols[_name] = (_n, _w)
    _n += _w
NPAR = _n
NPAR1 = _cols["mixer's"][0]
TRI = [0, 512, 1024, 896]


def gla_block(kind, h):
    if kind in ("g0", "g1"):
        return B_GLA + 5 + 6 * h + (kind == "g1")
    if h == 0:
        return B_GLA + 1 + ("v0", "q", "k", "v1").index(kind)
    return B_GLA + 1 + 6 * h + ("q", "k", "v0", "v1").index(kind)


GLA_HALVES = [{(i // 3, i % 3): i for i in range(12)}] * (GH - 1) + [{(0, 0): 0, (0, 1): 1, (1, 0): 2, (1, 1): 3}]
GLA_THROUGH = [{(0, 1): "g0", (1, 0): "g1", (1, 2): "q", (2, 1): "k", (3, 0): "v0", (3, 2): "v1"}] * (GH - 1) + [
    {(0, 1): "g0", (1, 1): "g1"}]


class Steps:

    def __init__(self, semaphore, noted):
        self.semaphore, self.noted, self.count, self.seen = semaphore, noted, 0, set()

    def did(self, instruction, *name):
        instruction.then_inc(self.semaphore, 1)
        self.count += 1
        if name:
            assert name not in self.seen, name
            self.seen.add(name)
            self.noted[name] = self.count

    def __getitem__(self, name):
        name = name if isinstance(name, tuple) else (name,)
        if name not in self.noted and FINAL:
            raise KeyError(name)
        return self.noted.get(name, 1)


FINAL = []


def build(nc, counts, W, X, PAR, POS, Y, STOP=99):
    with ExitStack() as ctx:
        scopes = [ctx]

        def sb(name, shape, dt=F32):
            return scopes[-1].enter_context(nc.sbuf_tensor(name, shape, dt))

        def sem(name):
            return ctx.enter_context(nc.semaphore(name))

        raw = sb("raw", [P, RAW, D])
        whi = [sb(f"whi{k}", [P, D], F32R) for k in range(2)]
        wlo = [sb(f"wlo{k}", [P, D], F32R) for k in range(2)]
        zero = sb("zero", [P, T])
        par = sb("par", [P, NPAR1])
        res = sb("res", [P, C, T])
        xh = sb("xh", [P, C, T], F32R)
        xl = sb("xl", [P, C, T], F32R)
        s1 = sb("s1", [P, T])
        s2 = sb("s2", [P, T])
        sq = sb("sq", [P, 2, T])
        mean = sb("mean", [P, T])
        rstd = sb("rstd", [P, T])
        tmp = sb("tmp", [P, 2, T])
        tmp2 = sb("tmp2", [P, 2, T])
        relu = sb("relu", [P, 2, T])

        with ExitStack() as mlp_scope:
            scopes.append(mlp_scope)
            hh = [sb(f"hh{k}", [P, C, T], F32R) for k in range(2)]
            hl = [sb(f"hl{k}", [P, C, T], F32R) for k in range(2)]
            scopes.pop()
        with ExitStack() as gla_scope:
            scopes.append(gla_scope)
            g_qd, g_kd, g_ke = (sb(f"g_{n}", [P, GH, T]) for n in ("qd", "kd", "ke"))
            g_vT = sb("g_vT", [P, 2, T])
            g_v = sb("g_v", [P, 2, TT, 256])
            g_g = sb("g_g", [P, 2, T])
            g_a1 = sb("g_a1", [16, T])
            g_dec = sb("g_dec", [P, GH, T // GC])
            g_att = sb("g_att", [P, 2, P])
            g_ket = sb("g_ket", [P, 2, P])
            g_S = sb("g_S", [P, 2, 256])
            g_on = sb("g_on", [P, 2, 256])
            g_junk = sb("g_junk", [P, 256])
            g_ss = sb("g_ss", [P, 4])
            g_junk2 = sb("g_junk2", [P, 1])
            g_oh, g_ol = (sb(f"g_{n}", [P, C, T], F32R) for n in ("oh", "ol"))
            scopes.pop()
        with ExitStack() as sb_scope:
            scopes.append(sb_scope)
            t_q, t_k, t_vT, t_v = (sb(f"t_{n}", [P, 2, T]) for n in ("q", "k", "vT", "v"))
            t_z, t_e, t_sp = (sb(f"t_{n}", [P, 2, 1280]) for n in ("z", "e", "sp"))
            t_sh, t_sl = (sb(f"t_{n}", [P, 1280], F32R) for n in ("sh", "sl"))
            t_oh, t_ol = (sb(f"t_{n}", [P, C, T], F32R) for n in ("oh", "ol"))
            t_one = sb("t_one", [P, 2, P], F32R)
            scopes.pop()
        with ExitStack() as mix_scope:
            scopes.append(mix_scope)
            par2 = sb("par2", [P, NPAR - NPAR1])
            m_o = sb("m_o", [P, 4, T])
            m_cq = sb("m_cq", [P, 2, T])
            m_ckv = sb("m_ckv", [P, T])
            m_kpe = sb("m_kpe", [64, T])
            m_dn = sb("m_dn", [P, 4])
            m_ss = sb("m_ss", [P, 4])
            a_cos = sb("a_cos", [64, T])
            a_sin = sb("a_sin", [64, T])
            a_posi = s1[0:64, :].bitcast(mybir.dt.int32)
            a_ang = relu[0:64, :, :]
            with ExitStack() as mlstm_scope:
                scopes.append(mlstm_scope)
                m_raw = sb("m_raw", [P, 4, T])
                m_qk = sb("m_qk", [P, 4, T])
                m_vT = sb("m_vT", [P, 4, T])
                m_v = sb("m_v", [P, TT, MH, 130])
                m_I = sb("m_I", [64, T])
                m_F = sb("m_F", [64, T])
                m_B = tmp2[0:64, 1, :]
                m_M = sb("m_M", [64, T])
                m_u = sb("m_u", [64, T])
                m_Gc = sb("m_Gc", [P, TT, 64])
                m_Ec = sb("m_Ec", [P, TT, 64])
                m_Md = tmp[:, 1, :]
                m_Mb = sq[:, 1, :]
                m_E = [sb("m_E", [P, 1280])[:, :], m_vT[:, :, :].rearrange("p c t -> p (c t)")[:, 0:1280]]
                m_P = [sb(f"m_P{k}", [P, 1280]) for k in range(2)]
                m_h0, m_h1, m_hn = (m_raw[:, k, :].rearrange("p (t n) -> p t n", n=P) for k in range(3))
                m_h = (m_h0, m_h1)
                scopes.pop()
            with ExitStack() as mla_scope:
                scopes.append(mla_scope)
                a_n = [[sb(f"a_n{k}{d}", [P, T]) for d in range(2)] for k in range(2)]
                a_r = [[sb(f"a_r{k}{d}", [64, T]) for d in range(2)] for k in range(2)]
                a_pre = [sb(f"a_pre{k}", [64, T]) for k in range(2)]
                a_swap = sb("a_swap", [64, T])
                a_v = sb("a_v", [P, TT, T])
                a_p = sb("a_p", [P, 2, T])
                a_pT = sb("a_pT", [P, TT, T])
                scopes.pop()
            scopes.pop()

        banks = ctx.enter_context(nc.psum_tensor("banks", [P, 8, 512], F32))
        gb = [banks[:, k, :] for k in range(2)]
        GATE_BANKS = (2, 5, 6, 7)

        def pc(name, a=0, b=None, rows=P):
            o, w = _cols[name]
            tile, o = (par, o) if o < NPAR1 else (par2, o - NPAR1)
            return tile[0:rows, o + a:o + (w if b is None else b)]

        loaded = [sem(f"loaded{r}") for r in range(RAW)]
        par_in = sem("par_in")
        par2_in = sem("par2_in")
        pos_in = sem("pos_in")
        x_in = [sem(f"x_in{c}") for c in range(C)]
        out_sem = sem("out_sem")
        zero_set = sem("zero_set")
        w_hi_done = sem("w_hi_done")
        w_ready = sem("w_ready")
        block_done = sem("block_done")
        bank_free = [sem(f"bank_free{k}") for k in range(2)]
        relu_done = sem("relu_done")
        up_squared = sem("up_squared")
        up_hi = sem("up_hi")
        hidden_ready = sem("hidden_ready")
        pe_step = sem("pe_step")
        act_step = sem("act_step")
        dve_step = sem("dve_step")


        PE = Steps(pe_step, counts[0])
        AS = Steps(act_step, counts[1])
        VS = Steps(dve_step, counts[2])
        NBX = B_SB if STOP == 1 else B_MIX if STOP == 2 else NB

        block = ctx.enter_context(nc.Block())

        def evacuated(eng, b):
            eng.wait_ge(bank_free[b % 2], b // 2 + 1)

        @block.sync
        def _(sp):
            sp.dma_start(par[:, :], PAR[:, 0:NPAR1]).then_inc(par_in, 16)
            for c in range(C):
                sp.dma_start(res[:, c, :], X[c]).then_inc(x_in[c], 16)
            for b in range(RAW):
                sp.dma_start(raw[:, b, :], W[b]).then_inc(loaded[b], 16)
            last = NBX // RAW * RAW
            with sp.Fori(RAW, last - RAW + 1, RAW) as i:
                for r in range(RAW):
                    sp.wait_ge(w_ready, i + (r - RAW + 1))
                    sp.dma_start(raw[:, r, :], W[i + r]).then_inc(loaded[r], 16)
            for b in range(last, NBX):
                sp.wait_ge(w_ready, b - RAW + 1)
                sp.dma_start(raw[:, b % RAW, :], W[b]).then_inc(loaded[b % RAW], 16)
            for c in range(C):
                sp.wait_ge(dve_step, VS["out", c])
                sp.dma_start(Y[c], res[:, c, :]).then_inc(out_sem, 16)
            sp.wait_ge(out_sem, 16 * C)

        @block.gpsimd
        def _(pool):
            nc.gpsimd.memset(zero[:, :], 0.0).then_inc(zero_set, 1)
            pool.wait_ge(zero_set, 1)

            def split(b, r, k, first=False):
                pool.wait_ge(loaded[r], (b // RAW + 1) * 16 if isinstance(b, int) else (b - r) * (16 // RAW) + 16)
                if not first:
                    pool.wait_ge(block_done, b - 1)
                nc.gpsimd.tensor_tensor(
                    whi[k][:, :].rearrange("p (a b) -> p a b", b=T), raw[:, r, :].rearrange("p (a b) -> p a b", b=T),
                    zero[:, :].unsqueeze(1).broadcast_to([P, D // T, T]), ALU.add).then_inc(w_hi_done, 1)
                pool.wait_ge(w_hi_done, b + 1)
                nc.gpsimd.tensor_tensor(wlo[k][:, :], raw[:, r, :], whi[k][:, :].bitcast(F32),
                                        ALU.subtract).then_inc(w_ready, 1)

            for b in range(RAW):
                split(b, b, b % 2, b < 2)
            last = NBX // RAW * RAW
            with pool.Fori(RAW, last - RAW + 1, RAW) as i:
                for r in range(RAW):
                    split(i + r, r, r % 2)
            for b in range(last, NBX):
                split(b, b % RAW, b % 2)

        @block.tensor
        def _(pe):
            def product(b, k, free, hi, lo, chunk_ready=None, out=None, chunks=range(C)):
                out = gb[k] if out is None else out
                if chunks[0] == 0:
                    pe.wait_ge(w_ready, b + 1)
                    if free is not None:
                        pe.wait_ge(bank_free[k], free)
                for c in chunks:
                    if chunk_ready:
                        pe.wait_ge(dve_step, chunk_ready[c])
                    w = slice(c * P, c * P + P)
                    pe.matmul(out, whi[k][:, w], hi[:, c, :], start=(c == 0), stop=False)
                    pe.matmul(out, wlo[k][:, w], hi[:, c, :], start=False, stop=False)
                    m = pe.matmul(out, whi[k][:, w], lo[:, c, :], start=False, stop=(c == C - 1))
                if chunks[-1] == C - 1:
                    m.then_inc(block_done, 1)

            def products(b0, n, hi=xh, lo=xl, chunk_ready=None):
                if n % 2:
                    product(b0, b0 % 2, b0 // 2 if b0 >= 2 else None, hi, lo, chunk_ready)
                    b0, n = b0 + 1, n - 1
                if b0 < 2:
                    for b in range(b0, b0 + 2):
                        product(b, b % 2, b // 2 if b >= 2 else None, hi, lo, chunk_ready)
                    b0, n = b0 + 2, n - 2
                with pe.Fori(0, n // 2) as i:
                    for j in range(2):
                        product(i * 2 + (b0 + j), (b0 + j) % 2, i + (b0 + j) // 2, hi, lo, chunk_ready)

            def mlp(b0, u0, chunk_ready):
                for q in range(FFQ):
                    products(b0, C, xh, xl, chunk_ready)
                    b0 += C
                    if q:
                        pe.wait_ge(hidden_ready, u0 + C * q)
                        products(b0, C, hh[(q - 1) % 2], hl[(q - 1) % 2])
                        b0 += C
                pe.wait_ge(hidden_ready, u0 + C * FFQ)
                products(b0, C, hh[(FFQ - 1) % 2], hl[(FFQ - 1) % 2])

            def norm_sums(name, parts):
                for k, part in enumerate(parts):
                    pe.wait_ge(dve_step, VS[name, "part", k])
                    PE.did(pe.matmul(banks[:, 2 + k, :], pc("ones"), part[:, :], start=True, stop=True),
                           name, "sum", k)

            def program(pe):
                product(B_GLA, 0, None, xh, xl, [VS["x split", c] for c in range(C)])
                product(B_GLA + 1, 1, None, xh, xl)
                evacuated(pe, B_GLA)
                for h in range(GH):
                    PE.did(pe.matmul(banks[:, GATE_BANKS[h], :], pc("wa2", h * P, h * P + P, rows=16), g_a1[:, :],
                                     start=True, stop=True), "gate", h)

                def plain(b):
                    product(b, b % 2, b // 2, xh, xl)

                def half(h, t, place):
                    i = GLA_HALVES[h].get((t, place))
                    if i is not None:
                        b = gla_block("g0", h) + i // 2
                        product(b, b % 2, b // 2, xh, xl, chunks=range(C // 2) if i % 2 == 0 else range(C // 2, C))

                def turn_v(h, e):
                    evacuated(pe, gla_block(f"v{e}", h))
                    if e:
                        pe.wait_ge(act_step, AS["v turned", h, 0])
                    elif h == 0:
                        pe.wait_ge(act_step, AS["z", 0])
                    for t in range(TT):
                        m = pe.transpose(banks[:, 2, t * P:t * P + P], g_vT[:, e, t * P:t * P + P], pc("ident"))
                    PE.did(m, "v turned", h, e)

                def turn_o(n):
                    h, t = divmod(n, TT)
                    pe.wait_ge(dve_step, VS["o normed", n])
                    if n >= 2 and n % 2 == 0:
                        pe.wait_ge(dve_step, VS["o gated", (n - 2) // TT, (n - 2) % TT // 2])
                    for e in range(2):
                        m = pe.transpose(banks[:, 4, e * 256 + (t % 2) * P:e * 256 + (t % 2) * P + P],
                                         g_on[:, n % 2, e * P:e * P + P], pc("ident"))
                    PE.did(m, "o turned", n)

                plain(B_GLA + 2)
                plain(B_GLA + 3)
                turn_v(0, 0)
                plain(B_GLA + 4)
                for h in range(GH):
                    for t in range(TT):
                        n = 4 * h + t
                        ts = slice(t * P, t * P + P)
                        if t == 0:
                            pe.wait_ge(dve_step, VS["k end", h])
                        if n:
                            pe.wait_ge(dve_step, VS["att masked", n - 1])
                        PE.did(pe.matmul(banks[:, 3, 0:P], g_kd[:, h, ts], g_qd[:, h, ts], start=True, stop=True),
                               "att", n)
                        if n:
                            pe.wait_ge(dve_step, VS["state", n - 1])
                        else:
                            pe.wait_ge(act_step, AS["z", GH - 1])
                        PE.did(pe.transpose(banks[:, 7, 256:256 + P], g_ke[:, h, ts], pc("ident")), "k turned", n)
                        if t == 0:
                            turn_v(h, 1)
                            if h:
                                turn_o(n - 1)
                        half(h, t, 0)
                        pe.wait_ge(act_step, AS["k turned", n])
                        if t == 0:
                            pe.wait_ge(act_step, AS["v turned", h, 1])
                        vs = g_v[:, h % 2, t, :]
                        m = pe.matmul(banks[:, 7, 0:256], g_ket[0:64, n % 2, :], vs[0:64], start=True, stop=True)
                        if t < 3:
                            m = pe.matmul(banks[:, 2, 0:256], g_ket[64:P, n % 2, :], vs[64:P], start=True, stop=True)
                        PE.did(m, "u", n)
                        pe.wait_ge(dve_step, VS["att masked", n])
                        if n >= 2:
                            pe.wait_ge(dve_step, VS["o normed", n - 2])
                        o = banks[:, 5 + n % 2, 0:256]
                        PE.did(pe.matmul(o, g_att[:, n % 2, :], vs, start=True, stop=True, skip_group_check=True))
                        for k in range(2):
                            if k:
                                half(h, t, 1)
                            c = 2 * t + k
                            if c:
                                pe.wait_ge(dve_step, VS["S", h, c])
                                r = slice(64 * k, 64 * k + 64)
                                PE.did(pe.matmul(o[r], g_qd[:, h, t * P + 64 * k:t * P + 64 * k + 64],
                                                 g_S[:, c % 2, :], start=False, stop=True, skip_group_check=True),
                                       "inter", h, c)
                        if t:
                            turn_o(n - 1)
                        if t == 3 and h + 1 < GH:
                            turn_v(h + 1, 0)
                        half(h, t, 2)
                turn_o(TT * GH - 1)
                products(B_GLA_OUT, C, g_oh, g_ol, [VS["mix1 split", c // 2, 1] for c in range(C)])
                norm_sums("ln1", (s1, s2))
                mlp(B_MLP1, 0, [VS["ln1 split", c] for c in range(C)])
                norm_sums("ln2", (s1, s2))
                if STOP > 1:
                    Z = banks[:, 2:5, :].rearrange("p a b -> p (a b)")
                    R = banks[:, 5:8, :].rearrange("p a b -> p (a b)")

                    def project(c, part):
                        b = B_SB + 3 * c + part
                        evacuated(pe, b - 1)
                        if part == 0 and c:
                            pe.wait_ge(act_step, AS["sv turned", c - 1])
                        product(b, b % 2, None, xh, xl,
                                [VS["ln2 split", k] for k in range(C)] if c == 0 else None, gb[0])

                    def turn_v(c):
                        evacuated(pe, B_SB + 3 * c + 2)
                        for t in range(TT):
                            m = pe.transpose(gb[0][:, t * P:t * P + P], t_vT[:, c % 2, t * P:t * P + P], pc("ident"))
                        PE.did(m, "sv turned", c)

                    def scores(h):
                        r, c = slice(64 * (h % 2), 64 * (h % 2) + 64), h // 2
                        evacuated(pe, B_SB + 3 * c)
                        evacuated(pe, B_SB + 3 * c + 1)
                        if h:
                            pe.wait_ge(dve_step, VS["sb z", h - 1])
                        for i in range(TT):
                            m = pe.matmul(Z[:, TRI[i]:TRI[i] + T - i * P], t_k[r, c % 2, i * P:i * P + P],
                                          t_q[r, c % 2, i * P:T], start=True, stop=True, skip_group_check=True)
                        PE.did(m, "sb z", h)

                    def sums(h):
                        pe.wait_ge(dve_step, VS["sb sp", h])
                        for i in range(TT):
                            for j in range(i, TT):
                                for part, tile in enumerate((t_sh, t_sl)):
                                    m = pe.matmul(R[:, TRI[i] + (j - i) * P:TRI[i] + T - i * P],
                                                  t_one[:, 1 if j == i else 0, :],
                                                  tile[:, TRI[j]:TRI[j] + T - j * P],
                                                  start=(j == i and part == 0), stop=(j == TT - 1 and part == 1),
                                                  skip_group_check=True)
                        PE.did(m, "sb R", h)

                    def outputs(h):
                        r0, c = 64 * (h % 2), h // 2
                        pe.wait_ge(act_step, AS["sb w", h])
                        if h >= 2:
                            pe.wait_ge(dve_step, VS["sb split", c - 1])
                        for i in range(TT):
                            m = pe.matmul(gb[1][r0:r0 + 64, i * P:T], t_v[:, c % 2, i * P + r0:i * P + r0 + 64],
                                          t_e[:, h % 2, TRI[i]:TRI[i] + T - i * P], start=(i == 0), stop=(i == 3),
                                          skip_group_check=True)
                        PE.did(m, "sb o", h)

                    for part in range(3):
                        project(0, part)
                    turn_v(0)
                    scores(0)
                    for h in range(SH):
                        c = h // 2 + 1
                        if h + 1 < SH:
                            scores(h + 1)
                        if h:
                            outputs(h - 1)
                        if c < C:
                            project(c, 2 if h % 2 else 0)
                        sums(h)
                        if c < C:
                            if h % 2:
                                turn_v(c)
                            else:
                                project(c, 1)
                    outputs(SH - 1)
                    pe.wait_ge(dve_step, VS["sb split", C - 1])
                    products(B_SB_OUT, C, t_oh, t_ol)
                    norm_sums("ln3", (s1, s2))
                    mlp(B_MLP2, 32, [VS["ln3 split", c] for c in range(C)])
                    norm_sums("ln4", (s1, s2))
                if STOP > 2:
                    norm_sums("rms1", (s2,))
                    products(B_MIX, 17, chunk_ready=[VS["rms1 split", c] for c in range(C)])
                    mixer_pe(pe)
                    pe.wait_ge(dve_step, VS["la out", AH - 1])
                    products(B_MIX_OUT, C, chunk_ready=[VS["mix split", c] for c in range(C)])
                    norm_sums("rms2", (s2,))
                    mlp(B_MLP3, 64, [VS["rms2 split", c] for c in range(C)])

            def mixer_pe(pe):
                pe.wait_ge(par2_in, 16)
                for b in range(B_MIX + 9, B_MIX + 13):
                    evacuated(pe, b)
                for t in range(TT):
                    if t >= 2:
                        pe.wait_ge(act_step, AS["mv turned", t - 2])
                    for h in range(MH):
                        m = pe.transpose(banks[:, 2 + t % 2, h * P:h * P + P], m_vT[:, h, t * P:t * P + P], pc("ident"))
                    PE.did(m, "mv turned", t)
                pe.wait_ge(act_step, AS["mv turned", 3])
                for k, (name, tile) in enumerate((("ml G", m_I), ("ml e", m_u))):
                    pe.wait_ge(*((dve_step, VS["ml G"]) if k == 0 else (act_step, AS["ml e"])))
                    for t in range(TT):
                        m = pe.transpose(banks[:, 2 + k, t * 64:t * 64 + 64], tile[:, t * P:t * P + P],
                                         pc("ident", 0, 64, rows=64))
                    PE.did(m, name)
                pe.wait_ge(dve_step, VS["la sq"])
                PE.did(pe.matmul(banks[:, 4, :], pc("ones"), s1[:, :], start=True, stop=True), "la sum", 0)
                pe.wait_ge(act_step, AS["la sq", 2])
                PE.did(pe.matmul(banks[:, 5, :], pc("ones"), s2[:, :], start=True, stop=True), "la sum", 1)

                Z = banks[:, 2:5, :].rearrange("p a b -> p (a b)")
                STEPS = 2 * MH

                def scores(j):
                    h, d = divmod(j, 2)
                    r = slice(64 * (h % 2), 64 * (h % 2) + 64)
                    q, k = m_qk[r, h // 2, :], m_qk[r, 2 + h // 2, :]
                    if j:
                        pe.wait_ge(dve_step, VS["ml P", j - 1])
                    for i in range(TT):
                        ts = slice(i * P, T) if d == 0 else slice(0, i * P + P)
                        o = TRI[3 - i if d else i]
                        m = pe.matmul(Z[:, o:o + ts.stop - ts.start], k[:, i * P:i * P + P], q[:, ts],
                                      start=True, stop=True, skip_group_check=True)
                    PE.did(m, "ml z", j)

                def maxima(j):
                    h, d = divmod(j, 2)
                    if j:
                        pe.wait_ge(dve_step, VS["ml Md", j - 1])
                    PE.did(pe.matmul(banks[:, 5, :], pc("sel", (4 * d + h) * P, (4 * d + h + 1) * P, rows=64),
                                     m_M[:, :], start=True, stop=True), "ml M", j)

                def numerators(j):
                    h, d = divmod(j, 2)
                    pe.wait_ge(dve_step, VS["ml P", j])
                    if j:
                        pe.wait_ge(dve_step, VS["ml h", j - 1])
                    for t in range(TT):
                        ss = range(t, TT) if d else range(t + 1)
                        for i in ss:
                            o = TRI[3 - i] + t * P if d else TRI[i] + (t - i) * P
                            m = pe.matmul(banks[:, 6 + t // 2, (t % 2) * 256:(t % 2) * 256 + 129],
                                          m_P[j % 2][:, o:o + P], m_v[:, i, h, 0:129], start=(i == ss[0]),
                                          stop=(i == ss[-1]), skip_group_check=True)
                    PE.did(m, "ml num", j)

                def turn_h(h):
                    pe.wait_ge(dve_step, VS["ml hn", h])
                    if h:
                        pe.wait_ge(dve_step, VS["out h", h - 1])
                    for t in range(TT):
                        m = pe.transpose(banks[:, 0, t * P:t * P + P], m_hn[:, t, :], pc("ident"))
                    PE.did(m, "ml hT", h)

                pe.wait_ge(dve_step, VS["ml cols"])
                pe.wait_ge(act_step, AS["la rstd", 1])
                maxima(0)
                scores(0)
                maxima(1)
                for j in range(STEPS):
                    if j + 1 < STEPS:
                        scores(j + 1)
                    numerators(j)
                    if j + 2 < STEPS:
                        maxima(j + 2)
                    if j % 2 and j > 1:
                        turn_h(j // 2 - 1)
                turn_h(MH - 1)

                v_cols = pc("wukv").rearrange("p (h n) -> p h n", n=256)[:, :, P:2 * P]
                pe.wait_ge(dve_step, VS["la c"])
                pe.wait_ge(dve_step, VS["ml h", STEPS - 1])
                for t in range(TT):
                    PE.did(pe.matmul(banks[:, 4 + t, :], m_ckv[:, t * P:t * P + P], v_cols, start=True, stop=True),
                           "la v", t)

                def before(h, step):
                    if step == 0:
                        if h:
                            pe.wait_ge(dve_step, VS["la key", h - 1])
                        else:
                            pe.wait_ge(act_step, AS["la v", 3])
                        for bank, width, at in ((2, P, 0), (3, 64, P)):
                            for k in range(2):
                                o = k * 768 + h * 192 + at
                                pe.matmul(banks[0:width, bank, :], pc("wuq", o, o + width), m_cq[:, k, :],
                                          start=(k == 0), stop=(k == 1))
                        PE.did(pe.matmul(banks[:, 4, :], pc("wukv", h * 256, h * 256 + 128), m_ckv[:, :],
                                         start=True, stop=True), "la n", h)
                    if step in (1, 2):
                        side = step - 1
                        pe.wait_ge(act_step, AS["la nsq", h, side])
                        if side:
                            pe.wait_ge(act_step, AS["la nrstd", h, 0])
                        elif h:
                            pe.wait_ge(act_step, AS["la nrstd", h - 1, 1])
                        n2, r2 = ((sq[:, 0, :], sq[0:64, 1, :]), (tmp[:, 0, :], tmp[0:64, 1, :]))[side]
                        pe.matmul(banks[:, 5, :], pc("ones"), n2, start=True, stop=False)
                        PE.did(pe.matmul(banks[:, 5, :], pc("ones", rows=64), r2, start=False, stop=True),
                               "la nsum", h, side)
                    if step in (3, 4):
                        side = step - 3
                        pe.wait_ge(dve_step, VS["la pre", h, side])
                        if side:
                            pe.wait_ge(dve_step, VS["la rope", h, 0])
                        PE.did(pe.matmul(banks[0:64, 3, :], pc("swap", rows=64), a_pre[side][:, :], start=True,
                                         stop=True), "la swap", h, side)

                def turn_p(n):
                    pe.wait_ge(dve_step, VS["la p", n])
                    if n:
                        pe.wait_ge(act_step, AS["la pT", n - 1])
                    for i in range(TT):
                        m = pe.transpose(banks[:, 0, i * P:i * P + P], a_p[:, n % 2, i * P:i * P + P], pc("ident"))
                    PE.did(m, "la pT", n)

                pe.wait_ge(dve_step, VS["out h", MH - 1])
                for step in range(5):
                    before(0, step)
                for h in range(AH):
                    for side in range(2):
                        pe.wait_ge(dve_step, VS["la rope", h, side])
                    for t in range(TT):
                        n = 4 * h + t
                        ts = slice(t * P, t * P + P)
                        if n >= 2:
                            pe.wait_ge(act_step, AS["la e", n - 2])
                        pe.matmul(banks[:, 6 + n % 2, :], a_n[0][h % 2][:, ts], a_n[1][h % 2][:, :], start=True,
                                  stop=False)
                        PE.did(pe.matmul(banks[:, 6 + n % 2, :], a_r[0][h % 2][:, ts], a_r[1][h % 2][:, :],
                                         start=False, stop=True), "la s", n)
                        if t:
                            turn_p(n - 1)
                        if h + 1 < AH:
                            before(h + 1, t)
                    turn_p(4 * h + 3)
                    if h + 1 < AH:
                        before(h + 1, 4)
                    pe.wait_ge(act_step, AS["la pT", 4 * h + 3])
                    if h:
                        pe.wait_ge(dve_step, VS["la out", h - 1])
                    for i in range(TT):
                        m = pe.matmul(banks[:, 1, :], a_v[:, i, h * P:h * P + P], a_pT[:, i, :], start=(i == 0),
                                      stop=(i == 3))
                    PE.did(m, "la out", h)

            program(pe)

        @block.scalar
        def _(act):
            def last():
                act.wait_ge(act_step, AS.count)

            def exp_and_ln():
                act.preload_act_table_set("natural_log_exp_and_others")

            def bank(b):
                act.wait_ge(block_done, b + 1)
                return gb[b % 2]

            def mlp(b0, u0):
                for q in range(FFQ):
                    b = b0 + (2 * q - 1 if q else 0) * C
                    u = u0 + C * q
                    with act.Fori(0, C // 2) as i:
                        for j in range(2):
                            act.wait_ge(up_squared, i * 2 + (u + j + 1))
                            act.wait_ge(block_done, i * 2 + (b + j + 1))
                            nc.scalar.activation(relu[:, j, :], gb[(b + j) % 2], ACT.Relu).then_inc(relu_done, 1)

            def squares(name, b0=None, normed=None):
                for c in range(C):
                    if b0 is None:
                        act.wait_ge(act_step, AS[normed, "out", c])
                    else:
                        evacuated(act, b0 + c)
                    if c >= 2:
                        act.wait_ge(dve_step, VS[name, "sq added", c - 2])
                    AS.did(nc.scalar.activation(sq[:, c % 2, :], res[:, c, :], ACT.Square), name, "sq", c)

            def norm(name, g, b, eps, center, split):
                act.wait_ge(dve_step, VS[name, "var"])
                AS.did(nc.scalar.activation(rstd[:, :], tmp2[:, 0, :], ACT.Ln, bias=pc(eps)))
                last()
                AS.did(nc.scalar.activation(rstd[:, :], rstd[:, :], ACT.Exp, scale=-0.5), name, "rstd")
                for c in range(C):
                    act.wait_ge(dve_step, VS[name, "scaled", c])
                    if center:
                        AS.did(nc.scalar.activation(res[:, c, :], tmp[:, c % 2, :], ACT.Identity,
                                                    scale=pc(g[0], g[1] + c, g[1] + c + 1),
                                                    bias=pc(b[0], b[1] + c, b[1] + c + 1)), name, "out", c)
                        if split:
                            last()
                            AS.did(nc.scalar.activation(xh[:, c, :], res[:, c, :], ACT.Copy), name, "hi", c)
                    else:
                        AS.did(nc.scalar.activation(tmp2[:, c % 2, :], tmp[:, c % 2, :], ACT.Copy,
                                                    scale=pc(g[0], g[1] + c, g[1] + c + 1)), name, "out", c)
                        last()
                        AS.did(nc.scalar.activation(xh[:, c, :], tmp2[:, c % 2, :], ACT.Copy), name, "hi", c)

            def mixer_act(act):
                act.dma_start(par2[:, :], PAR[:, NPAR1:NPAR]).then_inc(par2_in, 16)
                act.dma_start(a_posi, POS).then_inc(pos_in, 16)
                act.wait_ge(dve_step, VS["la ang"])
                AS.did(nc.scalar.activation(a_sin[:, :], a_ang[:, 0, :], ACT.Sin))
                AS.did(nc.scalar.activation(a_ang[:, 1, :], a_ang[:, 0, :], ACT.Abs))
                last()
                AS.did(nc.scalar.activation(a_cos[:, :], a_ang[:, 1, :], ACT.Sin, scale=-1.0,
                                            bias=pc("half_pi", rows=64)), "la tables")
                for c in range(4):
                    act.wait_ge(dve_step, VS["ml conv", c])
                    if c >= 2:
                        act.wait_ge(dve_step, VS["ml qk", c - 2])
                    AS.did(nc.scalar.activation(tmp[:, c % 2, :], m_qk[:, c, :], ACT.Sigmoid), "ml sig", c)
                for c in range(4):
                    evacuated(act, B_MIX + 5 + c)
                    AS.did(nc.scalar.activation(m_o[:, c, :], m_o[:, c, :], ACT.Sigmoid), "ml o", c)
                exp_and_ln()
                act.wait_ge(dve_step, VS["ml F"])
                AS.did(nc.scalar.activation(m_u[:, :], m_F[:, :], ACT.Abs))
                last()
                AS.did(nc.scalar.activation(m_u[:, :], m_u[:, :], ACT.Exp, scale=-1.0))
                last()
                AS.did(nc.scalar.activation(m_u[:, :], m_u[:, :], ACT.Ln, bias=pc("one", 0, 1, rows=64)), "ml l")
                act.wait_ge(dve_step, VS["ml m"])
                AS.did(nc.scalar.activation(m_u[:, :], m_F[:, :], ACT.Exp, scale=-1.0), "ml e")
                for t in range(TT):
                    act.wait_ge(pe_step, PE["mv turned", t])
                    AS.did(nc.scalar.activation(m_v[:, t, :, 0:P], banks[:, 2 + t % 2, :].rearrange(
                        "p (h n) -> p h n", n=P), ACT.Copy), "mv turned", t)
                for k in range(2):
                    evacuated(act, B_MIX + 13 + k)
                    AS.did(nc.scalar.activation(sq[:, k, :], m_cq[:, k, :], ACT.Square), "la sq", k)
                evacuated(act, B_MIX + 15)
                AS.did(nc.scalar.activation(s2[:, :], m_ckv[:, :], ACT.Square), "la sq", 2)
                for k, scale in enumerate((D / 256, D / 128)):
                    act.wait_ge(pe_step, PE["la sum", k])
                    r = (mean, rstd)[k]
                    AS.did(nc.scalar.activation(r[:, :], banks[:, 4 + k, :], ACT.Ln, scale=scale, bias=pc("rms_eps")))
                    last()
                    AS.did(nc.scalar.activation(r[:, :], r[:, :], ACT.Exp, scale=-0.5), "la rstd", k)
                STEPS = 2 * MH

                def weights(j):
                    h, d = divmod(j, 2)
                    E = m_E[j % 2]
                    act.wait_ge(dve_step, VS["ml Md", j])
                    if j >= 2:
                        act.wait_ge(dve_step, VS["ml P", j - 2])
                    for i in range(TT):
                        G = m_Gc[:, i, 32 * d + h:32 * d + h + 1]
                        a, b = (0, i * P) if d else (i * P + P, T)
                        o = TRI[3 - i] if d else TRI[i] + P
                        od = TRI[3 - i] + i * P if d else TRI[i]
                        if b > a:
                            AS.did(nc.scalar.activation(E[:, o:o + b - a], m_Mb[:, a:b], ACT.Exp, bias=G, scale=-1.0))
                        AS.did(nc.scalar.activation(E[:, od:od + P], m_Md[:, i * P:i * P + P], ACT.Exp, bias=G,
                                                    scale=-1.0), *(("ml E", j) if i == 3 else ()))

                def head_rstd(h):
                    act.wait_ge(dve_step, VS["ml h", 2 * h + 1])
                    if h:
                        act.wait_ge(dve_step, VS["ml hn", h - 1])
                    for t in range(TT):
                        AS.did(nc.scalar.activation(tmp[:, 0, t * P:t * P + P], m_h[h % 2][:, t, :], ACT.Square,
                                                    accum_out=m_ss[:, t:t + 1]))
                    last()
                    AS.did(nc.scalar.activation(m_ss[:, :], m_ss[:, :], ACT.Ln, scale=1 / 128.0, bias=pc("rms_eps")))
                    last()
                    AS.did(nc.scalar.activation(m_ss[:, :], m_ss[:, :], ACT.Exp, scale=-0.5), "ml rstd", h)

                weights(0)
                weights(1)
                for j in range(STEPS):
                    act.wait_ge(pe_step, PE["ml num", j])
                    if j:
                        act.wait_ge(dve_step, VS["ml h", j - 1])
                    dens = banks[:, 6:8, :].rearrange("p a (b c) -> p (a b) c", c=256)[:, :, 128]
                    AS.did(nc.scalar.activation(m_dn[:, :], dens, ACT.Abs), "ml den", j)
                    if j + 2 < STEPS:
                        weights(j + 2)
                    if j % 2 == 0 and j:
                        head_rstd(j // 2 - 1)
                head_rstd(MH - 1)

                for t in range(TT):
                    act.wait_ge(pe_step, PE["la v", t])
                    AS.did(nc.scalar.activation(a_v[:, t, :], banks[:, 4 + t, :], ACT.Copy), "la v", t)
                act.wait_ge(dve_step, VS["ml hn", MH - 1])
                AS.did(nc.scalar.activation(tmp[0:64, 1, :], m_kpe[:, :], ACT.Square))

                def before(h, step):
                    if step == 0:
                        act.wait_ge(pe_step, PE["la n", h])
                        if h:
                            act.wait_ge(pe_step, PE["la nsum", h - 1, 1])
                        AS.did(nc.scalar.activation(sq[:, 0, :], banks[:, 2, :], ACT.Square))
                        AS.did(nc.scalar.activation(sq[0:64, 1, :], banks[0:64, 3, :], ACT.Square), "la nsq", h, 0)
                        AS.did(nc.scalar.activation(tmp[:, 0, :], banks[:, 4, :], ACT.Square), "la nsq", h, 1)
                    if step in (1, 2):
                        side = step - 1
                        r = (rstd, mean)[side][:, :]
                        act.wait_ge(pe_step, PE["la nsum", h, side])
                        if h:
                            act.wait_ge(dve_step, VS["la pre", h - 1, side])
                        AS.did(nc.scalar.activation(r, banks[:, 5, :], ACT.Ln, scale=D / 192, bias=pc("rms_eps")))
                        last()
                        AS.did(nc.scalar.activation(r, r, ACT.Exp, scale=-0.5), "la nrstd", h, side)

                def copy_p(n):
                    h, t = divmod(n, TT)
                    act.wait_ge(pe_step, PE["la pT", n])
                    if h and t == 0:
                        act.wait_ge(pe_step, PE["la out", h - 1])
                    AS.did(nc.scalar.activation(a_pT[:, :, t * P:t * P + P], banks[:, 0, :].rearrange(
                        "p (i t) -> p i t", t=P), ACT.Copy), "la pT", n)

                for step in range(3):
                    before(0, step)
                for h in range(AH):
                    for t in range(TT):
                        n = 4 * h + t
                        act.wait_ge(dve_step, VS["la max", n])
                        if n >= 2:
                            act.wait_ge(pe_step, PE["la pT", n - 2])
                        AS.did(nc.scalar.activation(a_p[:, n % 2, :], banks[:, 6 + n % 2, :], ACT.Exp,
                                                    scale=192 ** -0.5, bias=m_dn[:, n % 2:n % 2 + 1],
                                                    accum_out=m_ss[:, n % 2:n % 2 + 1]), "la e", n)
                        if t:
                            copy_p(n - 1)
                        if h + 1 < AH:
                            before(h + 1, t)
                    copy_p(4 * h + 3)

            act.wait_ge(par_in, 16)
            for c in range(C):
                act.wait_ge(x_in[c], 16)
                AS.did(nc.scalar.activation(xh[:, c, :], res[:, c, :], ACT.Copy), "x hi", c)
            b = bank(0)
            nc.scalar.activation(g_a1[:, :], b[0:16, :], ACT.Copy).then_inc(bank_free[0], 1)
            exp_and_ln()

            def softplus(h):
                act.wait_ge(pe_step, PE["gate", h])
                z, e = g_ke[:, h, :], g_qd[:, h, :]
                AS.did(nc.scalar.activation(z, banks[:, GATE_BANKS[h], :], ACT.Identity, bias=pc("ba", h, h + 1)),
                       "z", h)
                last()
                AS.did(nc.scalar.activation(e, z, ACT.Abs))
                last()
                AS.did(nc.scalar.activation(e, e, ACT.Exp, scale=-1.0))
                last()
                AS.did(nc.scalar.activation(e, e, ACT.Ln, bias=pc("one", 0, 1)), "l", h)

            def decays(h):
                act.wait_ge(dve_step, VS["to end", h])
                b = g_kd[:, h, :]
                AS.did(nc.scalar.activation(g_qd[:, h, :], b, ACT.Exp, scale=1 / 16.0))
                AS.did(nc.scalar.activation(g_dec[:, h, :], b.rearrange("p (n c) -> p n c", c=GC)[:, :, GC - 1],
                                            ACT.Exp, scale=1 / 16.0))
                last()
                AS.did(nc.scalar.activation(b, b, ACT.Exp, scale=-1 / 16.0))
                AS.did(nc.scalar.activation(g_ke[:, h, :], g_ke[:, h, :], ACT.Exp, scale=1 / 16.0), "decays", h)

            def v_turned(h, e):
                act.wait_ge(pe_step, PE["v turned", h, e])
                AS.did(nc.scalar.activation(g_v[:, h % 2, :, e * P:e * P + P],
                                            banks[:, 2, :].rearrange("p (t n) -> p t n", n=P), ACT.Copy),
                       "v turned", h, e)

            softplus(0)
            softplus(1)
            decays(0)
            softplus(2)
            decays(1)
            softplus(3)
            decays(2)
            decays(3)
            v_turned(0, 0)
            for h in range(GH):
                for t in range(TT):
                    n = 4 * h + t
                    act.wait_ge(pe_step, PE["k turned", n])
                    AS.did(nc.scalar.activation(g_ket[:, n % 2, :], banks[:, 7, 256:256 + P], ACT.Copy),
                           "k turned", n)
                    if t == 0:
                        v_turned(h, 1)
                    if t == 2:
                        evacuated(act, gla_block("g0", h))
                        evacuated(act, gla_block("g1", h))
                        AS.did(nc.scalar.activation(tmp[:, :, :], g_g[:, :, :], ACT.Sigmoid), "g sig", h)
                        exp_and_ln()
                    act.wait_ge(pe_step, PE["inter", h, 2 * t + 1])
                    if n >= 2:
                        act.wait_ge(dve_step, VS["o normed", n - 2])
                    s = g_ss[:, 2 * (n % 2):2 * (n % 2) + 1]
                    d = g_ss[:, 2 * (n % 2) + 1:2 * (n % 2) + 2]
                    AS.did(nc.scalar.activation(g_junk[:, :], banks[:, 5 + n % 2, 0:256], ACT.Square, accum_out=s))
                    last()
                    AS.did(nc.scalar.activation(d, s, ACT.Ln, scale=1 / 256.0, bias=pc("rms_eps")))
                    last()
                    AS.did(nc.scalar.activation(d, d, ACT.Exp, scale=-0.5), "o rstd", n)
                    if t == 3 and h + 1 < GH:
                        v_turned(h + 1, 0)
            squares("ln1", B_GLA_OUT)
            norm("ln1", ("ln", 0), ("ln", 8), "ln_eps", True, True)
            mlp(B_MLP1, 0)
            squares("ln2", B_MLP1 + 7 * C)
            norm("ln2", ("ln", 16), ("ln", 24), "ln_eps", True, STOP > 1)
            if STOP > 1:
                AS.did(nc.scalar.activation(t_one[:, 0, :], pc("one"), ACT.Copy))
                AS.did(nc.scalar.activation(t_one[:, 1, :], pc("tri"), ACT.Copy), "ones split")

                def v_turned(c):
                    act.wait_ge(pe_step, PE["sv turned", c])
                    if c >= 2:
                        act.wait_ge(pe_step, PE["sb o", 2 * c - 3])
                    AS.did(nc.scalar.activation(t_v[:, c % 2, :], gb[0], ACT.Copy), "sv turned", c)

                def softplus(h):
                    e = t_e[:, h % 2, :]
                    act.wait_ge(dve_step, VS["sb m", h])
                    AS.did(nc.scalar.activation(e, e, ACT.Exp))
                    last()
                    AS.did(nc.scalar.activation(e, e, ACT.Ln, bias=pc("one", 0, 1)), "sb l", h)

                def take_pair(c, part):
                    b = B_SB + 3 * c + part
                    if c >= 2:
                        act.wait_ge(pe_step, PE[("sv turned", c - 2) if part == 2 else ("sb z", 2 * c - 3)])
                    bank(b)
                    nc.scalar.activation((t_q, t_k, t_vT)[part][:, c % 2, :], gb[0], ACT.Copy,
                                         scale=0.125 if part == 0 else 1.0).then_inc(bank_free[b % 2], 1)

                for part in range(3):
                    take_pair(0, part)
                v_turned(0)
                softplus(0)
                for h in range(SH):
                    c = h // 2 + 1
                    if h + 1 < SH:
                        softplus(h + 1)
                    if c < C:
                        take_pair(c, 2 if h % 2 else 0)
                    act.wait_ge(dve_step, VS["sb lw", h])
                    AS.did(nc.scalar.activation(t_e[:, h % 2, :], t_sp[:, h % 2, :], ACT.Exp), "sb w", h)
                    if c < C:
                        if h % 2:
                            v_turned(c)
                        else:
                            take_pair(c, 1)
                squares("ln3", B_SB_OUT)
                norm("ln3", ("ln", 32), ("ln", 40), "ln_eps", True, True)
                mlp(B_MLP2, 32)
                squares("ln4", B_MLP2 + 7 * C)
                norm("ln4", ("ln", 48), ("ln", 56), "ln_eps", True, False)
            if STOP > 2:
                squares("rms1", normed="ln4")
                norm("rms1", ("gmix", 0), None, "rms_eps", False, True)
                mixer_act(act)
                squares("rms2", B_MIX_OUT)
                norm("rms2", ("gffn", 0), None, "rms_eps", False, True)
                mlp(B_MLP3, 64)

        @block.vector
        def _(dve):
            def last():
                dve.wait_ge(dve_step, VS.count)

            def take(dst, b, scale=1.0, bank=None):
                dve.wait_ge(block_done, b + 1)
                nc.vector.tensor_scalar(dst, gb[b % 2] if bank is None else bank, scale, None, ALU.mult).then_inc(bank_free[b % 2], 1)

            def add_residual(name, b0, alpha, sums):
                for c in range(C):
                    b = b0 + c
                    dve.wait_ge(block_done, b + 1)
                    nc.vector.scalar_tensor_tensor(out=res[:, c, :], in0=res[:, c, :], scalar=alpha, in1=gb[b % 2],
                                                   op0=ALU.mult, op1=ALU.add).then_inc(bank_free[b % 2], 1)
                    evacuated(dve, b)
                    if sums:
                        add_sums(name, c, sums)

            def add_sums(name, c, sums):
                if sums == 2:
                    if c == 0:
                        VS.did(nc.vector.tensor_copy(s1[:, :], res[:, c, :]))
                    else:
                        last()
                        VS.did(nc.vector.tensor_tensor(s1[:, :], s1[:, :], res[:, c, :], ALU.add),
                               *((name, "part", 0) if c == C - 1 else ()))
                dve.wait_ge(act_step, AS[name, "sq", c])
                if c == 0:
                    VS.did(nc.vector.tensor_copy(s2[:, :], sq[:, 0, :]), name, "sq added", 0)
                else:
                    dve.wait_ge(dve_step, VS[name, "sq added", c - 1])
                    VS.did(nc.vector.tensor_tensor(s2[:, :], s2[:, :], sq[:, c % 2, :], ALU.add), name, "sq added", c)
                if c == C - 1:
                    last()
                    VS.did(nc.vector.tensor_copy(sq[0:1, 0, 0:2], s2[0:1, 0:2]), name, "part", 1 if sums == 2 else 0)

            def norm(name, center, split):
                if center:
                    dve.wait_ge(pe_step, PE[name, "sum", 0])
                    VS.did(nc.vector.tensor_copy(mean[:, :], banks[:, 2, :]))
                    last()
                    VS.did(nc.vector.tensor_tensor(tmp2[:, 1, :], mean[:, :], mean[:, :], ALU.mult))
                    last()
                    dve.wait_ge(pe_step, PE[name, "sum", 1])
                    VS.did(nc.vector.tensor_tensor(tmp2[:, 0, :], banks[:, 3, :], tmp2[:, 1, :], ALU.subtract))
                    last()
                    VS.did(nc.vector.tensor_scalar(tmp2[:, 0, :], tmp2[:, 0, :], 0.0, None, ALU.max), name, "var")
                else:
                    dve.wait_ge(pe_step, PE[name, "sum", 0])
                    VS.did(nc.vector.tensor_copy(tmp2[:, 0, :], banks[:, 2, :]), name, "var")

                def low(c):
                    dve.wait_ge(act_step, AS[name, "hi", c])
                    src = res[:, c, :] if center else tmp2[:, c % 2, :]
                    VS.did(nc.vector.tensor_tensor(xl[:, c, :], src, xh[:, c, :].bitcast(F32), ALU.subtract),
                           name + " split", c)

                dve.wait_ge(act_step, AS[name, "rstd"])
                for c in range(C):
                    if c >= 2:
                        dve.wait_ge(act_step, AS[name, "out", c - 2])
                    if center:
                        VS.did(nc.vector.tensor_tensor(tmp[:, c % 2, :], res[:, c, :], mean[:, :], ALU.subtract))
                        last()
                        VS.did(nc.vector.tensor_tensor(tmp[:, c % 2, :], tmp[:, c % 2, :], rstd[:, :], ALU.mult),
                               name, "scaled", c)
                    else:
                        VS.did(nc.vector.tensor_tensor(tmp[:, c % 2, :], res[:, c, :], rstd[:, :], ALU.mult),
                               name, "scaled", c)
                    if split and c:
                        low(c - 1)
                if split:
                    low(C - 1)

            def split_pair(c):
                dve.wait_ge(pe_step, PE["sb o", 2 * c + 1])
                VS.did(nc.vector.tensor_copy(t_oh[:, c, :], gb[1]))
                last()
                VS.did(nc.vector.tensor_tensor(t_ol[:, c, :], gb[1], t_oh[:, c, :].bitcast(F32), ALU.subtract),
                       "sb split", c)

            def mlp(b0, u0, alpha, name, sums):
                def down(b, first):
                    with dve.Fori(0, C // 2) as i:
                        for j in range(2):
                            dve.wait_ge(block_done, i * 2 + (b + j + 1))
                            r = res[:, bass.ds(i * 2 + j, 1), :].rearrange("p a t -> p (a t)")
                            nc.vector.scalar_tensor_tensor(
                                out=r, in0=r, scalar=alpha if first else 1.0, in1=gb[(b + j) % 2],
                                op0=ALU.mult, op1=ALU.add).then_inc(bank_free[(b + j) % 2], 1)

                for q in range(FFQ):
                    b = b0 + (2 * q - 1 if q else 0) * C
                    u = u0 + C * q
                    with dve.Fori(0, C // 2) as i:
                        for j in range(2):
                            dve.wait_ge(relu_done, i * 2 + (u + j + 1))
                            nc.vector.scalar_tensor_tensor(out=tmp2[:, j, :], in0=gb[(b + j) % 2], scalar=0.0,
                                                           in1=relu[:, j, :], op0=ALU.max,
                                                           op1=ALU.mult).then_inc(bank_free[(b + j) % 2], 1)
                            dve.wait_ge(bank_free[(b + j) % 2], i + ((b + j) // 2 + 1))
                            h = hh[q % 2][:, bass.ds(i * 2 + j, 1), :].rearrange("p a t -> p (a t)")
                            l = hl[q % 2][:, bass.ds(i * 2 + j, 1), :].rearrange("p a t -> p (a t)")
                            nc.vector.tensor_scalar(h, tmp2[:, j, :], 1.0, None, ALU.mult).then_inc(up_squared, 1)
                            dve.wait_ge(up_squared, i * 2 + (u + j + 3))
                            nc.vector.tensor_tensor(l, tmp2[:, j, :], h.bitcast(F32),
                                                    ALU.subtract).then_inc(hidden_ready, 1)
                    if q:
                        down(b + C, q == 1)
                add_residual(name, b0 + 7 * C, 1.0, sums)

            def split_out(c, src):
                last()
                VS.did(nc.vector.tensor_scalar(xh[:, c, :], src, 1.0, None, ALU.mult))
                last()
                VS.did(nc.vector.tensor_tensor(xl[:, c, :], src, xh[:, c, :].bitcast(F32), ALU.subtract),
                       "mix split", c)

            def mixer_dve(dve):
                dve.wait_ge(pos_in, 16)
                ang, k = a_ang[:, 0, :], a_ang[:, 1, :]
                VS.did(nc.vector.tensor_scalar(ang, a_posi, pc("freq", rows=64), None, ALU.mult))
                last()
                VS.did(nc.vector.tensor_scalar(k, ang, 1 / TWO_PI, ROUND, ALU.mult, ALU.add))
                last()
                VS.did(nc.vector.tensor_scalar(k, k, ROUND, None, ALU.subtract))
                for part in TWO_PI_PARTS:
                    last()
                    VS.did(nc.vector.scalar_tensor_tensor(out=ang, in0=k, scalar=-part, in1=ang, op0=ALU.mult,
                                                          op1=ALU.add))
                last()
                VS.did(nc.vector.tensor_scalar(ang, ang, 3.1415925, -3.1415925, ALU.min, ALU.max), "la ang")
                VS.did(nc.vector.memset(m_v[:, :, :, P:P + 2], 1.0))

                def convolve(c):
                    w = [pc("convw", 5 * c + j, 5 * c + j + 1) for j in range(5)]
                    evacuated(dve, B_MIX + c)
                    VS.did(nc.vector.tensor_scalar(m_qk[:, c, :], m_raw[:, c, :], w[2], pc("convb", c, c + 1),
                                                   ALU.mult, ALU.add))
                    for n, j in enumerate((0, 1, 3, 4)):
                        last()
                        a, b = max(0, 2 - j), T - max(0, j - 2)
                        o = m_qk[:, c, a:b]
                        VS.did(nc.vector.scalar_tensor_tensor(out=o, in0=m_raw[:, c, a + j - 2:b + j - 2],
                                                              scalar=w[j], in1=o, op0=ALU.mult, op1=ALU.add),
                               *(("ml conv", c) if n == 3 else ()))

                for c in range(4):
                    take(m_raw[:, c, :], B_MIX + c)
                k = (B_MIX + 4) % 2
                dve.wait_ge(block_done, B_MIX + 5)
                VS.did(nc.vector.tensor_copy(m_F[:, :], banks[0:64, k, :]))
                nc.vector.tensor_copy(m_I[:, :], banks[64:P, k, :]).then_inc(bank_free[k], 1)
                last()
                VS.did(nc.vector.tensor_scalar(m_F[:, :], m_F[:, :], pc("bf", rows=64), None, ALU.add), "ml F")
                evacuated(dve, B_MIX + 4)
                VS.did(nc.vector.tensor_scalar(m_I[:, :], m_I[:, :], pc("bi", rows=64), None, ALU.add))
                for c in range(4):
                    convolve(c)
                    take(m_o[:, c, :], B_MIX + 5 + c)
                for c in range(4):
                    dve.wait_ge(act_step, AS["ml sig", c])
                    VS.did(nc.vector.scalar_tensor_tensor(out=m_qk[:, c, :], in0=m_qk[:, c, :],
                                                          scalar=0.125 if c < 2 else 1.0, in1=tmp[:, c % 2, :],
                                                          op0=ALU.mult, op1=ALU.mult), "ml qk", c)
                    take(m_vT[:, c, :], B_MIX + 9 + c)
                dve.wait_ge(act_step, AS["ml l"])
                VS.did(nc.vector.scalar_tensor_tensor(out=m_F[:, :], in0=m_F[:, :], scalar=0.0, in1=m_u[:, :],
                                                      op0=ALU.min, op1=ALU.subtract))
                last()
                for d in range(2):
                    r, step = slice(32 * d, 32 * d + 32), -1 if d else 1
                    VS.did(nc.vector.tensor_tensor_scan(m_B[r, ::step], zero[r, 0:T], m_F[r, ::step], 0.0,
                                                        ALU.add, ALU.add))
                last()
                VS.did(nc.vector.tensor_tensor(m_I[:, :], m_I[:, :], m_B[:, :], ALU.subtract), "ml G")
                last()
                for d in range(2):
                    r, step = slice(32 * d, 32 * d + 32), -1 if d else 1
                    VS.did(nc.vector.tensor_tensor_scan(m_M[r, ::step], m_I[r, ::step], zero[r, 0:T], 0.0,
                                                        ALU.max, ALU.add))
                last()
                VS.did(nc.vector.tensor_tensor(m_F[:, :], m_B[:, :], m_M[:, :], ALU.add), "ml m")
                for c in range(2):
                    take(m_cq[:, c, :], B_MIX + 13 + c)
                take(m_ckv[:, :], B_MIX + 15)
                dve.wait_ge(block_done, B_MIX + 17)
                nc.vector.tensor_copy(m_kpe[:, :], banks[0:64, (B_MIX + 16) % 2, :])\
                    .then_inc(bank_free[(B_MIX + 16) % 2], 1)
                dve.wait_ge(act_step, AS["la sq", 1])
                VS.did(nc.vector.tensor_tensor(s1[:, :], sq[:, 0, :], sq[:, 1, :], ALU.add), "la sq")
                dve.wait_ge(pe_step, PE["ml G"])
                VS.did(nc.vector.tensor_copy(m_Gc[:, :, :].rearrange("p a b -> p (a b)"), banks[:, 2, 0:256]))
                dve.wait_ge(pe_step, PE["ml e"])
                VS.did(nc.vector.tensor_copy(m_Ec[:, :, :].rearrange("p a b -> p (a b)"), banks[:, 3, 0:256]),
                       "ml cols")
                for k in range(2):
                    dve.wait_ge(act_step, AS["la rstd", 0])
                    VS.did(nc.vector.scalar_tensor_tensor(out=m_cq[:, k, :], in0=m_cq[:, k, :],
                                                          scalar=pc("gcq", k, k + 1), in1=mean[:, :], op0=ALU.mult,
                                                          op1=ALU.mult))
                dve.wait_ge(act_step, AS["la rstd", 1])
                VS.did(nc.vector.scalar_tensor_tensor(out=m_ckv[:, :], in0=m_ckv[:, :], scalar=pc("gckv"),
                                                      in1=rstd[:, :], op0=ALU.mult, op1=ALU.mult), "la c")
                Z = banks[:, 2:5, :].rearrange("p a b -> p (a b)")[:, 0:1280]
                STEPS = 2 * MH

                def maxima(j):
                    d = j % 2
                    dve.wait_ge(pe_step, PE["ml M", j])
                    if j:
                        dve.wait_ge(act_step, AS["ml E", j - 1])
                    VS.did(nc.vector.tensor_copy(m_Mb[:, :], banks[:, 5, :]))
                    last()
                    VS.did(nc.vector.tensor_tensor(m_Md[:, :].rearrange("p (a b) -> p a b", b=P),
                                                   m_Mb[:, :].rearrange("p (a b) -> p a b", b=P),
                                                   pc("neg_bw" if d else "neg_fw").unsqueeze(1)
                                                   .broadcast_to([P, 4, P]), ALU.add), "ml Md", j)

                def weigh(j):
                    dve.wait_ge(act_step, AS["ml E", j])
                    dve.wait_ge(pe_step, PE["ml z", j])
                    if j >= 2:
                        dve.wait_ge(pe_step, PE["ml num", j - 2])
                    VS.did(nc.vector.tensor_tensor(m_P[j % 2][:, :], Z, m_E[j % 2], ALU.mult), "ml P", j)

                def quotient(j):
                    h, d = divmod(j, 2)
                    hs = m_h[h % 2]
                    dve.wait_ge(act_step, AS["ml den", j])
                    VS.did(nc.vector.tensor_tensor(m_dn[:, :], m_dn[:, :], m_Ec[:, :, 32 * d + h], ALU.max))
                    last()
                    VS.did(nc.vector.reciprocal(m_dn[:, :], m_dn[:, :]))
                    last()
                    for t in range(TT):
                        num = banks[:, 6 + t // 2, (t % 2) * 256:(t % 2) * 256 + P]
                        if d == 0:
                            ins = nc.vector.tensor_scalar(hs[:, t, :], num, m_dn[:, t:t + 1], None, ALU.mult)
                        else:
                            ins = nc.vector.scalar_tensor_tensor(out=hs[:, t, :], in0=num,
                                                                 scalar=m_dn[:, t:t + 1], in1=hs[:, t, :],
                                                                 op0=ALU.mult, op1=ALU.add)
                        VS.did(ins, *(("ml h", j) if t == 3 else ()))
                    last()

                def normalise(h):
                    dve.wait_ge(act_step, AS["ml rstd", h])
                    if h:
                        dve.wait_ge(pe_step, PE["ml hT", h - 1])
                    for t in range(TT):
                        VS.did(nc.vector.tensor_scalar(m_hn[:, t, :], m_h[h % 2][:, t, :], m_ss[:, t:t + 1], None,
                                                       ALU.mult), *(("ml hn", h) if t == 3 else ()))

                def put_out(h):
                    dve.wait_ge(pe_step, PE["ml hT", h])
                    dve.wait_ge(act_step, AS["ml o", h])
                    VS.did(nc.vector.scalar_tensor_tensor(out=tmp2[:, 0, :], in0=gb[0], scalar=pc("gout", h, h + 1),
                                                          in1=m_o[:, h, :], op0=ALU.mult, op1=ALU.mult), "out h", h)
                    split_out(h, tmp2[:, 0, :])

                maxima(0)
                maxima(1)
                weigh(0)
                for j in range(STEPS):
                    if j + 1 < STEPS:
                        weigh(j + 1)
                    if j + 2 < STEPS:
                        maxima(j + 2)
                    quotient(j)
                    if j % 2 == 0 and j:
                        normalise(j // 2 - 1)
                    if j % 2 and j > 1:
                        put_out(j // 2 - 1)
                normalise(MH - 1)
                put_out(MH - 1)

                dve.wait_ge(act_step, AS["la tables"])

                def before(h, step):
                    def scaled(side):
                        n_g, r_g = (("gqn", "gqr"), ("gkn", "gkr"))[side]
                        r = (rstd, mean)[side]
                        dve.wait_ge(act_step, AS["la nrstd", h, side])
                        VS.did(nc.vector.scalar_tensor_tensor(out=a_n[side][h % 2][:, :],
                                                              in0=banks[:, 4 if side else 2, :], scalar=pc(n_g),
                                                              in1=r[:, :], op0=ALU.mult, op1=ALU.mult),
                               *(("la key", h) if side else ()))
                        VS.did(nc.vector.scalar_tensor_tensor(out=a_pre[side][:, :],
                                                              in0=m_kpe[:, :] if side else banks[0:64, 3, :],
                                                              scalar=pc(r_g, rows=64), in1=r[0:64, :],
                                                              op0=ALU.mult, op1=ALU.mult), "la pre", h, side)
                        last()
                        VS.did(nc.vector.tensor_tensor(a_r[side][h % 2][:, :], a_pre[side][:, :], a_cos[:, :],
                                                       ALU.mult))

                    def turned(side):
                        dve.wait_ge(pe_step, PE["la swap", h, side])
                        VS.did(nc.vector.tensor_tensor(a_swap[:, :], banks[0:64, 3, :], a_sin[:, :], ALU.mult))
                        last()
                        r = a_r[side][h % 2][:, :]
                        VS.did(nc.vector.tensor_tensor(r, r, a_swap[:, :], ALU.add), "la rope", h, side)
                        last()

                    if step == 2:
                        scaled(0)
                    if step == 3:
                        scaled(1)
                        turned(0)
                    if step == 4:
                        turned(1)

                def normal_p(n):
                    dve.wait_ge(act_step, AS["la e", n])
                    VS.did(nc.vector.reciprocal(m_dn[:, 3:4], m_ss[:, n % 2:n % 2 + 1]))
                    last()
                    VS.did(nc.vector.tensor_scalar(a_p[:, n % 2, :], a_p[:, n % 2, :], m_dn[:, 3:4], None, ALU.mult),
                           "la p", n)
                    last()

                for step in range(5):
                    before(0, step)
                for h in range(AH):
                    for t in range(TT):
                        n = 4 * h + t
                        dve.wait_ge(pe_step, PE["la s", n])
                        VS.did(nc.vector.reduce_max(m_dn[:, 2:3], banks[:, 6 + n % 2, :], AX.X))
                        last()
                        VS.did(nc.vector.tensor_scalar(m_dn[:, n % 2:n % 2 + 1], m_dn[:, 2:3], -(192 ** -0.5), None,
                                                       ALU.mult), "la max", n)
                        normal_p(n)
                        if h + 1 < AH:
                            before(h + 1, t)
                    if h + 1 < AH:
                        before(h + 1, 4)
                    dve.wait_ge(pe_step, PE["la out", h])
                    VS.did(nc.vector.tensor_copy(tmp2[:, 1, :], banks[:, 1, :]), "la out", h)
                    split_out(MH + h, tmp2[:, 1, :])

            dve.wait_ge(par_in, 16)
            VS.did(nc.vector.memset(g_att[:, :, :], 0.0))
            nc.vector.memset(tmp[:, :, :], 0.0).then_inc(up_squared, 2)
            for c in range(C):
                dve.wait_ge(act_step, AS["x hi", c])
                VS.did(nc.vector.tensor_tensor(xl[:, c, :], res[:, c, :], xh[:, c, :].bitcast(F32), ALU.subtract),
                       "x split", c)

            def log_gates(h):
                z, b = g_ke[:, h, :], g_kd[:, h, :]
                dve.wait_ge(act_step, AS["l", h])
                VS.did(nc.vector.scalar_tensor_tensor(out=z, in0=z, scalar=0.0, in1=g_qd[:, h, :], op0=ALU.min,
                                                      op1=ALU.subtract))
                last()
                VS.did(nc.vector.tensor_tensor_scan(b, pc("reset"), z, 0.0, ALU.mult, ALU.add))
                last()
                b3 = b.rearrange("p (n c) -> p n c", c=GC)
                VS.did(nc.vector.tensor_tensor(z.rearrange("p (n c) -> p n c", c=GC),
                                               b3[:, :, GC - 1:GC].broadcast_to([P, T // GC, GC]), b3,
                                               ALU.subtract), "to end", h)

            def through(kind, h):
                b = gla_block(kind, h)
                dve.wait_ge(block_done, b + 1)
                if kind in ("g0", "g1"):
                    take(g_g[:, int(kind[1]), :], b)
                elif kind in ("v0", "v1"):
                    if h:
                        dve.wait_ge(pe_step, PE["v turned", h - 1, int(kind[1])])
                    take(g_vT[:, int(kind[1]), :], b)
                elif kind == "q":
                    dve.wait_ge(act_step, AS["decays", h])
                    nc.vector.scalar_tensor_tensor(out=g_qd[:, h, :], in0=gb[b % 2], scalar=P ** -0.5,
                                                   in1=g_qd[:, h, :], op0=ALU.mult,
                                                   op1=ALU.mult).then_inc(bank_free[b % 2], 1)
                else:
                    VS.did(nc.vector.tensor_tensor(g_kd[:, h, :], gb[b % 2], g_kd[:, h, :], ALU.mult))
                    nc.vector.tensor_tensor(g_ke[:, h, :], gb[b % 2], g_ke[:, h, :],
                                            ALU.mult).then_inc(bank_free[b % 2], 1)
                    evacuated(dve, b)
                    evacuated(dve, gla_block("q", h))
                    VS.did(nc.vector.tensor_copy(g_junk2[:, :], zero[:, 0:1]), "k end", h)

            def gated(h, pair):
                dve.wait_ge(pe_step, PE["o turned", 4 * h + 2 * pair + 1])
                out = tmp2[:, 0, :].rearrange("p (e t) -> p e t", e=2)
                ts, cs = slice(256 * pair, 256 * pair + 256), slice(2 * h, 2 * h + 2)
                VS.did(nc.vector.tensor_tensor(out, banks[:, 4, :].rearrange("p (e t) -> p e t", e=2),
                                               g_g[:, :, ts], ALU.mult), "o gated", h, pair)
                last()
                VS.did(nc.vector.tensor_scalar(g_oh[:, cs, ts], out, 1.0, None, ALU.mult))
                last()
                VS.did(nc.vector.tensor_tensor(g_ol[:, cs, ts], out, g_oh[:, cs, ts].bitcast(F32), ALU.subtract),
                       "mix1 split", h, pair)

            log_gates(0)
            through("v0", 0)
            log_gates(1)
            through("q", 0)
            log_gates(2)
            through("k", 0)
            log_gates(3)
            through("v1", 0)
            for h in range(GH):
                for t in range(TT):
                    n = 4 * h + t
                    ends = GLA_THROUGH[h]

                    def end_of(place):
                        if (t, place) in ends:
                            kind = ends[t, place]
                            through(kind, h if kind[0] == "g" else h + 1)

                    dve.wait_ge(pe_step, PE["att", n])
                    VS.did(nc.vector.copy_predicated(g_att[:, n % 2, :], pc("gla_mask").bitcast(mybir.dt.uint32),
                                                     banks[:, 3, 0:P]), "att masked", n)
                    if h and t == 0:
                        gated(h - 1, 1)
                    end_of(0)
                    for k in range(2):
                        c = 2 * t + k
                        if c == 7:
                            continue
                        dve.wait_ge(pe_step, PE["u", n])
                        if c >= 2:
                            dve.wait_ge(pe_step, PE["inter", h, c - 1])
                        elif h:
                            dve.wait_ge(pe_step, PE["inter", h - 1, 7])
                        u = banks[:, 2 if k else 7, 0:256]
                        if c == 0:
                            VS.did(nc.vector.tensor_copy(g_S[:, 1, :], u), "S", h, 1)
                        else:
                            dve.wait_ge(dve_step, VS["S", h, c])
                            VS.did(nc.vector.scalar_tensor_tensor(out=g_S[:, (c + 1) % 2, :], in0=g_S[:, c % 2, :],
                                                                  scalar=g_dec[:, h, c:c + 1], in1=u, op0=ALU.mult,
                                                                  op1=ALU.add), "S", h, c + 1)
                    VS.noted[("state", n)] = VS.count
                    end_of(1)
                    if t == 2:
                        dve.wait_ge(act_step, AS["g sig", h])
                        for e in range(2):
                            VS.did(nc.vector.scalar_tensor_tensor(out=g_g[:, e, :], in0=g_g[:, e, :],
                                                                  scalar=pc("normg", e, e + 1), in1=tmp[:, e, :],
                                                                  op0=ALU.mult, op1=ALU.mult))
                        last()
                    dve.wait_ge(act_step, AS["o rstd", n])
                    if n >= 2:
                        dve.wait_ge(pe_step, PE["o turned", n - 2])
                    VS.did(nc.vector.tensor_scalar(g_on[:, n % 2, :], banks[:, 5 + n % 2, 0:256],
                                                   g_ss[:, 2 * (n % 2) + 1:2 * (n % 2) + 2], None, ALU.mult),
                           "o normed", n)
                    if t == 2:
                        gated(h, 0)
                    end_of(2)
            gated(GH - 1, 1)
            add_residual("ln1", B_GLA_OUT, ALPHA, 2)
            norm("ln1", True, True)
            mlp(B_MLP1, 0, ALPHA, "ln2", 2)
            norm("ln2", True, STOP > 1)
            if STOP > 1:
                Z = banks[:, 2:5, :].rearrange("p a b -> p (a b)")[:, 0:1280]
                R = banks[:, 5:8, :].rearrange("p a b -> p (a b)")[:, 0:1280]

                def take_scores(h):
                    dve.wait_ge(pe_step, PE["sb z", h])
                    VS.did(nc.vector.tensor_copy(t_z[:, h % 2, :], Z), "sb z", h)
                    last()
                    if h >= 2:
                        dve.wait_ge(pe_step, PE["sb o", h - 2])
                    VS.did(nc.vector.tensor_scalar(t_e[:, h % 2, :], t_z[:, h % 2, :], 40.0, None, ALU.min),
                           "sb m", h)

                def diagonal(tile, mask, op):
                    d = tile.rearrange("p (a b) -> p a b", b=256)[:, 0:5:2, 0:P]
                    VS.did(nc.vector.tensor_tensor(d, d, pc(mask).unsqueeze(1).broadcast_to([P, 3, P]), op))
                    return nc.vector.tensor_tensor(tile[:, 896:1024], tile[:, 896:1024], pc(mask), op)

                def softplus(h):
                    sp = t_sp[:, h % 2, :]
                    dve.wait_ge(act_step, AS["sb l", h])
                    if h >= 2:
                        dve.wait_ge(act_step, AS["sb w", h - 2])
                    VS.did(nc.vector.tensor_tensor(sp, t_z[:, h % 2, :], t_e[:, h % 2, :], ALU.max))
                    last()
                    VS.did(diagonal(sp, "strict", ALU.mult), "sb masked", h)

                def split_softplus(h):
                    sp = t_sp[:, h % 2, :]
                    dve.wait_ge(dve_step, VS["sb masked", h])
                    if h:
                        dve.wait_ge(pe_step, PE["sb R", h - 1])
                    VS.did(nc.vector.tensor_scalar(t_sh[:, :], sp, 1.0, None, ALU.mult))
                    last()
                    VS.did(nc.vector.tensor_tensor(t_sl[:, :], sp, t_sh[:, :].bitcast(F32), ALU.subtract),
                           "sb sp", h)

                take_scores(0)
                dve.wait_ge(act_step, AS["ones split"])
                softplus(0)
                split_softplus(0)
                for h in range(SH):
                    if h + 1 < SH:
                        take_scores(h + 1)
                        softplus(h + 1)
                    sp = t_sp[:, h % 2, :]
                    dve.wait_ge(pe_step, PE["sb R", h])
                    VS.did(nc.vector.tensor_tensor(sp, t_z[:, h % 2, :], R, ALU.subtract))
                    last()
                    VS.did(diagonal(sp, "neg_sb", ALU.add), "sb lw", h)
                    if h + 1 < SH:
                        split_softplus(h + 1)
                    if h % 2 == 0 and h:
                        split_pair(h // 2 - 1)
                split_pair(C - 1)
                add_residual("ln3", B_SB_OUT, ALPHA, 2)
                norm("ln3", True, True)
                mlp(B_MLP2, 32, ALPHA, "ln4", 2)
                norm("ln4", True, False)
            if STOP > 2:
                for c in range(C):
                    dve.wait_ge(act_step, AS["ln4", "out", c])
                    add_sums("rms1", c, 1)
                norm("rms1", False, True)
                mixer_dve(dve)
                add_residual("rms2", B_MIX_OUT, 1.0, 1)
                norm("rms2", False, True)
                mlp(B_MLP3, 64, 1.0, "last", 0)
            for c in range(C if STOP > 2 else 0):
                VS.did(nc.vector.tensor_copy(tmp2[0:1, 0, c:c + 1], res[0:1, c, 0:1]), "out", c)
            if STOP == 1:
                for c in range(C):
                    dve.wait_ge(act_step, AS["ln2", "out", c])
                    VS.did(nc.vector.tensor_copy(tmp2[0:1, 0, c:c + 1], res[0:1, c, 0:1]), "out", c)
            if STOP == 2:
                for c in range(C):
                    dve.wait_ge(act_step, AS["ln4", "out", c])
                    VS.did(nc.vector.tensor_copy(tmp2[0:1, 0, c:c + 1], res[0:1, c, 0:1]), "out", c)


def blocks(w):
    w = np.asarray(w)
    n = w.shape[1] // P
    return w.reshape(C, P, n, P).transpose(2, 1, 0, 3).reshape(n, P, D)


def placed(w, at):
    w = np.asarray(w)
    out = np.zeros((D, P), w.dtype)
    out[:, at] = w
    return blocks(out)


def mlp_stream(up, down):
    up, down = blocks(up), [blocks(np.asarray(down)[q * D:q * D + D]) for q in range(FFQ)]
    parts = [up[0:C]]
    for q in range(1, FFQ):
        parts += [up[q * C:q * C + C], down[q - 1]]
    return np.concatenate(parts + [down[FFQ - 1]])


def chunked(v, rows=P):
    return np.asarray(v).reshape(-1, rows).T


def _dram(**inp):
    g = np.asarray(inp["gla_w_in"])[0]
    heads = {gla_block(kind, h): at * C // 2 + (2 if len(kind) == 2 else 1) * h + (kind[-1] == "1")
             for kind, at in (("q", 0), ("k", 1), ("v0", 2), ("v1", 2), ("g0", 4), ("g1", 4)) for h in range(GH)}
    stream = [placed(g[:, 3072:3088], np.arange(16)),
              blocks(g[:, 0:3072])[[heads[b] for b in range(B_GLA + 1, B_GLA_OUT)]], blocks(inp["gla_w_o"][0]),
              mlp_stream(inp["mlp_w_up"][0], inp["mlp_w_down"][0]),
              np.concatenate([blocks(inp["sb_w_q"][0]), blocks(inp["kv_w"])]).reshape(3, C, P, D).transpose(
                  1, 0, 2, 3).reshape(3 * C, P, D), blocks(inp["sb_w_o"][0]),
              mlp_stream(inp["mlp_w_up"][1], inp["mlp_w_down"][1])]
    m = np.asarray(inp["w_in_2"])[0]
    gates = 1536 + np.array([4, 5, 6, 7, 12, 13, 14, 15, 0, 1, 2, 3, 8, 9, 10, 11])
    at = np.concatenate([32 * k + np.arange(4) for k in range(4)])
    stream += [blocks(m[:, 0:512]), placed(m[:, gates], at), blocks(m[:, 1024:1536]), blocks(m[:, 512:1024]),
               blocks(m[:, 1552:1936]), placed(m[:, 1936:2000], np.arange(64)),
               blocks(inp["w_out_2"][0]), mlp_stream(inp["w_ff1_2"][0], inp["w_ff2_2"][0])]
    W = np.ascontiguousarray(np.concatenate(stream))
    par = np.zeros((P, NPAR), np.float32)

    def put(name, a, row=0):
        o, w = _cols[name]
        a = np.asarray(a)
        par[row:row + a.shape[0], o:o + a.shape[1]] = a

    put("ba", chunked(inp["gla_b_a"][0]))
    put("normg", chunked(inp["gla_norm_g"][0]))
    lg, lb = np.asarray(inp["ln_g"]), np.asarray(inp["ln_b"])
    put("ln", np.concatenate([chunked(a[l, k]) for l in range(2) for k in range(2) for a in (lg, lb)], axis=1))
    put("gmix", chunked(inp["g_mix_norm_2"][0]))
    put("gffn", chunked(inp["g_ffn_norm_2"][0]))
    put("gout", chunked(inp["g_mlstm_out_2"][0]))
    put("gcq", chunked(inp["g_cq_2"][0]))
    put("gckv", chunked(inp["g_ckv_2"][0]))
    for n, v in (("q", inp["g_q_2"][0]), ("k", inp["g_k_2"][0])):
        put(f"g{n}n", np.asarray(v)[0:128, None])
        put(f"g{n}r", np.asarray(v)[128:192, None])
    put("convw", np.asarray(inp["conv_w_2"][0]).reshape(5, 4, P).transpose(2, 1, 0).reshape(P, 20))
    put("convb", chunked(inp["conv_b_2"][0]))
    bg = np.asarray(inp["b_gates_2"][0]).reshape(4, 4)
    for n, k in (("bf", 1), ("bi", 0)):
        put(n, bg[k][:, None])
        put(n, bg[k + 2][:, None], 32)
    inv = (np.float32(10000.0) ** (-np.arange(0, 64, 2, dtype=np.float32) / np.float32(64))).astype(np.float32)
    put("freq", np.concatenate([inv, inv])[:, None])
    i = np.arange(P)
    s, t = i[:, None], i[None, :]
    put("ident", np.eye(P))
    put("strict", s < t)
    put("gla_mask", (s <= t) & (s // GC == t // GC))
    put("tri", s >= t)
    put("ones", np.full((P, P), 1.0 / D))
    put("one", np.ones((P, P)))
    put("ln_eps", np.full((P, 1), LN_EPS))
    put("rms_eps", np.full((P, 1), RMS_EPS))
    put("half_pi", np.full((P, 1), np.pi / 2))
    put("neg_fw", np.where(s > t, -NEG, 0.0))
    put("neg_bw", np.where(s < t, -NEG, 0.0))
    put("neg_sb", np.where(s >= t, NEG, 0.0))
    put("reset", np.broadcast_to((np.arange(T) % GC != 0), (P, T)))
    sel = np.zeros((64, 8, P))
    for d in range(2):
        for h in range(4):
            sel[32 * d + h, 4 * d + h] = 1
    put("sel", sel.reshape(64, 8 * P))
    swap = np.zeros((64, 64))
    swap[np.arange(32) + 32, np.arange(32)] = -1
    swap[np.arange(32), np.arange(32) + 32] = 1
    put("swap", swap)
    put("wa2", inp["gla_w_a2"][0])
    put("wuq", np.asarray(inp["w_uq_2"][0]).reshape(2, P, 768).transpose(1, 0, 2).reshape(P, 1536))
    put("wukv", inp["w_ukv_2"][0])
    x = np.ascontiguousarray(np.asarray(inp["x"])[0].T.reshape(C, P, T))
    pos = np.ascontiguousarray(np.broadcast_to(np.asarray(inp["positions_2"]).astype(np.int32), (64, T)))
    return W, x, par, pos


STOP_AT = 99


def kernel(**inputs):
    import concourse.bacc as bacc
    from concourse.bass_utils import run_bass_kernel_spmd

    W, x, par, pos = _dram(**inputs)
    counts = [{}, {}, {}]
    FINAL.clear()
    for second in range(2):
        if second:
            FINAL.append(True)
        nc = bacc.Bacc("TRN2", target_bir_lowering=False, num_devices=1)
        aps = [nc.dram_tensor(n, a.shape, mybir.dt.from_np(a.dtype), kind="ExternalInput").ap()
               for n, a in (("w_stream", W), ("x_t", x), ("params", par), ("pos", pos))]
        y = nc.dram_tensor("y_t", (C, P, T), F32, kind="ExternalOutput").ap()
        build(nc, counts, *aps, y, STOP=STOP_AT)
    r = run_bass_kernel_spmd(nc, [{"w_stream": W, "x_t": x, "params": par, "pos": pos}], core_ids=[0])
    return np.ascontiguousarray(r.results[0]["y_t"].reshape(D, T).T)[None]
```

```python
from contextlib import ExitStack

import numpy as np
import concourse.bass as bass
from concourse import mybir

F32 = mybir.dt.float32
F32R = mybir.dt.float32r
ALU = mybir.AluOpType
ACT = mybir.ActivationFunctionType
AX = mybir.AxisListType

P = 128
D = 1024
T = 512
C = D // P
TT = T // P
FFQ = 4
ALPHA = 4.0 ** 0.25
LN_EPS, RMS_EPS = 1e-5, 1e-6
GH = 4
GC = 64
SH = 16
MH = 4
AH = 4
RAW = 2
SLOTS = 4
TWO_PI = 2 * np.pi
NEG = -1.0e30
ROUND = 12582912.0
_rest = TWO_PI - 6.28125
_mid = float(np.float16(_rest))
TWO_PI_PARTS = (6.28125, _mid, float(np.float32(_rest - _mid)))

MLP_BLOCKS = 2 * FFQ * C
B_GLA = 0
B_GLA_OUT = B_GLA + 25
B_MLP1 = B_GLA_OUT + C
B_SB = B_MLP1 + MLP_BLOCKS
B_SB_OUT = B_SB + 3 * C
B_MLP2 = B_SB_OUT + C
B_MIX = B_MLP2 + MLP_BLOCKS
B_MIX_OUT = B_MIX + 17
B_MLP3 = B_MIX_OUT + C
NB = B_MLP3 + MLP_BLOCKS

_cols = {}
_n = 0
for _name, _w in (("ba", 4), ("normg", 2), ("ln", 2 * 2 * 2 * C), ("gmix", C), ("gffn", C), ("gout", MH),
                  ("gcq", 2), ("gckv", 1), ("gqn", 1), ("gqr", 1), ("gkn", 1), ("gkr", 1), ("convw", 20),
                  ("convb", 4), ("bf", 1), ("bi", 1), ("freq", 1), ("ident", P), ("strict", P), ("gla_mask", P),
                  ("tri", P), ("ones", P), ("one", P), ("ln_eps", 1), ("rms_eps", 1), ("half_pi", 1), ("neg_fw", P), ("neg_sb", P), ("neg_bw", P), ("reset", T), ("wa2", T),
                  ("mixer's", 0), ("sel", 8 * P), ("swap", 64), ("wuq", 2 * 768), ("wukv", 1024)):
    _cols[_name] = (_n, _w)
    _n += _w
NPAR = _n
NPAR1 = _cols["mixer's"][0]
TRI = [0, 512, 1024, 896]


def gla_block(kind, h):
    if kind in ("g0", "g1"):
        return B_GLA + 5 + 6 * h + (kind == "g1")
    if h == 0:
        return B_GLA + 1 + ("v0", "q", "k", "v1").index(kind)
    return B_GLA + 1 + 6 * h + ("q", "k", "v0", "v1").index(kind)


GLA_HALVES = [{(i // 3, i % 3): i for i in range(12)}] * (GH - 1) + [{(0, 0): 0, (0, 1): 1, (1, 0): 2, (1, 1): 3}]
GLA_THROUGH = [{(0, 1): "g0", (1, 0): "g1", (1, 2): "q", (2, 1): "k", (3, 0): "v0", (3, 2): "v1"}] * (GH - 1) + [
    {(0, 1): "g0", (1, 1): "g1"}]


class Steps:

    def __init__(self, semaphore, noted):
        self.semaphore, self.noted, self.count, self.seen = semaphore, noted, 0, set()

    def did(self, instruction, *name):
        instruction.then_inc(self.semaphore, 1)
        self.count += 1
        if name:
            assert name not in self.seen, name
            self.seen.add(name)
            self.noted[name] = self.count

    def __getitem__(self, name):
        name = name if isinstance(name, tuple) else (name,)
        if name not in self.noted and FINAL:
            raise KeyError(name)
        return self.noted.get(name, 1)


FINAL = []


def build(nc, counts, W, X, PAR, POS, Y):
    with ExitStack() as ctx:
        scopes = [ctx]

        def sb(name, shape, dt=F32):
            return scopes[-1].enter_context(nc.sbuf_tensor(name, shape, dt))

        def sem(name):
            return ctx.enter_context(nc.semaphore(name))

        raw = sb("raw", [P, RAW, D])
        whi = [sb(f"whi{k}", [P, D], F32R) for k in range(SLOTS)]
        wlo = [sb(f"wlo{k}", [P, D], F32R) for k in range(SLOTS)]
        zero = sb("zero", [P, T])
        par = sb("par", [P, NPAR1])
        res = sb("res", [P, C, T])
        xh = sb("xh", [P, C, T], F32R)
        xl = sb("xl", [P, C, T], F32R)
        s1 = sb("s1", [P, T])
        s2 = sb("s2", [P, T])
        sq = sb("sq", [P, 2, T])
        mean = sb("mean", [P, T])
        rstd = sb("rstd", [P, T])
        tmp = sb("tmp", [P, 2, T])
        tmp2 = sb("tmp2", [P, 2, T])
        relu = sb("relu", [P, 2, T])

        with ExitStack() as mlp_scope:
            scopes.append(mlp_scope)
            hh = [sb(f"hh{k}", [P, C, T], F32R) for k in range(2)]
            hl = [sb(f"hl{k}", [P, C, T], F32R) for k in range(2)]
            scopes.pop()
        with ExitStack() as gla_scope:
            scopes.append(gla_scope)
            g_qd, g_kd, g_ke = (sb(f"g_{n}", [P, GH, T]) for n in ("qd", "kd", "ke"))
            g_vT = sb("g_vT", [P, 2, T])
            g_v = sb("g_v", [P, 2, TT, 256])
            g_g = sb("g_g", [P, 2, T])
            g_a1 = sb("g_a1", [16, T])
            g_dec = sb("g_dec", [P, GH, T // GC])
            g_att = sb("g_att", [P, 2, P])
            g_ket = sb("g_ket", [P, 2, P])
            g_S = sb("g_S", [P, 2, 256])
            g_on = sb("g_on", [P, 2, 256])
            g_junk = sb("g_junk", [P, 256])
            g_ss = sb("g_ss", [P, 4])
            g_junk2 = sb("g_junk2", [P, 1])
            g_oh, g_ol = (sb(f"g_{n}", [P, C, T], F32R) for n in ("oh", "ol"))
            scopes.pop()
        with ExitStack() as sb_scope:
            scopes.append(sb_scope)
            t_q, t_v = (sb(f"t_{n}", [P, 2, T]) for n in ("q", "v"))
            t_k, t_vT = relu, tmp
            t_z, t_e, t_sp = (sb(f"t_{n}", [P, 2, 1280]) for n in ("z", "e", "sp"))
            t_sh, t_sl = (sb(f"t_{n}", [P, 1280], F32R) for n in ("sh", "sl"))
            t_oh, t_ol = (sb(f"t_{n}", [P, C, T], F32R) for n in ("oh", "ol"))
            t_one = sb("t_one", [P, 2, P], F32R)
            scopes.pop()
        with ExitStack() as mix_scope:
            scopes.append(mix_scope)
            par2 = sb("par2", [P, NPAR - NPAR1])
            m_o = sb("m_o", [P, 4, T])
            m_cq = sb("m_cq", [P, 2, T])
            m_ckv = sb("m_ckv", [P, T])
            m_kpe = sb("m_kpe", [64, T])
            m_dn = sb("m_dn", [P, 4])
            m_ss = sb("m_ss", [P, 4])
            a_cos = sb("a_cos", [64, T])
            a_sin = sb("a_sin", [64, T])
            a_posi = s1[0:64, :].bitcast(mybir.dt.int32)
            a_ang = relu[0:64, :, :]
            with ExitStack() as mlstm_scope:
                scopes.append(mlstm_scope)
                m_raw = sb("m_raw", [P, 4, T])
                m_qk = sb("m_qk", [P, 4, T])
                m_vT = sb("m_vT", [P, 4, T])
                m_v = sb("m_v", [P, TT, MH, 130])
                m_I, m_F = s2[0:64, :], s1[0:64, :]
                m_B = tmp2[0:64, 1, :]
                m_u, m_M = relu[0:64, 0, :], relu[0:64, 1, :]
                m_Gc = sb("m_Gc", [P, TT, 64])
                m_Ec = sb("m_Ec", [P, TT, 64])
                m_Md = tmp[:, 1, :]
                m_Mb = sq[:, 1, :]
                m_E = [sb("m_E", [P, 1280])[:, :], m_vT[:, :, :].rearrange("p c t -> p (c t)")[:, 0:1280]]
                m_P = [sb(f"m_P{k}", [P, 1280]) for k in range(2)]
                m_h0, m_h1, m_hn0, m_hn1 = (m_raw[:, k, :].rearrange("p (t n) -> p t n", n=P) for k in range(4))
                m_h, m_hn = (m_h0, m_h1), (m_hn0, m_hn1)
                scopes.pop()
            with ExitStack() as mla_scope:
                scopes.append(mla_scope)
                a_n = [[sb(f"a_n{k}{d}", [P, T]) for d in range(2)] for k in range(2)]
                a_r = [[sb(f"a_r{k}{d}", [64, T]) for d in range(2)] for k in range(2)]
                a_pre = [sb(f"a_pre{k}", [64, T]) for k in range(2)]
                a_swap = sb("a_swap", [64, T])
                a_v = sb("a_v", [P, TT, T])
                a_p = sb("a_p", [P, 2, T])
                a_pT = sb("a_pT", [P, TT, T])
                scopes.pop()
            scopes.pop()

        banks = ctx.enter_context(nc.psum_tensor("banks", [P, 8, 512], F32))
        gb = [banks[:, k, :] for k in range(2)]
        GATE_BANKS = (2, 5, 6, 7)
        OUT_STEP = (4, 5, 7)
        OUT_AT = {j: h for h, j in enumerate(OUT_STEP)}

        def pc(name, a=0, b=None, rows=P):
            o, w = _cols[name]
            tile, o = (par, o) if o < NPAR1 else (par2, o - NPAR1)
            return tile[0:rows, o + a:o + (w if b is None else b)]

        loaded = [sem(f"loaded{r}") for r in range(RAW)]
        par_in = sem("par_in")
        par2_in = sem("par2_in")
        pos_in = sem("pos_in")
        x_in = [sem(f"x_in{c}") for c in range(C)]
        out_sem = sem("out_sem")
        zero_set = sem("zero_set")
        w_hi_done = sem("w_hi_done")
        w_ready = sem("w_ready")
        block_done = sem("block_done")
        bank_free = [sem(f"bank_free{k}") for k in range(2)]
        relu_done = sem("relu_done")
        up_squared = sem("up_squared")
        hidden_ready = sem("hidden_ready")
        pe_step = sem("pe_step")
        act_step = sem("act_step")
        dve_step = sem("dve_step")
        pool_step = sem("pool_step")


        PE = Steps(pe_step, counts[0])
        AS = Steps(act_step, counts[1])
        VS = Steps(dve_step, counts[2])
        GS = Steps(pool_step, counts[3])

        block = ctx.enter_context(nc.Block())

        def evacuated(eng, b):
            eng.wait_ge(bank_free[b % 2], b // 2 + 1)

        def low_ready(name, center):
            return [(pool_step, GS[name, "split", c]) if center or c % 2 else (dve_step, VS[name, "split", c])
                    for c in range(C)]

        def sq_added(name, c):
            return (pool_step, GS[name, "sq added", c]) if name == "rms1" else (dve_step, VS[name, "sq added", c])

        @block.sync
        def _(sp):
            sp.dma_start(raw[:, 0, :], W[0]).then_inc(loaded[0], 16)
            for c in range(C):
                sp.dma_start(res[:, c, :], X[c]).then_inc(x_in[c], 16)
                if c == C // 2:
                    sp.dma_start(raw[:, 1, :], W[1]).then_inc(loaded[1], 16)
            sp.dma_start(par[:, :], PAR[:, 0:NPAR1]).then_inc(par_in, 16)
            with sp.Fori(RAW, NB - RAW + 1, RAW) as i:
                for r in range(RAW):
                    sp.wait_ge(w_ready, i + (r - RAW + 1))
                    sp.dma_start(raw[:, r, :], W[i + r]).then_inc(loaded[r], 16)
            for c in range(C):
                evacuated(sp, B_MLP3 + 7 * C + c)
                sp.dma_start(Y[c], res[:, c, :]).then_inc(out_sem, 16)
            sp.wait_ge(out_sem, 16 * C)

        @block.gpsimd
        def _(pool):
            nc.gpsimd.memset(zero[:, :], 0.0).then_inc(zero_set, 1)
            pool.wait_ge(zero_set, 1)

            def split(b, at):
                r, k = at % RAW, at % SLOTS
                pool.wait_ge(loaded[r], (b // RAW + 1) * 16 if isinstance(b, int) else (b - r) * (16 // RAW) + 16)
                if at >= SLOTS:
                    pool.wait_ge(block_done, b - SLOTS + 1)
                nc.gpsimd.tensor_tensor(
                    whi[k][:, :].rearrange("p (a b) -> p a b", b=T), raw[:, r, :].rearrange("p (a b) -> p a b", b=T),
                    zero[:, :].unsqueeze(1).broadcast_to([P, D // T, T]), ALU.add).then_inc(w_hi_done, 1)
                pool.wait_ge(w_hi_done, b + 1)
                nc.gpsimd.tensor_tensor(wlo[k][:, :], raw[:, r, :], whi[k][:, :].bitcast(F32),
                                        ALU.subtract).then_inc(w_ready, 1)

            def split_blocks(b, end):
                while b < end:
                    whole = (end - b) // SLOTS * SLOTS
                    if b < SLOTS or b % SLOTS or not whole:
                        split(b, b)
                        b += 1
                        continue
                    with pool.Fori(b, b + whole - SLOTS + 1, SLOTS) as i:
                        for r in range(SLOTS):
                            split(i + r, SLOTS + r)
                    b += whole

            def low_parts(name, center):
                for c in range(0 if center else 1, C, 1 if center else 2):
                    pool.wait_ge(act_step, AS[name, "hi", c])
                    GS.did(nc.gpsimd.tensor_tensor(xl[:, c, :], res[:, c, :] if center else tmp2[:, c % 2, :],
                                                   xh[:, c, :].bitcast(F32), ALU.subtract), name, "split", c)

            split_blocks(0, B_MLP1 + SLOTS)
            low_parts("ln1", True)
            split_blocks(B_MLP1 + SLOTS, B_SB + SLOTS)
            low_parts("ln2", True)
            split_blocks(B_SB + SLOTS, B_MLP2 + SLOTS)
            low_parts("ln3", True)
            split_blocks(B_MLP2 + SLOTS, B_MIX + SLOTS)
            for c in range(C - 1):
                pool.wait_ge(act_step, AS["rms1", "sq", c])
                if c:
                    pool.wait_ge(pool_step, GS["rms1", "sq added", c - 1])
                GS.did(nc.gpsimd.tensor_tensor(s2[:, :], sq[:, c % 2, :], s2[:, :] if c else zero[:, :], ALU.add),
                       "rms1", "sq added", c)
            low_parts("rms1", False)
            split_blocks(B_MIX + SLOTS, B_MLP3 + SLOTS)
            low_parts("rms2", False)
            split_blocks(B_MLP3 + SLOTS, NB)

        @block.tensor
        def _(pe):
            def product(b, at, free, hi, lo, chunk_ready=None, out=None, chunks=range(C)):
                k, slot = at % 2, at % SLOTS
                out = gb[k] if out is None else out
                if chunks[0] == 0:
                    pe.wait_ge(w_ready, b + 1)
                    if free is not None:
                        pe.wait_ge(bank_free[k], free)
                for c in chunks:
                    if chunk_ready:
                        pe.wait_ge(*chunk_ready[c])
                    w = slice(c * P, c * P + P)
                    pe.matmul(out, whi[slot][:, w], hi[:, c, :], start=(c == 0), stop=False)
                    pe.matmul(out, wlo[slot][:, w], hi[:, c, :], start=False, stop=False)
                    m = pe.matmul(out, whi[slot][:, w], lo[:, c, :], start=False, stop=(c == C - 1))
                if chunks[-1] == C - 1:
                    m.then_inc(block_done, 1)

            def first_pair(name, center, b, outs=None):
                outs = outs or [gb[b % 2], gb[(b + 1) % 2]]
                low = low_ready(name, center)
                pe.wait_ge(w_ready, b + 2)
                evacuated(pe, b - 2)
                evacuated(pe, b - 1)
                for c in range(C + 1):
                    if c < C:
                        pe.wait_ge(act_step, AS[name, "hi", c])
                        w = slice(c * P, c * P + P)
                        for j in range(2):
                            k = (b + j) % SLOTS
                            pe.matmul(outs[j], whi[k][:, w], xh[:, c, :], start=(c == 0), stop=False,
                                      skip_group_check=True)
                            pe.matmul(outs[j], wlo[k][:, w], xh[:, c, :], start=False, stop=False,
                                      skip_group_check=True)
                    if c:
                        pe.wait_ge(*low[c - 1])
                        w = slice((c - 1) * P, c * P)
                        for j in range(2):
                            m = pe.matmul(outs[j], whi[(b + j) % SLOTS][:, w], xl[:, c - 1, :], start=False,
                                          stop=(c == C), skip_group_check=True)
                            if c == C:
                                m.then_inc(block_done, 1)

            def products(b, n, hi=xh, lo=xl, chunk_ready=None):
                end = b + n
                while b < end:
                    whole = (end - b) // SLOTS
                    if b % SLOTS or not whole:
                        product(b, b, b // 2, hi, lo, chunk_ready)
                        b += 1
                        continue
                    with pe.Fori(0, whole) as i:
                        for j in range(SLOTS):
                            product(i * SLOTS + (b + j), b + j, i * (SLOTS // 2) + (b + j) // 2, hi, lo, chunk_ready)
                    b += whole * SLOTS

            def mlp(b0, u0, name, center):
                first_pair(name, center, b0)
                for q in range(FFQ):
                    products(b0 + (0 if q else 2), C if q else C - 2)
                    b0 += C
                    if q:
                        pe.wait_ge(hidden_ready, u0 + C * q)
                        products(b0, C, hh[(q - 1) % 2], hl[(q - 1) % 2])
                        b0 += C
                pe.wait_ge(hidden_ready, u0 + C * FFQ)
                products(b0, C, hh[(FFQ - 1) % 2], hl[(FFQ - 1) % 2])

            def norm_sums(name, center, b=None):
                sums = ((0, s1, 2), (1, s2, 3)) if center else ((1, s2, 2),)
                for k, part, bank in sums:
                    if k:
                        pe.wait_ge(*sq_added(name, C - 2))
                    else:
                        pe.wait_ge(dve_step, VS[name, "added", C - 2])
                    pe.matmul(banks[:, bank, :], pc("ones"), part[:, :], start=True, stop=False,
                              skip_group_check=True)
                for k, part, bank in sums:
                    if k:
                        pe.wait_ge(act_step, AS[name, "sq", C - 1])
                    else:
                        evacuated(pe, b)
                    PE.did(pe.matmul(banks[:, bank, :], pc("ones"), sq[:, 1, :] if k else res[:, C - 1, :],
                                     start=False, stop=True, skip_group_check=True), name, "sum", k)

            def program(pe):
                product(B_GLA, 0, None, xh, xl, [(dve_step, VS["x split", c]) for c in range(C)])
                product(B_GLA + 1, B_GLA + 1, None, xh, xl)
                evacuated(pe, B_GLA)
                pe.wait_ge(par_in, 16)
                for h in range(GH):
                    PE.did(pe.matmul(banks[:, GATE_BANKS[h], :], pc("wa2", h * P, h * P + P, rows=16), g_a1[:, :],
                                     start=True, stop=True), "gate", h)

                def plain(b):
                    product(b, b, b // 2, xh, xl)

                def half(h, t, place):
                    i = GLA_HALVES[h].get((t, place))
                    if i is not None:
                        b = gla_block("g0", h) + i // 2
                        product(b, b, b // 2, xh, xl, chunks=range(C // 2) if i % 2 == 0 else range(C // 2, C))

                def turn_v(h, e):
                    evacuated(pe, gla_block(f"v{e}", h))
                    if e:
                        pe.wait_ge(act_step, AS["v turned", h, 0])
                    elif h == 0:
                        pe.wait_ge(act_step, AS["z", 0])
                    for t in range(TT):
                        m = pe.transpose(banks[:, 2, t * P:t * P + P], g_vT[:, e, t * P:t * P + P], pc("ident"))
                    PE.did(m, "v turned", h, e)

                def turn_o(n):
                    h, t = divmod(n, TT)
                    pe.wait_ge(dve_step, VS["o normed", n])
                    if n >= 2 and n % 2 == 0:
                        pe.wait_ge(dve_step, VS["o gated", (n - 2) // TT, (n - 2) % TT // 2])
                    for e in range(2):
                        m = pe.transpose(banks[:, 4, e * 256 + (t % 2) * P:e * 256 + (t % 2) * P + P],
                                         g_on[:, n % 2, e * P:e * P + P], pc("ident"))
                    PE.did(m, "o turned", n)

                plain(B_GLA + 2)
                plain(B_GLA + 3)
                turn_v(0, 0)
                plain(B_GLA + 4)
                for h in range(GH):
                    for t in range(TT):
                        n = 4 * h + t
                        ts = slice(t * P, t * P + P)
                        if t == 0:
                            pe.wait_ge(dve_step, VS["k end", h])
                        if n:
                            pe.wait_ge(dve_step, VS["att masked", n - 1])
                        PE.did(pe.matmul(banks[:, 3, 0:P], g_kd[:, h, ts], g_qd[:, h, ts], start=True, stop=True),
                               "att", n)
                        if n:
                            pe.wait_ge(dve_step, VS["state", n - 1])
                        else:
                            pe.wait_ge(act_step, AS["z", GH - 1])
                        PE.did(pe.transpose(banks[:, 7, 256:256 + P], g_ke[:, h, ts], pc("ident")), "k turned", n)
                        if t == 0:
                            turn_v(h, 1)
                            if h:
                                turn_o(n - 1)
                        half(h, t, 0)
                        pe.wait_ge(act_step, AS["k turned", n])
                        if t == 0:
                            pe.wait_ge(act_step, AS["v turned", h, 1])
                        vs = g_v[:, h % 2, t, :]
                        m = pe.matmul(banks[:, 7, 0:256], g_ket[0:64, n % 2, :], vs[0:64], start=True, stop=True)
                        if t < 3:
                            m = pe.matmul(banks[:, 2, 0:256], g_ket[64:P, n % 2, :], vs[64:P], start=True, stop=True)
                        PE.did(m, "u", n)
                        pe.wait_ge(dve_step, VS["att masked", n])
                        if n >= 2:
                            pe.wait_ge(dve_step, VS["o normed", n - 2])
                        o = banks[:, 5 + n % 2, 0:256]
                        PE.did(pe.matmul(o, g_att[:, n % 2, :], vs, start=True, stop=True, skip_group_check=True))
                        for k in range(2):
                            if k:
                                half(h, t, 1)
                            c = 2 * t + k
                            if c:
                                pe.wait_ge(dve_step, VS["S", h, c])
                                r = slice(64 * k, 64 * k + 64)
                                PE.did(pe.matmul(o[r], g_qd[:, h, t * P + 64 * k:t * P + 64 * k + 64],
                                                 g_S[:, c % 2, :], start=False, stop=True, skip_group_check=True),
                                       "inter", h, c)
                        if t:
                            turn_o(n - 1)
                        if t == 3 and h + 1 < GH:
                            turn_v(h + 1, 0)
                        half(h, t, 2)
                turn_o(TT * GH - 1)
                products(B_GLA_OUT, C, g_oh, g_ol, [(dve_step, VS["mix1 split", c // 2, 1]) for c in range(C)])
                norm_sums("ln1", True, B_MLP1 - 1)
                mlp(B_MLP1, 0, "ln1", True)
                norm_sums("ln2", True, B_SB - 1)
                Z = banks[:, 2:5, :].rearrange("p a b -> p (a b)")
                R = banks[:, 5:8, :].rearrange("p a b -> p (a b)")

                def project(c, part):
                    b = B_SB + 3 * c + part
                    evacuated(pe, b - 1)
                    if part == 0 and c:
                        pe.wait_ge(act_step, AS["sv turned", c - 1])
                    product(b, b, None, xh, xl, out=gb[0])

                def turn_v(c):
                    evacuated(pe, B_SB + 3 * c + 2)
                    for t in range(TT):
                        m = pe.transpose(gb[0][:, t * P:t * P + P], t_vT[:, c % 2, t * P:t * P + P], pc("ident"))
                    PE.did(m, "sv turned", c)

                def scores(h):
                    r, c = slice(64 * (h % 2), 64 * (h % 2) + 64), h // 2
                    evacuated(pe, B_SB + 3 * c)
                    evacuated(pe, B_SB + 3 * c + 1)
                    if h:
                        pe.wait_ge(dve_step, VS["sb z", h - 1])
                    for i in range(TT):
                        m = pe.matmul(Z[:, TRI[i]:TRI[i] + T - i * P], t_k[r, c % 2, i * P:i * P + P],
                                      t_q[r, c % 2, i * P:T], start=True, stop=True, skip_group_check=True)
                    PE.did(m, "sb z", h)

                def sums(h):
                    pe.wait_ge(dve_step, VS["sb sp", h])
                    for i in range(TT):
                        for j in range(i, TT):
                            for part, tile in enumerate((t_sh, t_sl)):
                                m = pe.matmul(R[:, TRI[i] + (j - i) * P:TRI[i] + T - i * P],
                                              t_one[:, 1 if j == i else 0, :],
                                              tile[:, TRI[j]:TRI[j] + T - j * P],
                                              start=(j == i and part == 0), stop=(j == TT - 1 and part == 1),
                                              skip_group_check=True)
                    PE.did(m, "sb R", h)

                def outputs(h):
                    r0, c = 64 * (h % 2), h // 2
                    pe.wait_ge(act_step, AS["sb w", h])
                    if h >= 2:
                        pe.wait_ge(dve_step, VS["sb split", c - 1])
                    for i in range(TT):
                        m = pe.matmul(gb[1][r0:r0 + 64, i * P:T], t_v[:, c % 2, i * P + r0:i * P + r0 + 64],
                                      t_e[:, h % 2, TRI[i]:TRI[i] + T - i * P], start=(i == 0), stop=(i == 3),
                                      skip_group_check=True)
                    PE.did(m, "sb o", h)

                first_pair("ln2", True, B_SB, gb)
                project(0, 2)
                turn_v(0)
                scores(0)
                for h in range(SH):
                    c = h // 2 + 1
                    if h + 1 < SH:
                        scores(h + 1)
                    if h:
                        outputs(h - 1)
                    if c < C:
                        project(c, 2 if h % 2 else 0)
                    sums(h)
                    if c < C:
                        if h % 2:
                            turn_v(c)
                        else:
                            project(c, 1)
                outputs(SH - 1)
                pe.wait_ge(dve_step, VS["sb split", C - 1])
                products(B_SB_OUT, C, t_oh, t_ol)
                norm_sums("ln3", True, B_MLP2 - 1)
                mlp(B_MLP2, 32, "ln3", True)
                norm_sums("ln4", True, B_MIX - 1)
                norm_sums("rms1", False)
                first_pair("rms1", False, B_MIX)
                products(B_MIX + 2, 7)
                mixer_pe(pe)
                pe.wait_ge(dve_step, VS["la out", AH - 1])
                products(B_MIX_OUT, C, chunk_ready=[(dve_step, VS["mix split", c]) for c in range(C)])
                norm_sums("rms2", False)
                mlp(B_MLP3, 64, "rms2", False)

            def mixer_pe(pe):
                pe.wait_ge(par2_in, 16)
                for b in range(B_MIX + 5, B_MIX + 9):
                    evacuated(pe, b)
                for t in range(TT):
                    if t >= 2:
                        pe.wait_ge(act_step, AS["mv turned", t - 2])
                    for h in range(MH):
                        m = pe.transpose(banks[:, 2 + t % 2, h * P:h * P + P], m_vT[:, h, t * P:t * P + P], pc("ident"))
                    PE.did(m, "mv turned", t)
                pe.wait_ge(act_step, AS["mv turned", 3])
                for k, (name, tile) in enumerate((("ml G", m_I), ("ml e", m_u))):
                    pe.wait_ge(*((dve_step, VS["ml G"]) if k == 0 else (act_step, AS["ml e"])))
                    for t in range(TT):
                        m = pe.transpose(banks[:, 2 + k, t * 64:t * 64 + 64], tile[:, t * P:t * P + P],
                                         pc("ident", 0, 64, rows=64))
                    PE.did(m, name)
                Z = banks[:, 2:5, :].rearrange("p a b -> p (a b)")
                STEPS = 2 * MH

                def scores(j):
                    h, d = divmod(j, 2)
                    r = slice(64 * (h % 2), 64 * (h % 2) + 64)
                    q, k = m_qk[r, h // 2, :], m_qk[r, 2 + h // 2, :]
                    if j:
                        pe.wait_ge(dve_step, VS["ml P", j - 1])
                    for i in range(TT):
                        ts = slice(i * P, T) if d == 0 else slice(0, i * P + P)
                        o = TRI[3 - i if d else i]
                        m = pe.matmul(Z[:, o:o + ts.stop - ts.start], k[:, i * P:i * P + P], q[:, ts],
                                      start=True, stop=True, skip_group_check=True)
                    PE.did(m, "ml z", j)

                def maxima(j):
                    h, d = divmod(j, 2)
                    if j:
                        pe.wait_ge(dve_step, VS["ml Md", j - 1])
                    if j - 3 in OUT_AT:
                        pe.wait_ge(dve_step, VS["out h", OUT_AT[j - 3]])
                    PE.did(pe.matmul(banks[:, 5, :], pc("sel", (4 * d + h) * P, (4 * d + h + 1) * P, rows=64),
                                     m_M[:, :], start=True, stop=True), "ml M", j)

                def numerators(j):
                    h, d = divmod(j, 2)
                    pe.wait_ge(dve_step, VS["ml P", j])
                    if j:
                        pe.wait_ge(dve_step, VS["ml h", j - 1])
                    for t in range(TT):
                        ss = range(t, TT) if d else range(t + 1)
                        for i in ss:
                            o = TRI[3 - i] + t * P if d else TRI[i] + (t - i) * P
                            m = pe.matmul(banks[:, 6 + t // 2, (t % 2) * 256:(t % 2) * 256 + 129],
                                          m_P[j % 2][:, o:o + P], m_v[:, i, h, 0:129], start=(i == ss[0]),
                                          stop=(i == ss[-1]), skip_group_check=True)
                    PE.did(m, "ml num", j)

                def turn_h(h):
                    pe.wait_ge(dve_step, VS["ml hn", h])
                    bank = 5 if h + 1 < MH else 7
                    if bank == 5:
                        pe.wait_ge(dve_step, VS["ml Md", min(OUT_STEP[h] + 2, STEPS - 1)])
                        if h:
                            pe.wait_ge(dve_step, VS["out h", h - 1])
                    else:
                        pe.wait_ge(act_step, AS["la v", 1])
                    for t in range(TT):
                        m = pe.transpose(banks[:, bank, t * P:t * P + P], m_hn[h % 2][:, t, :], pc("ident"))
                    PE.did(m, "ml hT", h)

                def half(j, k):
                    b = B_MIX + 9 + j
                    product(b, b, b // 2, xh, xl, chunks=range(k * C // 2, (k + 1) * C // 2))

                pe.wait_ge(dve_step, VS["ml cols"])
                maxima(0)
                scores(0)
                maxima(1)
                for j in range(STEPS):
                    if j + 1 < STEPS:
                        scores(j + 1)
                    if j + 2 < STEPS:
                        maxima(j + 2)
                    half(j, 0)
                    numerators(j)
                    half(j, 1)
                    if j in OUT_AT:
                        turn_h(OUT_AT[j])
                pe.wait_ge(dve_step, VS["la sq"])
                PE.did(pe.matmul(banks[:, 2, :], pc("ones"), s1[:, :], start=True, stop=True), "la sum", 0)
                pe.wait_ge(act_step, AS["la sq", 2])
                PE.did(pe.matmul(banks[:, 3, :], pc("ones"), s2[:, :], start=True, stop=True), "la sum", 1)

                v_cols = pc("wukv").rearrange("p (h n) -> p h n", n=256)[:, :, P:2 * P]

                def latent_values(t):
                    if t == 2:
                        evacuated(pe, B_MIX + 15)
                        evacuated(pe, B_MIX + 16)
                    if t == 3:
                        pe.wait_ge(act_step, AS["la v", 0])
                    PE.did(pe.matmul(banks[:, (6, 7, 0, 6)[t], :], m_ckv[:, t * P:t * P + P], v_cols, start=True,
                                     stop=True), "la v", t)

                def before(h, step):
                    if step == 0:
                        if h:
                            pe.wait_ge(dve_step, VS["la key", h - 1])
                        else:
                            pe.wait_ge(dve_step, VS["la c"])
                        for bank, width, at in ((2, P, 0), (3, 64, P)):
                            for k in range(2):
                                o = k * 768 + h * 192 + at
                                pe.matmul(banks[0:width, bank, :], pc("wuq", o, o + width), m_cq[:, k, :],
                                          start=(k == 0), stop=(k == 1))
                        PE.did(pe.matmul(banks[:, 4, :], pc("wukv", h * 256, h * 256 + 128), m_ckv[:, :],
                                         start=True, stop=True), "la n", h)
                    if step == 1:
                        for side in range(2):
                            pe.wait_ge(act_step, AS["la nsq", h, side])
                            if side and h >= 2:
                                pe.wait_ge(dve_step, VS["la out", h - 2])
                            n2, r2 = ((sq[:, 0, :], sq[0:64, 1, :]), (tmp[:, 0, :], tmp[0:64, 1, :]))[side]
                            bank = (5, 1)[side]
                            pe.matmul(banks[:, bank, :], pc("ones"), n2, start=True, stop=False)
                            PE.did(pe.matmul(banks[:, bank, :], pc("ones", rows=64), r2, start=False, stop=True),
                                   "la nsum", h, side)
                    if step == 3:
                        for side in range(2):
                            pe.wait_ge(dve_step, VS["la pre", h, side])
                            PE.did(pe.matmul(banks[0:64, (3, 5)[side], :], pc("swap", rows=64), a_pre[side][:, :],
                                             start=True, stop=True), "la swap", h, side)

                def turn_p(n):
                    pe.wait_ge(dve_step, VS["la p", n])
                    if n:
                        pe.wait_ge(act_step, AS["la pT", n - 1])
                    for i in range(TT):
                        m = pe.transpose(banks[:, 0, i * P:i * P + P], a_p[:, n % 2, i * P:i * P + P], pc("ident"))
                    PE.did(m, "la pT", n)

                before(0, 0)
                pe.wait_ge(dve_step, VS["ml h", STEPS - 1])
                for t in range(3):
                    latent_values(t)
                pe.wait_ge(dve_step, VS["out h", MH - 2])
                before(0, 1)
                latent_values(3)
                turn_h(MH - 1)
                before(0, 3)
                pe.wait_ge(act_step, AS["la v", 3])
                pe.wait_ge(dve_step, VS["out h", MH - 1])
                for h in range(AH):
                    for side in range(2):
                        pe.wait_ge(dve_step, VS["la rope", h, side])
                    for t in range(TT):
                        n = 4 * h + t
                        ts = slice(t * P, t * P + P)
                        if n >= 2:
                            pe.wait_ge(act_step, AS["la e", n - 2])
                        pe.matmul(banks[:, 6 + n % 2, :], a_n[0][h % 2][:, ts], a_n[1][h % 2][:, :], start=True,
                                  stop=False)
                        PE.did(pe.matmul(banks[:, 6 + n % 2, :], a_r[0][h % 2][:, ts], a_r[1][h % 2][:, :],
                                         start=False, stop=True), "la s", n)
                        if t:
                            turn_p(n - 1)
                        if h + 1 < AH:
                            before(h + 1, t)
                    turn_p(4 * h + 3)
                    if h + 1 < AH:
                        pe.wait_ge(act_step, AS["la nrstd", h + 1, 1])
                    pe.wait_ge(act_step, AS["la pT", 4 * h + 3])
                    if h:
                        pe.wait_ge(dve_step, VS["la out", h - 1])
                    for i in range(TT):
                        m = pe.matmul(banks[:, 1, :], a_v[:, i, h * P:h * P + P], a_pT[:, i, :], start=(i == 0),
                                      stop=(i == 3))
                    PE.did(m, "la out", h)

            program(pe)

        @block.scalar
        def _(act):
            def last():
                act.wait_ge(act_step, AS.count)

            def exp_and_ln():
                act.preload_act_table_set("natural_log_exp_and_others")

            def bank(b):
                act.wait_ge(block_done, b + 1)
                return gb[b % 2]

            def mlp(b0, u0):
                for q in range(FFQ):
                    b = b0 + (2 * q - 1 if q else 0) * C
                    u = u0 + C * q
                    with act.Fori(0, C // 2) as i:
                        for j in range(2):
                            act.wait_ge(up_squared, i * 2 + (u + j + 1))
                            act.wait_ge(block_done, i * 2 + (b + j + 1))
                            nc.scalar.activation(relu[:, j, :], gb[(b + j) % 2], ACT.Relu).then_inc(relu_done, 1)

            def square(name, c):
                if c >= 2:
                    act.wait_ge(*sq_added(name, c - 2))
                AS.did(nc.scalar.activation(sq[:, c % 2, :], res[:, c, :], ACT.Square), name, "sq", c)

            def squares(name, b0):
                for c in range(C):
                    evacuated(act, b0 + c)
                    square(name, c)

            def norm(name, g, b, eps, center, split, next_norm=None):
                if center:
                    act.wait_ge(pe_step, PE[name, "sum", 0])
                    AS.did(nc.scalar.activation(tmp2[:, 1, :], banks[:, 2, :], ACT.Square), name, "mean sq")
                    act.wait_ge(dve_step, VS[name, "var"])
                    AS.did(nc.scalar.activation(rstd[:, :], tmp2[:, 0, :], ACT.Ln, bias=pc(eps)))
                else:
                    act.wait_ge(pe_step, PE[name, "sum", 1])
                    AS.did(nc.scalar.activation(rstd[:, :], banks[:, 2, :], ACT.Ln, bias=pc(eps)))
                last()
                AS.did(nc.scalar.activation(rstd[:, :], rstd[:, :], ACT.Exp, scale=-0.5), name, "rstd")
                for c in range(C):
                    act.wait_ge(dve_step, VS[name, "scaled", c])
                    if center:
                        AS.did(nc.scalar.activation(res[:, c, :], tmp[:, c % 2, :], ACT.Identity,
                                                    scale=pc(g[0], g[1] + c, g[1] + c + 1),
                                                    bias=pc(b[0], b[1] + c, b[1] + c + 1)), name, "out", c)
                        last()
                    if split:
                        AS.did(nc.scalar.activation(xh[:, c, :], res[:, c, :] if center else tmp2[:, c % 2, :],
                                                    ACT.Copy), name, "hi", c)
                    if next_norm:
                        square(next_norm, c)

            def mixer_act(act):
                act.dma_start(par2[:, :], PAR[:, NPAR1:NPAR]).then_inc(par2_in, 16)
                act.dma_start(a_posi, POS).then_inc(pos_in, 16)
                act.wait_ge(dve_step, VS["la ang"])
                AS.did(nc.scalar.activation(a_sin[:, :], a_ang[:, 0, :], ACT.Sin))
                AS.did(nc.scalar.activation(a_ang[:, 1, :], a_ang[:, 0, :], ACT.Abs))
                last()
                AS.did(nc.scalar.activation(a_cos[:, :], a_ang[:, 1, :], ACT.Sin, scale=-1.0,
                                            bias=pc("half_pi", rows=64)), "la tables")
                for c in range(4):
                    act.wait_ge(dve_step, VS["ml conv", c])
                    if c >= 2:
                        act.wait_ge(dve_step, VS["ml qk", c - 2])
                    AS.did(nc.scalar.activation(tmp[:, c % 2, :], m_qk[:, c, :], ACT.Sigmoid), "ml sig", c)
                exp_and_ln()
                act.wait_ge(dve_step, VS["ml F"])
                AS.did(nc.scalar.activation(m_u[:, :], m_F[:, :], ACT.Abs))
                last()
                AS.did(nc.scalar.activation(m_u[:, :], m_u[:, :], ACT.Exp, scale=-1.0))
                last()
                AS.did(nc.scalar.activation(m_u[:, :], m_u[:, :], ACT.Ln, bias=pc("one", 0, 1, rows=64)), "ml l")
                act.wait_ge(dve_step, VS["ml m"])
                AS.did(nc.scalar.activation(m_u[:, :], m_F[:, :], ACT.Exp, scale=-1.0), "ml e")
                for t in range(TT):
                    act.wait_ge(pe_step, PE["mv turned", t])
                    AS.did(nc.scalar.activation(m_v[:, t, :, 0:P], banks[:, 2 + t % 2, :].rearrange(
                        "p (h n) -> p h n", n=P), ACT.Copy), "mv turned", t)
                STEPS = 2 * MH

                def weights(j):
                    h, d = divmod(j, 2)
                    E = m_E[j % 2]
                    act.wait_ge(dve_step, VS["ml Md", j])
                    if j >= 2:
                        act.wait_ge(dve_step, VS["ml P", j - 2])
                    for i in range(TT):
                        G = m_Gc[:, i, 32 * d + h:32 * d + h + 1]
                        a, b = (0, i * P) if d else (i * P + P, T)
                        o = TRI[3 - i] if d else TRI[i] + P
                        od = TRI[3 - i] + i * P if d else TRI[i]
                        if b > a:
                            AS.did(nc.scalar.activation(E[:, o:o + b - a], m_Mb[:, a:b], ACT.Exp, bias=G, scale=-1.0))
                        AS.did(nc.scalar.activation(E[:, od:od + P], m_Md[:, i * P:i * P + P], ACT.Exp, bias=G,
                                                    scale=-1.0), *(("ml E", j) if i == 3 else ()))

                def head_rstd(h):
                    act.wait_ge(dve_step, VS["ml h", 2 * h + 1])
                    if h:
                        act.wait_ge(dve_step, VS["ml hn", h - 1])
                    for t in range(TT):
                        AS.did(nc.scalar.activation(tmp[:, 0, t * P:t * P + P], m_h[h % 2][:, t, :], ACT.Square,
                                                    accum_out=m_ss[:, t:t + 1]))
                    last()
                    AS.did(nc.scalar.activation(m_ss[:, :], m_ss[:, :], ACT.Ln, scale=1 / 128.0, bias=pc("rms_eps")))
                    last()
                    AS.did(nc.scalar.activation(m_ss[:, :], m_ss[:, :], ACT.Exp, scale=-0.5), "ml rstd", h)

                weights(0)
                weights(1)
                for j in range(STEPS):
                    if j + 2 < STEPS:
                        weights(j + 2)
                    act.wait_ge(pe_step, PE["ml num", j])
                    if j:
                        act.wait_ge(dve_step, VS["ml h", j - 1])
                    dens = banks[:, 6:8, :].rearrange("p a (b c) -> p (a b) c", c=256)[:, :, 128]
                    AS.did(nc.scalar.activation(m_dn[:, :], dens, ACT.Abs), "ml den", j)
                    if j == 4:
                        evacuated(act, B_MIX + 11)
                        evacuated(act, B_MIX + 12)
                        AS.did(nc.scalar.activation(m_o[:, :, :], m_o[:, :, :], ACT.Sigmoid), "ml o")
                        exp_and_ln()
                    if j % 2 == 0 and j:
                        head_rstd(j // 2 - 1)
                    if j == 6:
                        evacuated(act, B_MIX + 13)
                        evacuated(act, B_MIX + 14)
                        AS.did(nc.scalar.activation(sq[:, 0, :], m_cq[:, 0, :], ACT.Square))
                        AS.did(nc.scalar.activation(s1[:, :], m_cq[:, 1, :], ACT.Square), "la sq", 1)
                    if j == 7:
                        evacuated(act, B_MIX + 15)
                        AS.did(nc.scalar.activation(s2[:, :], m_ckv[:, :], ACT.Square), "la sq", 2)
                for k, scale in enumerate((D / 256, D / 128)):
                    act.wait_ge(pe_step, PE["la sum", k])
                    r = (mean, rstd)[k]
                    AS.did(nc.scalar.activation(r[:, :], banks[:, 2 + k, :], ACT.Ln, scale=scale, bias=pc("rms_eps")))
                    last()
                    AS.did(nc.scalar.activation(r[:, :], r[:, :], ACT.Exp, scale=-0.5), "la rstd", k)
                head_rstd(MH - 1)

                def latent_values(t):
                    act.wait_ge(pe_step, PE["la v", t])
                    AS.did(nc.scalar.activation(a_v[:, t, :], banks[:, (6, 7, 0, 6)[t], :], ACT.Copy), "la v", t)

                evacuated(act, B_MIX + 16)
                AS.did(nc.scalar.activation(tmp[0:64, 1, :], m_kpe[:, :], ACT.Square))

                def before(h, step):
                    if step == 0:
                        act.wait_ge(pe_step, PE["la n", h])
                        if h:
                            act.wait_ge(pe_step, PE["la nsum", h - 1, 1])
                        AS.did(nc.scalar.activation(sq[:, 0, :], banks[:, 2, :], ACT.Square))
                        AS.did(nc.scalar.activation(sq[0:64, 1, :], banks[0:64, 3, :], ACT.Square), "la nsq", h, 0)
                        AS.did(nc.scalar.activation(tmp[:, 0, :], banks[:, 4, :], ACT.Square), "la nsq", h, 1)
                    if step == 1:
                        for side in range(2):
                            r = (rstd, mean)[side][:, :]
                            act.wait_ge(pe_step, PE["la nsum", h, side])
                            if h:
                                act.wait_ge(dve_step, VS["la pre", h - 1, side])
                            AS.did(nc.scalar.activation(r, banks[:, (5, 1)[side], :], ACT.Ln, scale=D / 192,
                                                        bias=pc("rms_eps")))
                            last()
                            AS.did(nc.scalar.activation(r, r, ACT.Exp, scale=-0.5), "la nrstd", h, side)

                def copy_p(n):
                    h, t = divmod(n, TT)
                    act.wait_ge(pe_step, PE["la pT", n])
                    if h and t == 0:
                        act.wait_ge(pe_step, PE["la out", h - 1])
                    AS.did(nc.scalar.activation(a_pT[:, :, t * P:t * P + P], banks[:, 0, :].rearrange(
                        "p (i t) -> p i t", t=P), ACT.Copy), "la pT", n)

                before(0, 0)
                for t in range(3):
                    latent_values(t)
                before(0, 1)
                latent_values(3)
                for h in range(AH):
                    for t in range(TT):
                        n = 4 * h + t
                        act.wait_ge(dve_step, VS["la max", n])
                        if n >= 2:
                            act.wait_ge(pe_step, PE["la pT", n - 2])
                        AS.did(nc.scalar.activation(a_p[:, n % 2, :], banks[:, 6 + n % 2, :], ACT.Exp,
                                                    scale=192 ** -0.5, bias=m_dn[:, n % 2:n % 2 + 1],
                                                    accum_out=m_ss[:, n % 2:n % 2 + 1]), "la e", n)
                        if t:
                            copy_p(n - 1)
                        if h + 1 < AH:
                            before(h + 1, t)
                    copy_p(4 * h + 3)

            for c in range(C):
                act.wait_ge(x_in[c], 16)
                AS.did(nc.scalar.activation(xh[:, c, :], res[:, c, :], ACT.Copy), "x hi", c)
            b = bank(0)
            nc.scalar.activation(g_a1[:, :], b[0:16, :], ACT.Copy).then_inc(bank_free[0], 1)
            exp_and_ln()

            def softplus(h):
                act.wait_ge(pe_step, PE["gate", h])
                z, e = g_ke[:, h, :], g_qd[:, h, :]
                AS.did(nc.scalar.activation(z, banks[:, GATE_BANKS[h], :], ACT.Identity, bias=pc("ba", h, h + 1)),
                       "z", h)
                last()
                AS.did(nc.scalar.activation(e, z, ACT.Abs))
                last()
                AS.did(nc.scalar.activation(e, e, ACT.Exp, scale=-1.0))
                last()
                AS.did(nc.scalar.activation(e, e, ACT.Ln, bias=pc("one", 0, 1)), "l", h)

            def decays(h):
                act.wait_ge(dve_step, VS["to end", h])
                b = g_kd[:, h, :]
                AS.did(nc.scalar.activation(g_qd[:, h, :], b, ACT.Exp, scale=1 / 16.0))
                AS.did(nc.scalar.activation(g_dec[:, h, :], b.rearrange("p (n c) -> p n c", c=GC)[:, :, GC - 1],
                                            ACT.Exp, scale=1 / 16.0))
                last()
                AS.did(nc.scalar.activation(b, b, ACT.Exp, scale=-1 / 16.0))
                AS.did(nc.scalar.activation(g_ke[:, h, :], g_ke[:, h, :], ACT.Exp, scale=1 / 16.0), "decays", h)

            def v_turned(h, e):
                act.wait_ge(pe_step, PE["v turned", h, e])
                AS.did(nc.scalar.activation(g_v[:, h % 2, :, e * P:e * P + P],
                                            banks[:, 2, :].rearrange("p (t n) -> p t n", n=P), ACT.Copy),
                       "v turned", h, e)

            softplus(0)
            softplus(1)
            decays(0)
            softplus(2)
            decays(1)
            softplus(3)
            decays(2)
            decays(3)
            v_turned(0, 0)
            for h in range(GH):
                for t in range(TT):
                    n = 4 * h + t
                    act.wait_ge(pe_step, PE["k turned", n])
                    AS.did(nc.scalar.activation(g_ket[:, n % 2, :], banks[:, 7, 256:256 + P], ACT.Copy),
                           "k turned", n)
                    if t == 0:
                        v_turned(h, 1)
                    if t == 2:
                        evacuated(act, gla_block("g0", h))
                        evacuated(act, gla_block("g1", h))
                        AS.did(nc.scalar.activation(tmp[:, :, :], g_g[:, :, :], ACT.Sigmoid), "g sig", h)
                        exp_and_ln()
                    act.wait_ge(pe_step, PE["inter", h, 2 * t + 1])
                    if n >= 2:
                        act.wait_ge(dve_step, VS["o normed", n - 2])
                    s = g_ss[:, 2 * (n % 2):2 * (n % 2) + 1]
                    d = g_ss[:, 2 * (n % 2) + 1:2 * (n % 2) + 2]
                    AS.did(nc.scalar.activation(g_junk[:, :], banks[:, 5 + n % 2, 0:256], ACT.Square, accum_out=s))
                    last()
                    AS.did(nc.scalar.activation(d, s, ACT.Ln, scale=1 / 256.0, bias=pc("rms_eps")))
                    last()
                    AS.did(nc.scalar.activation(d, d, ACT.Exp, scale=-0.5), "o rstd", n)
                    if t == 3 and h + 1 < GH:
                        v_turned(h + 1, 0)
            squares("ln1", B_GLA_OUT)
            norm("ln1", ("ln", 0), ("ln", 8), "ln_eps", True, True)
            mlp(B_MLP1, 0)
            squares("ln2", B_MLP1 + 7 * C)
            norm("ln2", ("ln", 16), ("ln", 24), "ln_eps", True, True)
            AS.did(nc.scalar.activation(t_one[:, 0, :], pc("one"), ACT.Copy))
            AS.did(nc.scalar.activation(t_one[:, 1, :], pc("tri"), ACT.Copy), "ones split")

            def v_turned(c):
                act.wait_ge(pe_step, PE["sv turned", c])
                if c >= 2:
                    act.wait_ge(pe_step, PE["sb o", 2 * c - 3])
                AS.did(nc.scalar.activation(t_v[:, c % 2, :], gb[0], ACT.Copy), "sv turned", c)

            def softplus(h):
                e = t_e[:, h % 2, :]
                act.wait_ge(dve_step, VS["sb m", h])
                AS.did(nc.scalar.activation(e, e, ACT.Exp))
                last()
                AS.did(nc.scalar.activation(e, e, ACT.Ln, bias=pc("one", 0, 1)), "sb l", h)

            def take_pair(c, part):
                b = B_SB + 3 * c + part
                if c >= 2:
                    act.wait_ge(pe_step, PE[("sv turned", c - 2) if part == 2 else ("sb z", 2 * c - 3)])
                bank(b)
                src = gb[1 if c == 0 and part == 1 else 0]
                nc.scalar.activation((t_q, t_k, t_vT)[part][:, c % 2, :], src, ACT.Copy,
                                     scale=0.125 if part == 0 else 1.0).then_inc(bank_free[b % 2], 1)

            for part in range(3):
                take_pair(0, part)
            v_turned(0)
            softplus(0)
            for h in range(SH):
                c = h // 2 + 1
                if h + 1 < SH:
                    softplus(h + 1)
                if c < C:
                    take_pair(c, 2 if h % 2 else 0)
                act.wait_ge(dve_step, VS["sb lw", h])
                AS.did(nc.scalar.activation(t_e[:, h % 2, :], t_sp[:, h % 2, :], ACT.Exp), "sb w", h)
                if c < C:
                    if h % 2:
                        v_turned(c)
                    else:
                        take_pair(c, 1)
            squares("ln3", B_SB_OUT)
            norm("ln3", ("ln", 32), ("ln", 40), "ln_eps", True, True)
            mlp(B_MLP2, 32)
            squares("ln4", B_MLP2 + 7 * C)
            norm("ln4", ("ln", 48), ("ln", 56), "ln_eps", True, False, "rms1")
            norm("rms1", ("gmix", 0), None, "rms_eps", False, True)
            mixer_act(act)
            squares("rms2", B_MIX_OUT)
            norm("rms2", ("gffn", 0), None, "rms_eps", False, True)
            mlp(B_MLP3, 64)

        @block.vector
        def _(dve):
            def last():
                dve.wait_ge(dve_step, VS.count)

            def take(dst, b, scale=1.0, bank=None):
                dve.wait_ge(block_done, b + 1)
                nc.vector.tensor_scalar(dst, gb[b % 2] if bank is None else bank, scale, None, ALU.mult).then_inc(bank_free[b % 2], 1)

            def add_residual(name, b0, alpha, sums):
                for c in range(C):
                    b = b0 + c
                    dve.wait_ge(block_done, b + 1)
                    nc.vector.scalar_tensor_tensor(out=res[:, c, :], in0=res[:, c, :], scalar=alpha, in1=gb[b % 2],
                                                   op0=ALU.mult, op1=ALU.add).then_inc(bank_free[b % 2], 1)
                    if c == C - 1 or not sums:
                        continue
                    evacuated(dve, b)
                    if sums == 2:
                        if c:
                            dve.wait_ge(dve_step, VS[name, "added", c - 1])
                        VS.did(nc.vector.tensor_tensor(s1[:, :], res[:, c, :], s1[:, :] if c else zero[:, :],
                                                       ALU.add), name, "added", c)
                    dve.wait_ge(act_step, AS[name, "sq", c])
                    if c:
                        dve.wait_ge(dve_step, VS[name, "sq added", c - 1])
                    VS.did(nc.vector.tensor_tensor(s2[:, :], sq[:, c % 2, :], s2[:, :] if c else zero[:, :],
                                                   ALU.add), name, "sq added", c)

            def norm(name, center):
                def less_mean(c):
                    VS.did(nc.vector.tensor_tensor(res[:, c, :], res[:, c, :], banks[:, 2, :], ALU.subtract),
                           name, "centred", c)

                if center:
                    dve.wait_ge(pe_step, PE[name, "sum", 1])
                    dve.wait_ge(act_step, AS[name, "mean sq"])
                    VS.did(nc.vector.tensor_tensor(tmp2[:, 0, :], banks[:, 3, :], tmp2[:, 1, :], ALU.subtract))
                    last()
                    VS.did(nc.vector.tensor_scalar(tmp2[:, 0, :], tmp2[:, 0, :], 0.0, None, ALU.max), name, "var")
                    less_mean(0)
                    less_mean(1)
                dve.wait_ge(act_step, AS[name, "rstd"])
                for c in range(C):
                    if center:
                        if c >= 2:
                            dve.wait_ge(act_step, AS[name, "out", c - 2])
                        dve.wait_ge(dve_step, VS[name, "centred", c])
                        VS.did(nc.vector.tensor_tensor(tmp[:, c % 2, :], res[:, c, :], rstd[:, :], ALU.mult),
                               name, "scaled", c)
                        if c + 2 < C:
                            less_mean(c + 2)
                        continue
                    if c >= 2:
                        dve.wait_ge(*low_ready(name, center)[c - 2])
                    g = pc(*({"rms1": ("gmix", c, c + 1), "rms2": ("gffn", c, c + 1)}[name]))
                    VS.did(nc.vector.scalar_tensor_tensor(out=tmp2[:, c % 2, :], in0=res[:, c, :], scalar=g,
                                                          in1=rstd[:, :], op0=ALU.mult, op1=ALU.mult),
                           name, "scaled", c)
                    if c % 2 == 0:
                        dve.wait_ge(act_step, AS[name, "hi", c])
                        VS.did(nc.vector.tensor_tensor(xl[:, c, :], tmp2[:, c % 2, :], xh[:, c, :].bitcast(F32),
                                                       ALU.subtract), name, "split", c)

            def split_pair(c):
                dve.wait_ge(pe_step, PE["sb o", 2 * c + 1])
                VS.did(nc.vector.tensor_copy(t_oh[:, c, :], gb[1]))
                last()
                VS.did(nc.vector.tensor_tensor(t_ol[:, c, :], gb[1], t_oh[:, c, :].bitcast(F32), ALU.subtract),
                       "sb split", c)

            def mlp(b0, u0, alpha, name, sums):
                def down(b, first):
                    with dve.Fori(0, C // 2) as i:
                        for j in range(2):
                            dve.wait_ge(block_done, i * 2 + (b + j + 1))
                            r = res[:, bass.ds(i * 2 + j, 1), :].rearrange("p a t -> p (a t)")
                            nc.vector.scalar_tensor_tensor(
                                out=r, in0=r, scalar=alpha if first else 1.0, in1=gb[(b + j) % 2],
                                op0=ALU.mult, op1=ALU.add).then_inc(bank_free[(b + j) % 2], 1)

                for q in range(FFQ):
                    b = b0 + (2 * q - 1 if q else 0) * C
                    u = u0 + C * q
                    with dve.Fori(0, C // 2) as i:
                        for j in range(2):
                            dve.wait_ge(relu_done, i * 2 + (u + j + 1))
                            nc.vector.scalar_tensor_tensor(out=tmp2[:, j, :], in0=gb[(b + j) % 2], scalar=0.0,
                                                           in1=relu[:, j, :], op0=ALU.max,
                                                           op1=ALU.mult).then_inc(bank_free[(b + j) % 2], 1)
                            dve.wait_ge(bank_free[(b + j) % 2], i + ((b + j) // 2 + 1))
                            h = hh[q % 2][:, bass.ds(i * 2 + j, 1), :].rearrange("p a t -> p (a t)")
                            l = hl[q % 2][:, bass.ds(i * 2 + j, 1), :].rearrange("p a t -> p (a t)")
                            nc.vector.tensor_scalar(h, tmp2[:, j, :], 1.0, None, ALU.mult).then_inc(up_squared, 1)
                            dve.wait_ge(up_squared, i * 2 + (u + j + 3))
                            nc.vector.tensor_tensor(l, tmp2[:, j, :], h.bitcast(F32),
                                                    ALU.subtract).then_inc(hidden_ready, 1)
                    if q:
                        down(b + C, q == 1)
                add_residual(name, b0 + 7 * C, 1.0, sums)

            def split_out(c, src):
                last()
                VS.did(nc.vector.tensor_scalar(xh[:, c, :], src, 1.0, None, ALU.mult))
                last()
                VS.did(nc.vector.tensor_tensor(xl[:, c, :], src, xh[:, c, :].bitcast(F32), ALU.subtract),
                       "mix split", c)

            def mixer_dve(dve):
                dve.wait_ge(pos_in, 16)
                ang, k = a_ang[:, 0, :], a_ang[:, 1, :]
                VS.did(nc.vector.tensor_scalar(ang, a_posi, pc("freq", rows=64), None, ALU.mult))
                last()
                VS.did(nc.vector.tensor_scalar(k, ang, 1 / TWO_PI, ROUND, ALU.mult, ALU.add))
                last()
                VS.did(nc.vector.tensor_scalar(k, k, ROUND, None, ALU.subtract))
                for part in TWO_PI_PARTS:
                    last()
                    VS.did(nc.vector.scalar_tensor_tensor(out=ang, in0=k, scalar=-part, in1=ang, op0=ALU.mult,
                                                          op1=ALU.add))
                last()
                VS.did(nc.vector.tensor_scalar(ang, ang, 3.1415925, -3.1415925, ALU.min, ALU.max), "la ang")
                VS.did(nc.vector.memset(m_v[:, :, :, P:P + 2], 1.0))

                def convolve(c):
                    w = [pc("convw", 5 * c + j, 5 * c + j + 1) for j in range(5)]
                    evacuated(dve, B_MIX + c)
                    VS.did(nc.vector.tensor_scalar(m_qk[:, c, :], m_raw[:, c, :], w[2], pc("convb", c, c + 1),
                                                   ALU.mult, ALU.add))
                    for n, j in enumerate((0, 1, 3, 4)):
                        last()
                        a, b = max(0, 2 - j), T - max(0, j - 2)
                        o = m_qk[:, c, a:b]
                        VS.did(nc.vector.scalar_tensor_tensor(out=o, in0=m_raw[:, c, a + j - 2:b + j - 2],
                                                              scalar=w[j], in1=o, op0=ALU.mult, op1=ALU.add),
                               *(("ml conv", c) if n == 3 else ()))

                for c in range(4):
                    take(m_raw[:, c, :], B_MIX + c)
                    convolve(c)
                k = (B_MIX + 4) % 2
                dve.wait_ge(block_done, B_MIX + 5)
                VS.did(nc.vector.tensor_copy(m_F[:, :], banks[0:64, k, :]))
                nc.vector.tensor_copy(m_I[:, :], banks[64:P, k, :]).then_inc(bank_free[k], 1)
                last()
                VS.did(nc.vector.tensor_scalar(m_F[:, :], m_F[:, :], pc("bf", rows=64), None, ALU.add), "ml F")
                evacuated(dve, B_MIX + 4)
                VS.did(nc.vector.tensor_scalar(m_I[:, :], m_I[:, :], pc("bi", rows=64), None, ALU.add))
                for c in range(4):
                    dve.wait_ge(act_step, AS["ml sig", c])
                    VS.did(nc.vector.scalar_tensor_tensor(out=m_qk[:, c, :], in0=m_qk[:, c, :],
                                                          scalar=0.125 if c < 2 else 1.0, in1=tmp[:, c % 2, :],
                                                          op0=ALU.mult, op1=ALU.mult), "ml qk", c)
                take(m_vT[:, 0, :], B_MIX + 5)
                dve.wait_ge(act_step, AS["ml l"])
                VS.did(nc.vector.scalar_tensor_tensor(out=m_F[:, :], in0=m_F[:, :], scalar=0.0, in1=m_u[:, :],
                                                      op0=ALU.min, op1=ALU.subtract))
                last()
                for d in range(2):
                    r, step = slice(32 * d, 32 * d + 32), -1 if d else 1
                    VS.did(nc.vector.tensor_tensor_scan(m_B[r, ::step], zero[r, 0:T], m_F[r, ::step], 0.0,
                                                        ALU.add, ALU.add))
                last()
                VS.did(nc.vector.tensor_tensor(m_I[:, :], m_I[:, :], m_B[:, :], ALU.subtract), "ml G")
                last()
                for d in range(2):
                    r, step = slice(32 * d, 32 * d + 32), -1 if d else 1
                    VS.did(nc.vector.tensor_tensor_scan(m_M[r, ::step], m_I[r, ::step], zero[r, 0:T], 0.0,
                                                        ALU.max, ALU.add))
                last()
                VS.did(nc.vector.tensor_tensor(m_F[:, :], m_B[:, :], m_M[:, :], ALU.add), "ml m")
                for c in range(1, 4):
                    take(m_vT[:, c, :], B_MIX + 5 + c)
                dve.wait_ge(pe_step, PE["ml G"])
                VS.did(nc.vector.tensor_copy(m_Gc[:, :, :].rearrange("p a b -> p (a b)"), banks[:, 2, 0:256]))
                dve.wait_ge(pe_step, PE["ml e"])
                VS.did(nc.vector.tensor_copy(m_Ec[:, :, :].rearrange("p a b -> p (a b)"), banks[:, 3, 0:256]),
                       "ml cols")
                Z = banks[:, 2:5, :].rearrange("p a b -> p (a b)")[:, 0:1280]
                STEPS = 2 * MH

                def maxima(j):
                    d = j % 2
                    dve.wait_ge(pe_step, PE["ml M", j])
                    if j:
                        dve.wait_ge(act_step, AS["ml E", j - 1])
                    VS.did(nc.vector.tensor_copy(m_Mb[:, :], banks[:, 5, :]))
                    last()
                    VS.did(nc.vector.tensor_tensor(m_Md[:, :].rearrange("p (a b) -> p a b", b=P),
                                                   m_Mb[:, :].rearrange("p (a b) -> p a b", b=P),
                                                   pc("neg_bw" if d else "neg_fw").unsqueeze(1)
                                                   .broadcast_to([P, 4, P]), ALU.add), "ml Md", j)

                def weigh(j):
                    dve.wait_ge(act_step, AS["ml E", j])
                    dve.wait_ge(pe_step, PE["ml z", j])
                    if j >= 2:
                        dve.wait_ge(pe_step, PE["ml num", j - 2])
                    VS.did(nc.vector.tensor_tensor(m_P[j % 2][:, :], Z, m_E[j % 2], ALU.mult), "ml P", j)

                def quotient(j):
                    h, d = divmod(j, 2)
                    hs = m_h[h % 2]
                    dve.wait_ge(act_step, AS["ml den", j])
                    VS.did(nc.vector.tensor_tensor(m_dn[:, :], m_dn[:, :], m_Ec[:, :, 32 * d + h], ALU.max))
                    last()
                    VS.did(nc.vector.reciprocal(m_dn[:, :], m_dn[:, :]))
                    last()
                    for t in range(TT):
                        num = banks[:, 6 + t // 2, (t % 2) * 256:(t % 2) * 256 + P]
                        if d == 0:
                            ins = nc.vector.tensor_scalar(hs[:, t, :], num, m_dn[:, t:t + 1], None, ALU.mult)
                        else:
                            ins = nc.vector.scalar_tensor_tensor(out=hs[:, t, :], in0=num,
                                                                 scalar=m_dn[:, t:t + 1], in1=hs[:, t, :],
                                                                 op0=ALU.mult, op1=ALU.add)
                        VS.did(ins, *(("ml h", j) if t == 3 else ()))
                    last()

                def normalise(h):
                    dve.wait_ge(act_step, AS["ml rstd", h])
                    if h >= 2:
                        dve.wait_ge(pe_step, PE["ml hT", h - 2])
                    for t in range(TT):
                        VS.did(nc.vector.tensor_scalar(m_hn[h % 2][:, t, :], m_h[h % 2][:, t, :], m_ss[:, t:t + 1], None,
                                                       ALU.mult), *(("ml hn", h) if t == 3 else ()))

                def put_out(h):
                    dve.wait_ge(pe_step, PE["ml hT", h])
                    dve.wait_ge(act_step, AS["ml o"])
                    VS.did(nc.vector.scalar_tensor_tensor(out=m_o[:, h, :], in0=banks[:, 5 if h + 1 < MH else 7, :],
                                                          scalar=pc("gout", h, h + 1), in1=m_o[:, h, :],
                                                          op0=ALU.mult, op1=ALU.mult), "out h", h)

                def through(j):
                    b = B_MIX + 9 + j
                    if j == 7:
                        dve.wait_ge(block_done, b + 1)
                        nc.vector.tensor_copy(m_kpe[:, :], banks[0:64, b % 2, :]).then_inc(bank_free[b % 2], 1)
                    else:
                        take(m_o[:, j, :] if j < 4 else m_cq[:, j - 4, :] if j < 6 else m_ckv[:, :], b)

                maxima(0)
                maxima(1)
                weigh(0)
                for j in range(STEPS):
                    if j + 1 < STEPS:
                        weigh(j + 1)
                    if j + 2 < STEPS:
                        maxima(j + 2)
                    if j == 7:
                        dve.wait_ge(act_step, AS["la sq", 1])
                        VS.did(nc.vector.tensor_tensor(s1[:, :], sq[:, 0, :], s1[:, :], ALU.add), "la sq")
                    quotient(j)
                    if j % 2 == 0 and j:
                        normalise(j // 2 - 1)
                    through(j)
                    if j in OUT_AT:
                        put_out(OUT_AT[j])
                for k in range(2):
                    dve.wait_ge(act_step, AS["la rstd", 0])
                    VS.did(nc.vector.scalar_tensor_tensor(out=m_cq[:, k, :], in0=m_cq[:, k, :],
                                                          scalar=pc("gcq", k, k + 1), in1=mean[:, :], op0=ALU.mult,
                                                          op1=ALU.mult))
                dve.wait_ge(act_step, AS["la rstd", 1])
                VS.did(nc.vector.scalar_tensor_tensor(out=m_ckv[:, :], in0=m_ckv[:, :], scalar=pc("gckv"),
                                                      in1=rstd[:, :], op0=ALU.mult, op1=ALU.mult), "la c")
                normalise(MH - 1)

                dve.wait_ge(act_step, AS["la tables"])

                def before(h, step):
                    def scaled(side):
                        n_g, r_g = (("gqn", "gqr"), ("gkn", "gkr"))[side]
                        r = (rstd, mean)[side]
                        dve.wait_ge(act_step, AS["la nrstd", h, side])
                        VS.did(nc.vector.scalar_tensor_tensor(out=a_n[side][h % 2][:, :],
                                                              in0=banks[:, 4 if side else 2, :], scalar=pc(n_g),
                                                              in1=r[:, :], op0=ALU.mult, op1=ALU.mult),
                               *(("la key", h) if side else ()))
                        VS.did(nc.vector.scalar_tensor_tensor(out=a_pre[side][:, :],
                                                              in0=m_kpe[:, :] if side else banks[0:64, 3, :],
                                                              scalar=pc(r_g, rows=64), in1=r[0:64, :],
                                                              op0=ALU.mult, op1=ALU.mult), "la pre", h, side)
                        last()
                        VS.did(nc.vector.tensor_tensor(a_r[side][h % 2][:, :], a_pre[side][:, :], a_cos[:, :],
                                                       ALU.mult))

                    def turned(side):
                        dve.wait_ge(pe_step, PE["la swap", h, side])
                        VS.did(nc.vector.tensor_tensor(a_swap[:, :], banks[0:64, (3, 5)[side], :], a_sin[:, :], ALU.mult))
                        last()
                        r = a_r[side][h % 2][:, :]
                        VS.did(nc.vector.tensor_tensor(r, r, a_swap[:, :], ALU.add), "la rope", h, side)
                        last()

                    if step in (1, 2):
                        scaled(step - 1)
                    if step == 3:
                        turned(0)
                        turned(1)

                def normal_p(n):
                    dve.wait_ge(act_step, AS["la e", n])
                    VS.did(nc.vector.reciprocal(m_dn[:, 3:4], m_ss[:, n % 2:n % 2 + 1]))
                    last()
                    VS.did(nc.vector.tensor_scalar(a_p[:, n % 2, :], a_p[:, n % 2, :], m_dn[:, 3:4], None, ALU.mult),
                           "la p", n)
                    last()

                before(0, 1)
                before(0, 2)
                put_out(MH - 1)
                before(0, 3)
                for c in range(MH):
                    split_out(c, m_o[:, c, :])
                for h in range(AH):
                    for t in range(TT):
                        n = 4 * h + t
                        if h + 1 < AH and t == 2:
                            before(h + 1, 1)
                        dve.wait_ge(pe_step, PE["la s", n])
                        VS.did(nc.vector.reduce_max(m_dn[:, 2:3], banks[:, 6 + n % 2, :], AX.X))
                        last()
                        VS.did(nc.vector.tensor_scalar(m_dn[:, n % 2:n % 2 + 1], m_dn[:, 2:3], -(192 ** -0.5), None,
                                                       ALU.mult), "la max", n)
                        if h + 1 < AH and t == 2:
                            before(h + 1, 2)
                        normal_p(n)
                        if h + 1 < AH and t == 3:
                            before(h + 1, 3)
                    dve.wait_ge(pe_step, PE["la out", h])
                    VS.did(nc.vector.tensor_copy(tmp2[:, 1, :], banks[:, 1, :]), "la out", h)
                    split_out(MH + h, tmp2[:, 1, :])

            VS.did(nc.vector.memset(g_att[:, :, :], 0.0))
            nc.vector.memset(tmp[:, :, :], 0.0).then_inc(up_squared, 2)
            for c in range(C):
                dve.wait_ge(act_step, AS["x hi", c])
                VS.did(nc.vector.tensor_tensor(xl[:, c, :], res[:, c, :], xh[:, c, :].bitcast(F32), ALU.subtract),
                       "x split", c)

            def log_gates(h):
                z, b = g_ke[:, h, :], g_kd[:, h, :]
                dve.wait_ge(act_step, AS["l", h])
                VS.did(nc.vector.scalar_tensor_tensor(out=z, in0=z, scalar=0.0, in1=g_qd[:, h, :], op0=ALU.min,
                                                      op1=ALU.subtract))
                last()
                VS.did(nc.vector.tensor_tensor_scan(b, pc("reset"), z, 0.0, ALU.mult, ALU.add))
                last()
                b3 = b.rearrange("p (n c) -> p n c", c=GC)
                VS.did(nc.vector.tensor_tensor(z.rearrange("p (n c) -> p n c", c=GC),
                                               b3[:, :, GC - 1:GC].broadcast_to([P, T // GC, GC]), b3,
                                               ALU.subtract), "to end", h)

            def through(kind, h):
                b = gla_block(kind, h)
                dve.wait_ge(block_done, b + 1)
                if kind in ("g0", "g1"):
                    take(g_g[:, int(kind[1]), :], b)
                elif kind in ("v0", "v1"):
                    if h:
                        dve.wait_ge(pe_step, PE["v turned", h - 1, int(kind[1])])
                    take(g_vT[:, int(kind[1]), :], b)
                elif kind == "q":
                    dve.wait_ge(act_step, AS["decays", h])
                    nc.vector.scalar_tensor_tensor(out=g_qd[:, h, :], in0=gb[b % 2], scalar=P ** -0.5,
                                                   in1=g_qd[:, h, :], op0=ALU.mult,
                                                   op1=ALU.mult).then_inc(bank_free[b % 2], 1)
                else:
                    VS.did(nc.vector.tensor_tensor(g_kd[:, h, :], gb[b % 2], g_kd[:, h, :], ALU.mult))
                    nc.vector.tensor_tensor(g_ke[:, h, :], gb[b % 2], g_ke[:, h, :],
                                            ALU.mult).then_inc(bank_free[b % 2], 1)
                    evacuated(dve, b)
                    evacuated(dve, gla_block("q", h))
                    VS.did(nc.vector.tensor_copy(g_junk2[:, :], zero[:, 0:1]), "k end", h)

            def gated(h, pair):
                dve.wait_ge(pe_step, PE["o turned", 4 * h + 2 * pair + 1])
                out = tmp2[:, 0, :].rearrange("p (e t) -> p e t", e=2)
                ts, cs = slice(256 * pair, 256 * pair + 256), slice(2 * h, 2 * h + 2)
                VS.did(nc.vector.tensor_tensor(out, banks[:, 4, :].rearrange("p (e t) -> p e t", e=2),
                                               g_g[:, :, ts], ALU.mult), "o gated", h, pair)
                last()
                VS.did(nc.vector.tensor_scalar(g_oh[:, cs, ts], out, 1.0, None, ALU.mult))
                last()
                VS.did(nc.vector.tensor_tensor(g_ol[:, cs, ts], out, g_oh[:, cs, ts].bitcast(F32), ALU.subtract),
                       "mix1 split", h, pair)

            log_gates(0)
            through("v0", 0)
            log_gates(1)
            through("q", 0)
            log_gates(2)
            through("k", 0)
            log_gates(3)
            through("v1", 0)
            for h in range(GH):
                for t in range(TT):
                    n = 4 * h + t
                    ends = GLA_THROUGH[h]

                    def end_of(place):
                        if (t, place) in ends:
                            kind = ends[t, place]
                            through(kind, h if kind[0] == "g" else h + 1)

                    dve.wait_ge(pe_step, PE["att", n])
                    VS.did(nc.vector.copy_predicated(g_att[:, n % 2, :], pc("gla_mask").bitcast(mybir.dt.uint32),
                                                     banks[:, 3, 0:P]), "att masked", n)
                    if h and t == 0:
                        gated(h - 1, 1)
                    end_of(0)
                    for k in range(2):
                        c = 2 * t + k
                        if c == 7:
                            continue
                        dve.wait_ge(pe_step, PE["u", n])
                        if c >= 2:
                            dve.wait_ge(pe_step, PE["inter", h, c - 1])
                        elif h:
                            dve.wait_ge(pe_step, PE["inter", h - 1, 7])
                        u = banks[:, 2 if k else 7, 0:256]
                        if c == 0:
                            VS.did(nc.vector.tensor_copy(g_S[:, 1, :], u), "S", h, 1)
                        else:
                            dve.wait_ge(dve_step, VS["S", h, c])
                            VS.did(nc.vector.scalar_tensor_tensor(out=g_S[:, (c + 1) % 2, :], in0=g_S[:, c % 2, :],
                                                                  scalar=g_dec[:, h, c:c + 1], in1=u, op0=ALU.mult,
                                                                  op1=ALU.add), "S", h, c + 1)
                    VS.noted[("state", n)] = VS.count
                    end_of(1)
                    if t == 2:
                        dve.wait_ge(act_step, AS["g sig", h])
                        for e in range(2):
                            VS.did(nc.vector.scalar_tensor_tensor(out=g_g[:, e, :], in0=g_g[:, e, :],
                                                                  scalar=pc("normg", e, e + 1), in1=tmp[:, e, :],
                                                                  op0=ALU.mult, op1=ALU.mult))
                        last()
                    dve.wait_ge(act_step, AS["o rstd", n])
                    if n >= 2:
                        dve.wait_ge(pe_step, PE["o turned", n - 2])
                    VS.did(nc.vector.tensor_scalar(g_on[:, n % 2, :], banks[:, 5 + n % 2, 0:256],
                                                   g_ss[:, 2 * (n % 2) + 1:2 * (n % 2) + 2], None, ALU.mult),
                           "o normed", n)
                    if t == 2:
                        gated(h, 0)
                    end_of(2)
            gated(GH - 1, 1)
            add_residual("ln1", B_GLA_OUT, ALPHA, 2)
            norm("ln1", True)
            mlp(B_MLP1, 0, ALPHA, "ln2", 2)
            norm("ln2", True)
            Z = banks[:, 2:5, :].rearrange("p a b -> p (a b)")[:, 0:1280]
            R = banks[:, 5:8, :].rearrange("p a b -> p (a b)")[:, 0:1280]

            def take_scores(h):
                dve.wait_ge(pe_step, PE["sb z", h])
                VS.did(nc.vector.tensor_copy(t_z[:, h % 2, :], Z), "sb z", h)
                last()
                if h >= 2:
                    dve.wait_ge(pe_step, PE["sb o", h - 2])
                VS.did(nc.vector.tensor_scalar(t_e[:, h % 2, :], t_z[:, h % 2, :], 40.0, None, ALU.min),
                       "sb m", h)

            def diagonal(tile, mask, op):
                d = tile.rearrange("p (a b) -> p a b", b=256)[:, 0:5:2, 0:P]
                VS.did(nc.vector.tensor_tensor(d, d, pc(mask).unsqueeze(1).broadcast_to([P, 3, P]), op))
                return nc.vector.tensor_tensor(tile[:, 896:1024], tile[:, 896:1024], pc(mask), op)

            def softplus(h):
                sp = t_sp[:, h % 2, :]
                dve.wait_ge(act_step, AS["sb l", h])
                if h >= 2:
                    dve.wait_ge(act_step, AS["sb w", h - 2])
                VS.did(nc.vector.tensor_tensor(sp, t_z[:, h % 2, :], t_e[:, h % 2, :], ALU.max))
                last()
                VS.did(diagonal(sp, "strict", ALU.mult), "sb masked", h)

            def split_softplus(h):
                sp = t_sp[:, h % 2, :]
                dve.wait_ge(dve_step, VS["sb masked", h])
                if h:
                    dve.wait_ge(pe_step, PE["sb R", h - 1])
                VS.did(nc.vector.tensor_scalar(t_sh[:, :], sp, 1.0, None, ALU.mult))
                last()
                VS.did(nc.vector.tensor_tensor(t_sl[:, :], sp, t_sh[:, :].bitcast(F32), ALU.subtract),
                       "sb sp", h)

            take_scores(0)
            dve.wait_ge(act_step, AS["ones split"])
            softplus(0)
            split_softplus(0)
            for h in range(SH):
                if h + 1 < SH:
                    take_scores(h + 1)
                    softplus(h + 1)
                if h % 2 == 0 and h:
                    split_pair(h // 2 - 1)
                sp = t_sp[:, h % 2, :]
                dve.wait_ge(pe_step, PE["sb R", h])
                VS.did(nc.vector.tensor_tensor(sp, t_z[:, h % 2, :], R, ALU.subtract))
                last()
                VS.did(diagonal(sp, "neg_sb", ALU.add), "sb lw", h)
                if h + 1 < SH:
                    split_softplus(h + 1)
            split_pair(C - 1)
            add_residual("ln3", B_SB_OUT, ALPHA, 2)
            norm("ln3", True)
            mlp(B_MLP2, 32, ALPHA, "ln4", 2)
            norm("ln4", True)
            norm("rms1", False)
            mixer_dve(dve)
            add_residual("rms2", B_MIX_OUT, 1.0, 1)
            norm("rms2", False)
            mlp(B_MLP3, 64, 1.0, "last", 0)


def blocks(w):
    w = np.asarray(w)
    n = w.shape[1] // P
    return w.reshape(C, P, n, P).transpose(2, 1, 0, 3).reshape(n, P, D)


def placed(w, at):
    w = np.asarray(w)
    out = np.zeros((D, P), w.dtype)
    out[:, at] = w
    return blocks(out)


def mlp_stream(up, down):
    up, down = blocks(up), [blocks(np.asarray(down)[q * D:q * D + D]) for q in range(FFQ)]
    parts = [up[0:C]]
    for q in range(1, FFQ):
        parts += [up[q * C:q * C + C], down[q - 1]]
    return np.concatenate(parts + [down[FFQ - 1]])


def chunked(v, rows=P):
    return np.asarray(v).reshape(-1, rows).T


def _dram(**inp):
    g = np.asarray(inp["gla_w_in"])[0]
    heads = {gla_block(kind, h): at * C // 2 + (2 if len(kind) == 2 else 1) * h + (kind[-1] == "1")
             for kind, at in (("q", 0), ("k", 1), ("v0", 2), ("v1", 2), ("g0", 4), ("g1", 4)) for h in range(GH)}
    stream = [placed(g[:, 3072:3088], np.arange(16)),
              blocks(g[:, 0:3072])[[heads[b] for b in range(B_GLA + 1, B_GLA_OUT)]], blocks(inp["gla_w_o"][0]),
              mlp_stream(inp["mlp_w_up"][0], inp["mlp_w_down"][0]),
              np.concatenate([blocks(inp["sb_w_q"][0]), blocks(inp["kv_w"])]).reshape(3, C, P, D).transpose(
                  1, 0, 2, 3).reshape(3 * C, P, D), blocks(inp["sb_w_o"][0]),
              mlp_stream(inp["mlp_w_up"][1], inp["mlp_w_down"][1])]
    m = np.asarray(inp["w_in_2"])[0]
    gates = 1536 + np.array([4, 5, 6, 7, 12, 13, 14, 15, 0, 1, 2, 3, 8, 9, 10, 11])
    at = np.concatenate([32 * k + np.arange(4) for k in range(4)])
    stream += [blocks(m[:, 0:512]), placed(m[:, gates], at), blocks(m[:, 512:1024]), blocks(m[:, 1024:1536]),
               blocks(m[:, 1552:1936]), placed(m[:, 1936:2000], np.arange(64)),
               blocks(inp["w_out_2"][0]), mlp_stream(inp["w_ff1_2"][0], inp["w_ff2_2"][0])]
    W = np.ascontiguousarray(np.concatenate(stream))
    par = np.zeros((P, NPAR), np.float32)

    def put(name, a, row=0):
        o, w = _cols[name]
        a = np.asarray(a)
        par[row:row + a.shape[0], o:o + a.shape[1]] = a

    put("ba", chunked(inp["gla_b_a"][0]))
    put("normg", chunked(inp["gla_norm_g"][0]))
    lg, lb = np.asarray(inp["ln_g"]), np.asarray(inp["ln_b"])
    put("ln", np.concatenate([chunked(a[l, k]) for l in range(2) for k in range(2) for a in (lg, lb)], axis=1))
    put("gmix", chunked(inp["g_mix_norm_2"][0]))
    put("gffn", chunked(inp["g_ffn_norm_2"][0]))
    put("gout", chunked(inp["g_mlstm_out_2"][0]))
    put("gcq", chunked(inp["g_cq_2"][0]))
    put("gckv", chunked(inp["g_ckv_2"][0]))
    for n, v in (("q", inp["g_q_2"][0]), ("k", inp["g_k_2"][0])):
        put(f"g{n}n", np.asarray(v)[0:128, None])
        put(f"g{n}r", np.asarray(v)[128:192, None])
    put("convw", np.asarray(inp["conv_w_2"][0]).reshape(5, 4, P).transpose(2, 1, 0).reshape(P, 20))
    put("convb", chunked(inp["conv_b_2"][0]))
    bg = np.asarray(inp["b_gates_2"][0]).reshape(4, 4)
    for n, k in (("bf", 1), ("bi", 0)):
        put(n, bg[k][:, None])
        put(n, bg[k + 2][:, None], 32)
    inv = (np.float32(10000.0) ** (-np.arange(0, 64, 2, dtype=np.float32) / np.float32(64))).astype(np.float32)
    put("freq", np.concatenate([inv, inv])[:, None])
    i = np.arange(P)
    s, t = i[:, None], i[None, :]
    put("ident", np.eye(P))
    put("strict", s < t)
    put("gla_mask", (s <= t) & (s // GC == t // GC))
    put("tri", s >= t)
    put("ones", np.full((P, P), 1.0 / D))
    put("one", np.ones((P, P)))
    put("ln_eps", np.full((P, 1), LN_EPS))
    put("rms_eps", np.full((P, 1), RMS_EPS))
    put("half_pi", np.full((P, 1), np.pi / 2))
    put("neg_fw", np.where(s > t, -NEG, 0.0))
    put("neg_bw", np.where(s < t, -NEG, 0.0))
    put("neg_sb", np.where(s >= t, NEG, 0.0))
    put("reset", np.broadcast_to((np.arange(T) % GC != 0), (P, T)))
    sel = np.zeros((64, 8, P))
    for d in range(2):
        for h in range(4):
            sel[32 * d + h, 4 * d + h] = 1
    put("sel", sel.reshape(64, 8 * P))
    swap = np.zeros((64, 64))
    swap[np.arange(32) + 32, np.arange(32)] = -1
    swap[np.arange(32), np.arange(32) + 32] = 1
    put("swap", swap)
    put("wa2", inp["gla_w_a2"][0])
    put("wuq", np.asarray(inp["w_uq_2"][0]).reshape(2, P, 768).transpose(1, 0, 2).reshape(P, 1536))
    put("wukv", inp["w_ukv_2"][0])
    x = np.ascontiguousarray(np.asarray(inp["x"])[0].T.reshape(C, P, T))
    pos = np.ascontiguousarray(np.broadcast_to(np.asarray(inp["positions_2"]).astype(np.int32), (64, T)))
    return W, x, par, pos


def kernel(**inputs):
    import concourse.bacc as bacc
    from concourse.bass_utils import run_bass_kernel_spmd

    W, x, par, pos = _dram(**inputs)
    counts = [{}, {}, {}, {}]
    FINAL.clear()
    for second in range(2):
        if second:
            FINAL.append(True)
        nc = bacc.Bacc("TRN2", target_bir_lowering=False, num_devices=1)
        aps = [nc.dram_tensor(n, a.shape, mybir.dt.from_np(a.dtype), kind="ExternalInput").ap()
               for n, a in (("w_stream", W), ("x_t", x), ("params", par), ("pos", pos))]
        y = nc.dram_tensor("y_t", (C, P, T), F32, kind="ExternalOutput").ap()
        build(nc, counts, *aps, y)
    r = run_bass_kernel_spmd(nc, [{"w_stream": W, "x_t": x, "params": par, "pos": pos}], core_ids=[0])
    return np.ascontiguousarray(r.results[0]["y_t"].reshape(D, T).T)[None]
```
